# Optimizing a Trainium2 kernel written in Bass

```python
import jax
import jax.numpy as jnp
from jax import lax
import numpy as np

D_MODEL = 1024
BATCH = 1
SEQ = 512
DEPTH = 1

GRID_W = 64
MEM_LEN = 256
EPS = 1e-6
NEG_INF = -1e30

NA_HEADS = 8
NA_WIDTH = D_MODEL // 2
NA_HEAD_DIM = NA_WIDTH // NA_HEADS
NA_WIN_ROWS = 8
NA_WIN_COLS = 16
NA_QBLOCK_COLS = 16
NA_KBLOCK_COLS = NA_QBLOCK_COLS + NA_WIN_COLS

POOL_SIZES = (2, 4, 8, 16)
POOL_WIDTH = D_MODEL // 2
POOL_GROUP = POOL_WIDTH // len(POOL_SIZES)

XA_HEADS = 4
XA_WIDTH = D_MODEL // 2
XA_HEAD_DIM = XA_WIDTH // XA_HEADS

N_BRANCH = 3
IN_COLS = 3 * NA_WIDTH + POOL_WIDTH + XA_WIDTH + N_BRANCH * D_MODEL

PEER_HEADS = 8
PEER_KEYS = 128
PEER_EXPERTS = PEER_KEYS * PEER_KEYS
PEER_QDIM = 256
PEER_TOPK = 16
PEER_CHUNK = 64

kernel_name = 'hybrid_na_pool_memxattn_peer_encoder'

def rms_norm(x, g):
    xf = x.astype(jnp.float32)
    y = xf * lax.rsqrt(jnp.mean(xf * xf, axis=-1, keepdims=True) + EPS)
    return (y * g.astype(jnp.float32)).astype(x.dtype)

def neighbourhood_attention(q, k, v, rpb):
    B, S, H, dh = q.shape
    rows = S // GRID_W
    wr = min(NA_WIN_ROWS, rows)
    n_cb = GRID_W // NA_QBLOCK_COLS
    qg = q.reshape(B, rows, GRID_W, H, dh)
    kg = k.reshape(B, rows, GRID_W, H, dh)
    vg = v.reshape(B, rows, GRID_W, H, dh)
    qc = np.arange(GRID_W).reshape(n_cb, NA_QBLOCK_COLS)
    kb0 = np.clip(np.arange(n_cb) * NA_QBLOCK_COLS - NA_WIN_COLS // 2, 0, GRID_W - NA_KBLOCK_COLS)
    kc = kb0[:, None] + np.arange(NA_KBLOCK_COLS)[None, :]
    cs = np.clip(qc - NA_WIN_COLS // 2, 0, GRID_W - NA_WIN_COLS)
    col_ok = (kc[:, None, :] >= cs[:, :, None]) & (kc[:, None, :] < cs[:, :, None] + NA_WIN_COLS)
    dc_idx = np.clip(kc[:, None, :] - qc[:, :, None], -(NA_WIN_COLS - 1), NA_WIN_COLS - 1) + NA_WIN_COLS - 1
    mask = np.broadcast_to(col_ok[:, :, None, :], (n_cb, NA_QBLOCK_COLS, wr, NA_KBLOCK_COLS))
    mask = mask.reshape(n_cb, NA_QBLOCK_COLS, wr * NA_KBLOCK_COLS)
    scale = dh ** -0.5

    def row_block(r):
        rs = jnp.clip(r - wr // 2, 0, rows - wr)
        q_r = lax.dynamic_index_in_dim(qg, r, axis=1, keepdims=False)
        k_r = lax.dynamic_slice_in_dim(kg, rs, wr, axis=1)
        v_r = lax.dynamic_slice_in_dim(vg, rs, wr, axis=1)
        q_b = q_r.reshape(B, n_cb, NA_QBLOCK_COLS, H, dh)
        k_b = jnp.stack([k_r[:, :, int(s):int(s) + NA_KBLOCK_COLS] for s in kb0], axis=1)
        v_b = jnp.stack([v_r[:, :, int(s):int(s) + NA_KBLOCK_COLS] for s in kb0], axis=1)
        k_b = k_b.reshape(B, n_cb, wr * NA_KBLOCK_COLS, H, dh)
        v_b = v_b.reshape(B, n_cb, wr * NA_KBLOCK_COLS, H, dh)
        dr_idx = rs + jnp.arange(wr) - r + (NA_WIN_ROWS - 1)
        bias = rpb[:, dr_idx[None, None, :, None], dc_idx[:, :, None, :]]
        bias = bias.reshape(H, n_cb, NA_QBLOCK_COLS, wr * NA_KBLOCK_COLS).astype(jnp.float32)
        s = jnp.einsum('bjqhd,bjkhd->bhjqk', q_b, k_b).astype(jnp.float32) * scale + bias[None]
        s = jnp.where(mask[None, None], s, NEG_INF)
        p = jax.nn.softmax(s, axis=-1).astype(v.dtype)
        o = jnp.einsum('bhjqk,bjkhd->bjqhd', p, v_b)
        return o.reshape(B, GRID_W, H, dh)

    out = lax.map(row_block, jnp.arange(rows))
    return out.transpose(1, 0, 2, 3, 4).reshape(B, S, H * dh)

def multiscale_pool(p, w_group, scale):
    B, S, C = p.shape
    pf = p.astype(jnp.float32)
    csum = jnp.concatenate([jnp.zeros((B, 1, C), jnp.float32), jnp.cumsum(pf, axis=1)], axis=1)
    t = np.arange(S)
    outs = []
    for g, w in enumerate(POOL_SIZES):
        lo = np.clip(t - w // 2, 0, S)
        hi = np.clip(t + w // 2, 0, S)
        cnt = (hi - lo).astype(np.float32)[None, :, None]
        sl = slice(g * POOL_GROUP, (g + 1) * POOL_GROUP)
        cg = csum[..., sl]
        outs.append((cg[:, hi] - cg[:, lo]) / cnt - pf[..., sl])
    pooled = jnp.stack(outs, axis=2).astype(p.dtype)
    mixed = jnp.einsum('bsgc,gcd->bsgd', pooled, w_group).reshape(B, S, C)
    return mixed * scale

def memory_attention(q_x, mem_n, w_mem_kv, q_g, k_g):
    B, S, _ = q_x.shape
    M = mem_n.shape[1]
    q = rms_norm(q_x.reshape(B, S, XA_HEADS, XA_HEAD_DIM), q_g)
    kv = mem_n @ w_mem_kv
    k = rms_norm(kv[..., :XA_WIDTH].reshape(B, M, XA_HEADS, XA_HEAD_DIM), k_g)
    v = kv[..., XA_WIDTH:].reshape(B, M, XA_HEADS, XA_HEAD_DIM)
    s = jnp.einsum('bshd,bmhd->bhsm', q, k).astype(jnp.float32) * (XA_HEAD_DIM ** -0.5)
    p = jax.nn.softmax(s, axis=-1).astype(v.dtype)
    return jnp.einsum('bhsm,bmhd->bshd', p, v).reshape(B, S, XA_WIDTH)

def peer_ffn(hn, w_q, sub_keys, u, v):
    B, S, D = hn.shape
    nc = S // PEER_CHUNK
    hc = hn.reshape(B, nc, PEER_CHUNK, D).transpose(1, 0, 2, 3)

    def chunk(hb):
        T = hb.shape[1]
        q = (hb @ w_q).reshape(B, T, PEER_HEADS, 2, PEER_QDIM // 2)
        s = jnp.einsum('bthpd,hpnd->bthpn', q, sub_keys).astype(jnp.float32)
        s1, i1 = lax.top_k(s[..., 0, :], PEER_TOPK)
        s2, i2 = lax.top_k(s[..., 1, :], PEER_TOPK)
        cand = (s1[..., :, None] + s2[..., None, :]).reshape(B, T, PEER_HEADS, PEER_TOPK * PEER_TOPK)
        cidx = (i1[..., :, None] * PEER_KEYS + i2[..., None, :]).reshape(B, T, PEER_HEADS, PEER_TOPK * PEER_TOPK)
        top_s, pos = lax.top_k(cand, PEER_TOPK)
        eidx = jnp.take_along_axis(cidx, pos, axis=-1)
        g = jax.nn.softmax(top_s, axis=-1)
        u_sel = u[eidx]
        v_sel = v[eidx]
        a = jax.nn.gelu(jnp.einsum('btd,bthkd->bthk', hb, u_sel).astype(jnp.float32), approximate=False)
        return jnp.einsum('bthk,bthkd->btd', (g * a).astype(hb.dtype), v_sel)

    out = lax.map(chunk, hc)
    return out.transpose(1, 0, 2, 3).reshape(B, S, D)

def setup_inputs(seed: int = 0) -> dict:
    key = jax.random.key(seed)
    ks = jax.random.split(key, 24)
    f32 = jnp.float32
    L = DEPTH

    def nrm(k, shape, scale):
        return jax.random.normal(k, shape, f32) * scale

    def gain(k, shape):
        return 1.0 + 0.05 * jax.random.normal(k, shape, f32)

    return {
        'x': nrm(ks[0], (BATCH, SEQ, D_MODEL), 1.0),
        'mem': nrm(ks[1], (BATCH, MEM_LEN, D_MODEL), 1.0),
        'mix_norm_g': gain(ks[2], (L, D_MODEL)),
        'mem_norm_g': gain(ks[3], (L, D_MODEL)),
        'w_in': nrm(ks[4], (L, D_MODEL, IN_COLS), D_MODEL ** -0.5),
        'gate_b': nrm(ks[5], (L, N_BRANCH * D_MODEL), 0.1),
        'w_mem_kv': nrm(ks[6], (L, D_MODEL, 2 * XA_WIDTH), D_MODEL ** -0.5),
        'na_q_g': gain(ks[7], (L, NA_HEAD_DIM)),
        'na_k_g': gain(ks[8], (L, NA_HEAD_DIM)),
        'na_rpb': nrm(ks[9], (L, NA_HEADS, 2 * NA_WIN_ROWS - 1, 2 * NA_WIN_COLS - 1), 0.5),
        'pool_w': nrm(ks[10], (L, len(POOL_SIZES), POOL_GROUP, POOL_GROUP), POOL_GROUP ** -0.5),
        'pool_scale': gain(ks[11], (L, POOL_WIDTH)),
        'xa_q_g': gain(ks[12], (L, XA_HEAD_DIM)),
        'xa_k_g': gain(ks[13], (L, XA_HEAD_DIM)),
        'w_branch_na': nrm(ks[14], (L, NA_WIDTH, D_MODEL), NA_WIDTH ** -0.5),
        'w_branch_pool': nrm(ks[15], (L, POOL_WIDTH, D_MODEL), POOL_WIDTH ** -0.5),
        'w_branch_xa': nrm(ks[16], (L, XA_WIDTH, D_MODEL), XA_WIDTH ** -0.5),
        'w_out': nrm(ks[17], (L, D_MODEL, D_MODEL), D_MODEL ** -0.5),
        'ffn_norm_g': gain(ks[18], (L, D_MODEL)),
        'peer_w_q': nrm(ks[19], (L, D_MODEL, PEER_HEADS * PEER_QDIM), D_MODEL ** -0.5),
        'peer_sub_keys': nrm(ks[20], (L, PEER_HEADS, 2, PEER_KEYS, PEER_QDIM // 2), (PEER_QDIM // 2) ** -0.5),
        'peer_u': nrm(ks[21], (L, PEER_EXPERTS, D_MODEL), D_MODEL ** -0.5),
        'peer_v': nrm(ks[22], (L, PEER_EXPERTS, D_MODEL), 0.5),
    }

def reference(x, mem, mix_norm_g, mem_norm_g, w_in, gate_b, w_mem_kv, na_q_g, na_k_g, na_rpb,
              pool_w, pool_scale, xa_q_g, xa_k_g, w_branch_na, w_branch_pool, w_branch_xa, w_out,
              ffn_norm_g, peer_w_q, peer_sub_keys, peer_u, peer_v):
    B, S, D = x.shape
    c0 = 3 * NA_WIDTH
    c1 = c0 + POOL_WIDTH
    c2 = c1 + XA_WIDTH
    h = x
    for l in range(DEPTH):
        xn = rms_norm(h, mix_norm_g[l])
        proj = xn @ w_in[l]
        qkv = proj[..., :c0].reshape(B, S, 3, NA_HEADS, NA_HEAD_DIM)
        q_na = rms_norm(qkv[:, :, 0], na_q_g[l])
        k_na = rms_norm(qkv[:, :, 1], na_k_g[l])
        y_na = neighbourhood_attention(q_na, k_na, qkv[:, :, 2], na_rpb[l])
        y_pool = multiscale_pool(proj[..., c0:c1], pool_w[l], pool_scale[l])
        mem_n = rms_norm(mem, mem_norm_g[l])
        y_xa = memory_attention(proj[..., c1:c2], mem_n, w_mem_kv[l], xa_q_g[l], xa_k_g[l])
        gate = jax.nn.sigmoid((proj[..., c2:] + gate_b[l]).astype(jnp.float32))
        gate = gate.reshape(B, S, N_BRANCH, D).astype(h.dtype)
        merged = (gate[:, :, 0] * (y_na @ w_branch_na[l])
                  + gate[:, :, 1] * (y_pool @ w_branch_pool[l])
                  + gate[:, :, 2] * (y_xa @ w_branch_xa[l]))
        h = h + merged @ w_out[l]
        hn = rms_norm(h, ffn_norm_g[l])
        h = h + peer_ffn(hn, peer_w_q[l], peer_sub_keys[l], peer_u[l], peer_v[l])
    return h


_drawn_inputs = setup_inputs


def setup_inputs(seed=0):
    import zlib

    import numpy as np

    out = dict(_drawn_inputs(seed))
    spreads = {}
    factors = {'mem_norm_g': 3.691,
     'na_q_g': 3.702,
     'na_k_g': 3.868,
     'xa_q_g': 5.034,
     'xa_k_g': 4.423,
     'pool_scale': 3.396}
    for name, (base, spread) in spreads.items():
        noise = np.random.default_rng([zlib.crc32(name.encode()), seed]).standard_normal(out[name].shape)
        drawn = base * np.exp(spread * noise) if base else spread * noise
        out[name] = jnp.asarray(drawn.astype(out[name].dtype))
    for name, factor in factors.items():
        out[name] = (out[name] * factor).astype(out[name].dtype)
    return out
```

```python
import numpy as np

import concourse.bass as bass
from concourse import mybir
from concourse.alu_op_type import AluOpType as ALU

F32 = mybir.dt.float32
F32R = mybir.dt.float32r
U32 = mybir.dt.uint32
ACT = mybir.ActivationFunctionType
AX_X = mybir.AxisListType.X

P = 128
D = 1024
KD = D // P
T = 512
TT = T // P
M = 256
MT = M // P
W = 512
KW = W // P
NORM_EPS = 1e-6
MASKED = -1e30

GRID_R, GRID_C = 8, 64
NA_H, NA_D = 8, 64
XA_H, XA_D = 4, 128
QCOLS, KCOLS, WCOLS = 16, 32, 16
NJ = GRID_C // QCOLS
KEY0 = [min(max(j * QCOLS - WCOLS // 2, 0), GRID_C - KCOLS) * GRID_R for j in range(NJ)]
VARIANT = [0, 1, 1, 2]
POOL = (2, 4, 8, 16)
PAD = 8

HEADS, KEYS, TOPK = 8, 128, 16
HP = 2 * HEADS
TB = 32
NTB = T // TB
GC = 4
CHUNKS = KEYS
GROUPS = CHUNKS // GC
HALF = 512

BASE = 16640
KB = 1024


def at_least(eng, sem, value):
    if isinstance(value, int) and value <= 0:
        return
    eng.wait_ge(sem, value)


def held(eng, *waits):
    for sem, value in waits:
        at_least(eng, sem, value)
    eng.nop(nofuse=True)


def sbuf(nc, name, shape, dtype, kb):
    return nc.alloc_sbuf_tensor_at(name, shape, dtype, offset=BASE + int(kb * KB))


def stage_norm(nc, sem, mem_, io):
    x, ident = mem_["xbuf"], mem_["ident"]
    bank = mem_["bank"]
    NT = TT + MT
    with nc.Block() as block:

        @block.sync
        def _(sp):
            for i in range(NT):
                src = io["x"][i * P:(i + 1) * P, :] if i < TT else io["mem"][(i - TT) * P:(i - TT + 1) * P, :]
                sp.dma_start(x[:, i, :], src).then_inc(sem["x_loaded"][i], 16)
            sp.dma_start(mem_["consts"][:], io["consts"]).then_inc(sem["consts_loaded"], 16)
            for n in range(2):
                load_weights(sp, sem, mem_, io, n)

        @block.scalar
        def _(act):
            act.wait_ge(sem["eps_set"], 1)
            for i in range(NT):
                act.wait_ge(sem["x_loaded"][i], 16)
                if i:
                    act.wait_ge(sem["x_squares"], i)
                nc.scalar.activation(mem_["junk"][:], x[:, i, :], ACT.Square,
                                     accum_out=mem_["ss"][:, i:i + 1]).then_inc(sem["x_squares"], 1)
                act.wait_ge(sem["x_squares"], i + 1)
                nc.scalar.activation(mem_["sd"][:, i:i + 1], mem_["ss"][:, i:i + 1], ACT.Sqrt,
                                     scale=1.0 / D, bias=mem_["eps"][:, 0:1]).then_inc(sem["x_roots"], 1)

        @block.vector
        def _(dve):
            nc.vector.memset(mem_["eps"][:], NORM_EPS).then_inc(sem["eps_set"], 1)
            dve.wait_ge(sem["consts_loaded"], 16)

            def evacuate(i):
                g = mem_["mix_g"] if i < TT else mem_["mem_g"]
                dst = mem_["xnT"] if i < TT else mem_["memnT"]
                t0 = (i if i < TT else i - TT) * P
                for h in range(2):
                    n = 2 * i + h
                    dve.wait_ge(sem["xT_ready"], n + 1)
                    gain = g[:, 4 * h:4 * h + 4].unsqueeze(2).to_broadcast([P, 4, P])
                    nc.vector.tensor_tensor(dst[:, 4 * h:4 * h + 4, t0:t0 + P], bank4(bank[n % 2]), gain,
                                            ALU.mult).then_inc(sem["xT_copied"], 1)

            for i in range(NT):
                dve.wait_ge(sem["x_roots"], i + 1)
                nc.vector.reciprocal(mem_["rstd"][:, i:i + 1], mem_["sd"][:, i:i + 1]).then_inc(sem["x_rstd"], 1)
                dve.wait_ge(sem["x_rstd"], i + 1)
                nc.vector.tensor_scalar(x[:, i, :], x[:, i, :], mem_["rstd"][:, i:i + 1], None,
                                        ALU.mult).then_inc(sem["x_normed"], 1)
                if i:
                    evacuate(i - 1)
            evacuate(NT - 1)

        @block.tensor
        def _(pe):
            pe.wait_ge(sem["consts_loaded"], 16)
            for i in range(NT):
                pe.wait_ge(sem["x_normed"], i + 1)
                for h in range(2):
                    n = 2 * i + h
                    if n >= 2:
                        pe.wait_ge(sem["xT_copied"], n - 1)
                    for q in range(4):
                        last = nc.tensor.transpose(bank4(bank[n % 2])[:, q, :],
                                                   x[:, i, (4 * h + q) * P:(4 * h + q + 1) * P], ident)
                    last.then_inc(sem["xT_ready"], 1)


def bank4(bank):
    return bank[:].rearrange("p (a b) -> p a b", a=4)


N_KV, N_MIX, N_GATE, N_WQ = 2, 5, KD, 4
FIRST_GATE = N_KV + N_MIX
FIRST_WQ = FIRST_GATE + N_GATE


def load_weights(sp, sem, mem_, io, n):
    ring = mem_["wring"]
    if n < N_KV:
        src = io["w_kv"][n]
    elif n < FIRST_GATE:
        src = io["w_mix"][n - N_KV]
    elif n < FIRST_WQ:
        src = io["w_gate"][n - FIRST_GATE]
    else:
        src = io["w_q"][n - FIRST_WQ]
    sp.dma_start(ring[:, n % 2, 0:src.shape[1]], src).then_inc(sem["w_loaded"][n % 2], 16)


def weights_arrived(eng, sem, n):
    eng.wait_ge(sem["w_loaded"][n % 2], 16 * (n // 2 + 1))


KV_JOBS = 2 * MT
MIX_JOBS = KV_JOBS + N_MIX * TT
POOL_MIX = MIX_JOBS
TURNS = 2 + 3 * TT
UNITS = NJ * NA_H + TT * XA_H


def stage_attend(nc, sem, mem_, io):
    bank, ident = mem_["bank"], mem_["ident"]
    prod_bank, turn_bank, score_bank, out_bank = bank[0:2], bank[2:4], bank[4:6], bank[6:8]
    ring, xnT, memnT = mem_["wring"], mem_["xnT"], mem_["memnT"]
    nraw, kvmem, vna, vsh = mem_["nraw"], mem_["kvmem"], mem_["vna"], mem_["vsh"]
    qkxT, kmT, yT = mem_["qkxT"], mem_["kmT"], mem_["yT"]
    bias = mem_["bias"]
    ppad, pooled = mem_["ppad"], mem_["pooledT"]

    def is_na(u):
        return u < NJ * NA_H

    with nc.Block() as block:

        @block.sync
        def _(sp):
            sp.dma_start(mem_["gains"][:], io["gains"]).then_inc(sem["gains_loaded"], 16)
            for n in range(2, FIRST_GATE + 2):
                used = n - 2
                sp.wait_ge(sem["prod_ready"], 2 * (used + 1) if used < N_KV else KV_JOBS + TT * (used - N_KV + 1))
                load_weights(sp, sem, mem_, io, n)
                if n == 4:
                    sp.dma_start(bias[:], io["bias"]).then_inc(sem["bias_loaded"], 16)
            sp.wait_ge(sem["prod_copied"], KV_JOBS + 4 * TT)
            sp.dma_start(vsh[0:64, :, :], vna[64:128, 0:3, :]).then_inc(sem["vsh_loaded"], 16)
            sp.dma_start(vsh[64:128, :, :], vna[0:64, 1:4, :]).then_inc(sem["vsh_loaded"], 16)
            sp.wait_ge(sem["turn_ready"], 2 + TT)
            sp.dma_start(mem_["pool_w"][:], io["pool_w"]).then_inc(sem["pool_loaded"], 16)

        @block.tensor
        def _(pe):
            job = 0
            for n in range(FIRST_GATE):
                weights_arrived(pe, sem, n)
                w = ring[:, n % 2, :].rearrange("p (k f) -> p k f", k=KD)
                for i in range(MT if n < N_KV else TT):
                    if job >= 2:
                        pe.wait_ge(sem["prod_copied"], job - 1)
                    for k in range(KD):
                        if n < N_KV:
                            lhsT, rhs = memnT[:, k, i * P:(i + 1) * P], w[:, k, :]
                        elif n < N_KV + 4:
                            lhsT, rhs = xnT[:, k, i * P:(i + 1) * P], w[:, k, :]
                        else:
                            lhsT, rhs = w[:, k, i * P:(i + 1) * P], xnT[:, k, :]
                        last = nc.tensor.matmul(prod_bank[job % 2][:], lhsT, rhs, start=(k == 0), stop=(k == KD - 1))
                    last.then_inc(sem["prod_ready"], 1)
                    job += 1

            for n in range(TURNS):
                stage = 0 if n < 2 else 1 + (n - 2) // TT
                pe.wait_ge(sem["normed"], stage + 1)
                if n >= 2:
                    pe.wait_ge(sem["turn_copied"], n - 1)
                for q in range(4):
                    if n < 2:
                        src = kvmem[:, 0, q % 2, (2 * n + q // 2) * P:(2 * n + q // 2 + 1) * P]
                    else:
                        f = (n - 2) % TT
                        src = nraw[:, stage - 1, q, f * P:(f + 1) * P]
                    last = nc.tensor.transpose(bank4(turn_bank[n % 2])[:, q, :], src, ident)
                last.then_inc(sem["turn_ready"], 1)

            def scores(u):
                if u == 0:
                    pe.wait_ge(sem["turn_copied"], TURNS)
                if u >= 2:
                    pe.wait_ge(sem["logits"], u - 1)
                out = score_bank[u % 2][:, 0:M]
                if is_na(u):
                    j, h = divmod(u, NA_H)
                    rows = slice(64 * (h % 2), 64 * (h % 2) + 64)
                    lhsT = qkxT[rows, 0, h // 2, j * P:(j + 1) * P]
                    rhs = qkxT[rows, 1, h // 2, KEY0[j]:KEY0[j] + M]
                else:
                    i, h = divmod(u - NJ * NA_H, XA_H)
                    lhsT, rhs = qkxT[:, 2, h, i * P:(i + 1) * P], kmT[:, h, :]
                nc.tensor.matmul(out, lhsT, rhs, start=True, stop=True).then_inc(sem["scored"], 1)

            def turn(u):
                pe.wait_ge(sem["probs"], u + 1)
                if u >= 2:
                    pe.wait_ge(sem["probsT_copied"], u - 1)
                for q in range(2):
                    last = nc.tensor.transpose(turn_bank[u % 2][:, q * P:(q + 1) * P],
                                               mem_["prob"][:, u % 3, q * P:(q + 1) * P], ident)
                last.then_inc(sem["probsT"], 1)

            def values(u):
                pe.wait_ge(sem["probsT_copied"], u + 1)
                if u == 0:
                    pe.wait_ge(sem["vsh_loaded"], 32)
                if u >= 2:
                    pe.wait_ge(sem["mixed_copied"], u - 1)
                for q in range(2):
                    if is_na(u):
                        j, h = divmod(u, NA_H)
                        cols = slice(h * NA_D, (h + 1) * NA_D)
                        k0 = KEY0[j] // P + q
                        v = vna[:, k0, cols] if KEY0[j] % P == 0 else vsh[:, k0, cols]
                        out = out_bank[u % 2][64 * (h % 2):64 * (h % 2) + 64, 0:P]
                    else:
                        h = (u - NJ * NA_H) % XA_H
                        v = kvmem[:, 1, q, h * P:(h + 1) * P]
                        out = out_bank[u % 2][:, 0:P]
                    last = nc.tensor.matmul(out, v, mem_["probT"][:, u % 2, q * P:(q + 1) * P],
                                            start=(q == 0), stop=(q == 1))
                last.then_inc(sem["mixed"], 1)

            for s in range(UNITS + 3):
                if s < UNITS:
                    scores(s)
                if 0 <= s - 2 < UNITS:
                    turn(s - 2)
                if 0 <= s - 3 < UNITS:
                    values(s - 3)
            pe.wait_ge(sem["pooled"], 4)
            pe.wait_ge(sem["pool_loaded"], 16)
            for g in range(4):
                pe.wait_ge(sem["prod_copied"], POOL_MIX + g - 1)
                nc.tensor.matmul(prod_bank[g % 2][:], mem_["pool_w"][:, g, :], pooled[:, g, :],
                                 start=True, stop=True).then_inc(sem["prod_ready"], 1)

        @block.scalar
        def _(act):
            def copied(n, out, src, **how):
                act.wait_ge(sem["prod_ready"], n + 1)
                nc.scalar.activation(out, src, ACT.Copy, **how).then_inc(sem["prod_copied"], 1)

            def root(stage, groups, dim):
                act.wait_ge(sem["sums"], stage + 1)
                nc.scalar.activation(mem_["gsd"][:, stage, 0:groups], mem_["gss"][:, stage, 0:groups], ACT.Sqrt,
                                     scale=1.0 / dim, bias=mem_["eps"][:, 0:1]).then_inc(sem["roots"], 1)

            for n in range(KV_JOBS):
                copied(n, kvmem[:, n // MT, n % MT, :], prod_bank[n % 2][:])
            act.wait_ge(sem["pads_cleared"], 1)
            for n in range(KV_JOBS, MIX_JOBS):
                part, i = divmod(n - KV_JOBS, TT)
                if part < 3:
                    copied(n, nraw[:, part, i, :], prod_bank[n % 2][:])
                elif part == 3:
                    copied(n, vna[:, i, :], prod_bank[n % 2][:])
                else:
                    copied(n, ppad[:, i, PAD:PAD + T].rearrange("p (r c) -> p c r", c=GRID_C),
                           prod_bank[n % 2][:].rearrange("p (c r) -> p c r", r=GRID_R))
                if i == TT - 1 and part < 4:
                    root(*[(0, XA_H * MT, XA_D), (1, NA_H * TT, NA_D), (2, NA_H * TT, NA_D), (3, XA_H * TT, XA_D)][part])
            for s in range(UNITS + 2):
                if s < UNITS:
                    act.wait_ge(sem["maxima"], s + 1)
                    if s >= 3:
                        act.wait_ge(sem["probsT"], s - 2)
                    nc.scalar.activation(mem_["prob"][:, s % 3, :], mem_["logit"][:, s % 2, :], ACT.Exp,
                                         bias=mem_["nmax"][:, s:s + 1], scale=1.0,
                                         accum_out=mem_["total"][:, s:s + 1]).then_inc(sem["exps"], 1)
                u = s - 2
                if 0 <= u < UNITS:
                    act.wait_ge(sem["probsT"], u + 1)
                    if u >= 2:
                        act.wait_ge(sem["mixed"], u - 1)
                    nc.scalar.activation(mem_["probT"][:, u % 2, :], turn_bank[u % 2][:, 0:M],
                                         ACT.Copy).then_inc(sem["probsT_copied"], 1)
            for g in range(4):
                act.wait_ge(sem["prod_ready"], POOL_MIX + g + 1)
                nc.scalar.activation(yT[:, 1, g, :], prod_bank[g % 2][:], ACT.Copy,
                                     scale=mem_["pool_scale"][:, g:g + 1]).then_inc(sem["prod_copied"], 1)

        @block.gpsimd
        def _(pool):
            nc.gpsimd.memset(ppad[:], 0.0).then_inc(sem["pads_cleared"], 1)
            rows = mem_["wsum"]
            step = 0
            for g in range(4):
                pool.wait_ge(sem["prod_copied"], KV_JOBS + 4 * TT + g + 1)
                src = ppad[:, g, :]
                lo, hi = 0, T + 2 * PAD
                half = 1
                for level in range(g + 1):
                    shift_lo, shift_hi = (1, 0) if level == 0 else (half // 2, half // 2)
                    lo, hi = lo + shift_lo, hi - shift_hi
                    dst = rows[:, level % 2, :]
                    nc.gpsimd.tensor_tensor(dst[:, lo:hi], src[:, lo - shift_lo:hi - shift_lo],
                                            src[:, lo + shift_hi:hi + shift_hi], ALU.add).then_inc(sem["pool_step"], 1)
                    step += 1
                    pool.wait_ge(sem["pool_step"], step)
                    src = dst
                    half *= 2
                w = POOL[g]
                mean = rows[:, g % 2, PAD:PAD + T]
                nc.gpsimd.tensor_scalar(mean, mean, 1.0 / w, None, ALU.mult).then_inc(sem["pool_step"], 1)
                step += 1
                pool.wait_ge(sem["pool_step"], step)
                for e, cols in ((0, slice(0, PAD)), (1, slice(T - PAD, T))):
                    nc.gpsimd.tensor_tensor(mean[:, cols], mean[:, cols], mem_["edge"][:, g, e, :],
                                            ALU.mult).then_inc(sem["pool_step"], 1)
                    step += 1
                pool.wait_ge(sem["pool_step"], step)
                nc.gpsimd.tensor_tensor(pooled[:, g, :].rearrange("p (c r) -> p c r", r=GRID_R),
                                        mean.rearrange("p (r c) -> p c r", c=GRID_C),
                                        ppad[:, g, PAD:PAD + T].rearrange("p (r c) -> p c r", c=GRID_C),
                                        ALU.subtract).then_inc(sem["pooled"], 1)
                pool.wait_ge(sem["pooled"], g + 1)

        @block.vector
        def _(dve):
            tmp = mem_["tmp"]
            stages = [
                (kvmem[:, 0], MT, XA_H, XA_D, MT, 256),
                (nraw[:, 0], TT, NA_H, NA_D, KV_JOBS + TT, 0),
                (nraw[:, 1], TT, NA_H, NA_D, KV_JOBS + 2 * TT, 64),
                (nraw[:, 2], TT, XA_H, XA_D, KV_JOBS + 3 * TT, 128),
            ]

            def sums(s):
                t, tiles, heads, dim, need, _ = stages[s]
                n = tiles * heads
                dve.wait_ge(sem["prod_copied"], need)
                flat = t.rearrange("p a b -> p (a b)")
                nc.vector.tensor_tensor(tmp[:, 0:n * dim], flat, flat, ALU.mult).then_inc(sem["squares"], 1)
                dve.wait_ge(sem["squares"], s + 1)
                nc.vector.tensor_reduce(mem_["gss"][:, s, 0:n], tmp[:, 0:n * dim].rearrange("p (g d) -> p g d", d=dim),
                                        AX_X, ALU.add).then_inc(sem["sums"], 1)
                dve.wait_ge(sem["sums"], s + 1)

            def norm(s):
                t, tiles, heads, dim, _, g0 = stages[s]
                n = tiles * heads
                dve.wait_ge(sem["roots"], s + 1)
                nc.vector.reciprocal(mem_["grstd"][:, s, 0:n], mem_["gsd"][:, s, 0:n]).then_inc(sem["grstds"], 1)
                dve.wait_ge(sem["grstds"], s + 1)
                v = t.rearrange("p a (h d) -> p (a h) d", d=dim)
                nc.vector.tensor_tensor(v, v, mem_["grstd"][:, s, 0:n].unsqueeze(2).to_broadcast([P, n, dim]),
                                        ALU.mult).then_inc(sem["scaled"], 1)
                dve.wait_ge(sem["scaled"], s + 1)
                nc.vector.tensor_tensor(v, v, mem_["gains"][:, g0:g0 + dim].unsqueeze(1).to_broadcast([P, n, dim]),
                                        ALU.mult).then_inc(sem["normed"], 1)

            dve.wait_ge(sem["gains_loaded"], 16)
            sums(0)
            sums(1)
            norm(0)
            sums(2)
            norm(1)
            sums(3)
            norm(2)
            norm(3)
            dve.wait_ge(sem["bias_loaded"], 16)
            for v in range(3):
                for h in range(NA_H):
                    table = bias[:, v, h, :].rearrange("p (c r) -> p c r", r=GRID_R)
                    last = nc.vector.tensor_tensor(table, table, mem_["mask"][:, v, :].unsqueeze(2)
                                                   .to_broadcast([P, KCOLS, GRID_R]), ALU.add)
                last.then_inc(sem["masked"], 1)
            dve.wait_ge(sem["masked"], 3)
            for n in range(TURNS):
                dve.wait_ge(sem["turn_ready"], n + 1)
                if n < 2:
                    dst = kmT[:, 2 * n:2 * n + 2, :].rearrange("p a b -> p (a b)")
                else:
                    dst = qkxT[:, (n - 2) // TT, (n - 2) % TT, :]
                nc.vector.tensor_copy(dst, turn_bank[n % 2][:]).then_inc(sem["turn_copied"], 1)

            def logits(u):
                dve.wait_ge(sem["scored"], u + 1)
                if u >= 2:
                    dve.wait_ge(sem["exps"], u - 1)
                out, src = mem_["logit"][:, u % 2, :], score_bank[u % 2][:, 0:M]
                if is_na(u):
                    j, h = divmod(u, NA_H)
                    nc.vector.scalar_tensor_tensor(out, src, NA_D ** -0.5, bias[:, VARIANT[j], h, :],
                                                   ALU.mult, ALU.add).then_inc(sem["logits"], 1)
                else:
                    nc.vector.tensor_scalar(out, src, XA_D ** -0.5, None, ALU.mult).then_inc(sem["logits"], 1)
                dve.wait_ge(sem["logits"], u + 1)
                nc.vector.tensor_reduce(mem_["nmax"][:, u:u + 1], out, AX_X, ALU.max,
                                        negate=True).then_inc(sem["maxima"], 1)

            def normalise(u):
                dve.wait_ge(sem["exps"], u + 1)
                nc.vector.reciprocal(mem_["inv"][:, u:u + 1], mem_["total"][:, u:u + 1]).then_inc(sem["invs"], 1)
                dve.wait_ge(sem["invs"], u + 1)
                p = mem_["prob"][:, u % 3, :]
                nc.vector.tensor_scalar(p, p, mem_["inv"][:, u:u + 1], None, ALU.mult).then_inc(sem["probs"], 1)

            def mixed(u):
                dve.wait_ge(sem["mixed"], u + 1)
                if is_na(u):
                    j, h = divmod(u, NA_H)
                    rows = slice(64 * (h % 2), 64 * (h % 2) + 64)
                    dst, src = yT[rows, 0, h // 2, j * P:(j + 1) * P], out_bank[u % 2][rows, 0:P]
                else:
                    i, h = divmod(u - NJ * NA_H, XA_H)
                    dst, src = yT[:, 2, h, i * P:(i + 1) * P], out_bank[u % 2][:, 0:P]
                nc.vector.tensor_copy(dst, src).then_inc(sem["mixed_copied"], 1)

            for s in range(UNITS + 4):
                if s < UNITS:
                    logits(s)
                if 0 <= s - 1 < UNITS:
                    normalise(s - 1)
                if 0 <= s - 4 < UNITS:
                    mixed(s - 4)


def stage_merge(nc, sem, mem_, io):
    bank = mem_["bank"]
    gate_bank, branch_bank, out_bank = bank[0:2], bank[2:4], bank[4:8]
    ring, xnT, yT = mem_["wring"], mem_["xnT"], mem_["yT"]
    wbr, wout, gate, merged, h = mem_["wbr"], mem_["wout"], mem_["gate"], mem_["merged"], mem_["h"]
    JOBS = 3 * KD
    with nc.Block() as block:

        @block.sync
        def _(sp):
            for b in range(3):
                sp.dma_start(wbr[:, b], io["w_branch"][b]).then_inc(sem["wbr_loaded"][b], 16)
            for cc in range(2, N_GATE):
                sp.wait_ge(sem["gates_ready"], 3 * (cc - 1))
                load_weights(sp, sem, mem_, io, FIRST_GATE + cc)
                if cc == 2:
                    sp.dma_start(wout[:], io["w_out"]).then_inc(sem["wout_loaded"], 16)
                    for i in range(TT):
                        sp.dma_start(h[:, i, :], io["x"][i * P:(i + 1) * P, :]).then_inc(sem["h_loaded"], 16)
            for n in range(2):
                sp.wait_ge(sem["gates_ready"], 3 * (N_GATE - 1 + n))
                load_weights(sp, sem, mem_, io, FIRST_WQ + n)

        @block.tensor
        def _(pe):
            for cc in range(KD):
                n = FIRST_GATE + cc
                weights_arrived(pe, sem, n)
                w = ring[:, n % 2, 0:KD * 3 * P].rearrange("p (k f) -> p k f", k=KD)
                for b in range(3):
                    job = 3 * cc + b
                    if job >= 2:
                        pe.wait_ge(sem["gates"], job - 1)
                    for k in range(KD):
                        last = nc.tensor.matmul(gate_bank[job % 2][:], w[:, k, b * P:(b + 1) * P], xnT[:, k, :],
                                                start=(k == 0), stop=(k == KD - 1))
                    last.then_inc(sem["gates_ready"], 1)
                for b in range(3):
                    job = 3 * cc + b
                    if cc == 0:
                        pe.wait_ge(sem["wbr_loaded"][b], 16)
                    if job >= 2:
                        pe.wait_ge(sem["gated"], job - 1)
                    for k in range(KW):
                        last = nc.tensor.matmul(branch_bank[job % 2][:], wbr[:, b, k, cc * P:(cc + 1) * P],
                                                yT[:, b, k, :], start=(k == 0), stop=(k == KW - 1))
                    last.then_inc(sem["branches_ready"], 1)
            pe.wait_ge(sem["wout_loaded"], 16)
            pe.wait_ge(sem["merged"], 2 * KD)
            for n in range(2 * TT):
                i, half = divmod(n, 2)
                if n >= 4:
                    pe.wait_ge(sem["h_added"], n - 3)
                for k in range(KD):
                    last = nc.tensor.matmul(out_bank[n % 4][:], merged[:, k, i * P:(i + 1) * P],
                                            wout[:, k, half * HALF:(half + 1) * HALF],
                                            start=(k == 0), stop=(k == KD - 1))
                last.then_inc(sem["out_ready"], 1)

        @block.scalar
        def _(act):
            for job in range(JOBS):
                cc, b = divmod(job, 3)
                act.wait_ge(sem["gates_ready"], job + 1)
                if job >= 4:
                    act.wait_ge(sem["gated"], job - 3)
                nc.scalar.activation(gate[:, job % 4, :], gate_bank[job % 2][:], ACT.Sigmoid,
                                     bias=mem_["gate_b"][:, b * KD + cc:b * KD + cc + 1],
                                     scale=1.0).then_inc(sem["gates"], 1)

        @block.vector
        def _(dve):
            tmp = mem_["gtmp"]
            for job in range(JOBS):
                cc, b = divmod(job, 3)
                dve.wait_ge(sem["gates"], job + 1)
                dve.wait_ge(sem["branches_ready"], job + 1)
                dst = merged[:, cc, :] if b == 0 else tmp[:, b - 1, :]
                if b and cc:
                    dve.wait_ge(sem["merged"], 2 * (cc - 1) + b)
                nc.vector.tensor_tensor(dst, branch_bank[job % 2][:], gate[:, job % 4, :],
                                        ALU.mult).then_inc(sem["gated"], 1)
                dve.wait_ge(sem["gated"], job + 1)
                if b:
                    if b == 2:
                        dve.wait_ge(sem["merged"], 2 * cc + 1)
                    nc.vector.tensor_tensor(merged[:, cc, :], merged[:, cc, :], dst,
                                            ALU.add).then_inc(sem["merged"], 1)
            dve.wait_ge(sem["h_loaded"], 16 * TT)
            for n in range(2 * TT):
                i, half = divmod(n, 2)
                dve.wait_ge(sem["out_ready"], n + 1)
                part = h[:, i, half * HALF:(half + 1) * HALF]
                nc.vector.tensor_tensor(part, part, out_bank[n % 4][:], ALU.add).then_inc(sem["h_added"], 1)


def stage_query(nc, sem, mem_, io):
    bank, ident = mem_["bank"], mem_["ident"]
    prod_bank, turn_bank = bank[0:4], bank[4:6]
    h, ring = mem_["h"], mem_["wring"]
    hn32, hnr, hnl, qpT = mem_["hn32"], mem_["hnr"], mem_["hnl"], mem_["qpT"]
    with nc.Block() as block:

        @block.sync
        def _(sp):
            sp.dma_start(mem_["keysT"][:], io["keysT"]).then_inc(sem["keys_loaded"], 16)
            for n in range(2, N_WQ):
                sp.wait_ge(sem["query_ready"], 4 * (n - 1))
                load_weights(sp, sem, mem_, io, FIRST_WQ + n)

        @block.scalar
        def _(act):
            for i in range(TT):
                if i:
                    act.wait_ge(sem["h_squares"], i)
                nc.scalar.activation(mem_["junk2"][:], h[:, i, :], ACT.Square,
                                     accum_out=mem_["ss"][:, i:i + 1]).then_inc(sem["h_squares"], 1)
                act.wait_ge(sem["h_squares"], i + 1)
                nc.scalar.activation(mem_["sd"][:, i:i + 1], mem_["ss"][:, i:i + 1], ACT.Sqrt,
                                     scale=1.0 / D, bias=mem_["eps"][:, 0:1]).then_inc(sem["h_roots"], 1)
            for n in range(HP):
                act.wait_ge(sem["query_ready"], n + 1)
                nc.scalar.activation(qpT[:, n, :], prod_bank[n % 4][:], ACT.Copy).then_inc(sem["query_copied"], 1)

        @block.vector
        def _(dve):
            def split(i):
                for half in range(2):
                    n = 2 * i + half
                    dve.wait_ge(sem["hT_ready"], n + 1)
                    where = (slice(None), slice(4 * half, 4 * half + 4), slice(i * P, (i + 1) * P))
                    gain = mem_["ffn_g"][:, 4 * half:4 * half + 4].unsqueeze(2).to_broadcast([P, 4, P])
                    nc.vector.tensor_tensor(hn32[where], bank4(turn_bank[n % 2]), gain,
                                            ALU.mult).then_inc(sem["hT_copied"], 1)
                    dve.wait_ge(sem["hT_copied"], n + 1)
                    nc.vector.tensor_copy(hnr[where], hn32[where]).then_inc(sem["hT_rounded"], 1)
                    dve.wait_ge(sem["hT_rounded"], n + 1)
                    nc.vector.tensor_tensor(hnl[where], hn32[where], hnr[where].bitcast(F32),
                                            ALU.subtract).then_inc(sem["hT_rest"], 1)

            for i in range(TT):
                dve.wait_ge(sem["h_roots"], i + 1)
                nc.vector.reciprocal(mem_["rstd"][:, i:i + 1], mem_["sd"][:, i:i + 1]).then_inc(sem["h_rstd"], 1)
                dve.wait_ge(sem["h_rstd"], i + 1)
                if i >= 2:
                    dve.wait_ge(sem["hT_ready"], 2 * (i - 1))
                nc.vector.tensor_scalar(mem_["hn"][:, i % 2, :], h[:, i, :], mem_["rstd"][:, i:i + 1], None,
                                        ALU.mult).then_inc(sem["h_normed"], 1)
                if i:
                    split(i - 1)
            split(TT - 1)

        @block.tensor
        def _(pe):
            for i in range(TT):
                pe.wait_ge(sem["h_normed"], i + 1)
                for half in range(2):
                    n = 2 * i + half
                    if n >= 2:
                        pe.wait_ge(sem["hT_copied"], n - 1)
                    for q in range(4):
                        k = 4 * half + q
                        last = nc.tensor.transpose(bank4(turn_bank[n % 2])[:, q, :],
                                                   mem_["hn"][:, i % 2, k * P:(k + 1) * P], ident)
                    last.then_inc(sem["hT_ready"], 1)
            pe.wait_ge(sem["hT_copied"], 2 * TT)
            for n in range(HP):
                load = FIRST_WQ + n // 4
                if n % 4 == 0:
                    weights_arrived(pe, sem, load)
                w = ring[:, load % 2, :].rearrange("p (k f) -> p k f", k=KD)
                if n >= 4:
                    pe.wait_ge(sem["query_copied"], n - 3)
                for k in range(KD):
                    last = nc.tensor.matmul(prod_bank[n % 4][:], w[:, k, (n % 4) * P:(n % 4 + 1) * P], hn32[:, k, :],
                                            start=(k == 0), stop=(k == KD - 1))
                last.then_inc(sem["query_ready"], 1)


def stage_select(nc, sem, mem_, io):
    bank, ident = mem_["bank"], mem_["ident"]
    qpT, keysT, selT = mem_["qpT"], mem_["keysT"], mem_["selT"]
    score, rest = mem_["score"], mem_["score_rest"]
    best, where, bestf = mem_["best"], mem_["where"], mem_["wheref"]
    cand, crest = mem_["cand"], mem_["cand_rest"]
    top, pos = mem_["top"], mem_["pos"]
    part, partf, pick = mem_["part"], mem_["partf"], mem_["pick"]
    low = -3.0e38

    with nc.Block() as block:

        @block.sync
        def _(sp):
            sp.wait_ge(sem["keys_loaded"], 16)

        @block.tensor
        def _(pe):
            with pe.Fori(0, TT) as i:
                pe.wait_ge(sem["keys_loaded"], 16)
                pe.wait_ge(sem["tile_queries"], i + 1)
                for b in range(4):
                    pe.wait_ge(sem["score_room"], 4 * i + b + 1)
                    for q in range(4):
                        f = 4 * b + q
                        last = nc.tensor.matmul(bank4(bank[b])[:, q, :], mem_["qtile"][:, f, :], keysT[:, f, :],
                                                start=True, stop=True)
                    last.then_inc(sem["scores_ready"], 1)
                pe.wait_ge(sem["picked"], 3 * i + 3)
                pe.wait_ge(sem["turn_room"], i + 1)
                for n in range(3):
                    last = nc.tensor.transpose(bank4(bank[4])[:, n, :], pick[:, n, :], ident)
                last.then_inc(sem["picks_turned"], 1)

        @block.scalar
        def _(act):
            act.sem_inc(sem["score_room"], 4)
            act.sem_inc(sem["turn_room"], 1)
            with act.Fori(0, TT) as i:
                nc.scalar.activation(mem_["qtile"][:], qpT[:, :, bass.ds(i * P, P)],
                                     ACT.Copy).then_inc(sem["tile_queries"], 1)
                for b in range(4):
                    held(act, (sem["scores_ready"], 4 * i + b + 1), (sem["scores_used"], i + 1))
                    nc.scalar.activation(score[:, 4 * b:4 * b + 4, :], bank4(bank[b]),
                                         ACT.Copy).then_inc(sem["score_room"], 1)
                held(act, (sem["top_ready"], i + 1))
                nc.scalar.activation(mem_["expo"][:], mem_["shifted"][:], ACT.Exp).then_inc(sem["expo_ready"], 1)
                held(act, (sem["picks_turned"], i + 1))
                nc.scalar.activation(selT[:, :, bass.ds(i * P, P)], bank4(bank[4])[:, 0:3, :],
                                     ACT.Copy).then_inc(sem["turn_room"], 1)

        @block.vector
        def _(dve):
            count = [0]
            PER_TILE = 18

            def done(ins):
                ins.then_inc(sem["select_step"], 1)
                count[0] += 1
                held(dve, (sem["select_step"], tile * PER_TILE + count[0]))

            dve.sem_inc(sem["scores_used"], 1)
            with dve.Fori(0, TT) as tile:
                held(dve, (sem["score_room"], 4 * tile + 8))
                for f in range(HP):
                    ins = nc.vector.max(best[:, f, 0:8], score[:, f, :])
                done(ins)
                for f in range(HP):
                    nc.vector.max_index(where[:, f, 0:8], best[:, f, 0:8], score[:, f, :])
                for f in range(HP):
                    ins = nc.vector.match_replace(rest[:, f, :], best[:, f, 0:8], score[:, f, :], low)
                done(ins)
                dve.sem_inc(sem["scores_used"], 1)
                for f in range(HP):
                    ins = nc.vector.max(best[:, f, 8:16], rest[:, f, :])
                done(ins)
                for f in range(HP):
                    ins = nc.vector.max_index(where[:, f, 8:16], best[:, f, 8:16], rest[:, f, :])
                done(ins)
                done(nc.vector.tensor_copy(bestf[:], where[:]))
                pair = best[:].rearrange("p (h two) k -> p h two k", two=2)
                a = pair[:, :, 0, :].unsqueeze(3).to_broadcast([P, HEADS, TOPK, TOPK])
                b = pair[:, :, 1, :].unsqueeze(2).to_broadcast([P, HEADS, TOPK, TOPK])
                done(nc.vector.tensor_tensor(cand[:].rearrange("p h (a b) -> p h a b", a=TOPK), a, b, ALU.add))
                for h in range(HEADS):
                    ins = nc.vector.max(top[:, h, 0:8], cand[:, h, :])
                done(ins)
                for h in range(HEADS):
                    nc.vector.max_index(pos[:, h, 0:8], top[:, h, 0:8], cand[:, h, :])
                for h in range(HEADS):
                    ins = nc.vector.match_replace(crest[:, h, :], top[:, h, 0:8], cand[:, h, :], low)
                done(ins)
                for h in range(HEADS):
                    ins = nc.vector.max(top[:, h, 8:16], crest[:, h, :])
                done(ins)
                for h in range(HEADS):
                    ins = nc.vector.max_index(pos[:, h, 8:16], top[:, h, 8:16], crest[:, h, :])
                done(ins)
                nc.vector.tensor_tensor(mem_["shifted"][:], top[:], top[:, :, 0:1].to_broadcast([P, HEADS, TOPK]),
                                        ALU.subtract).then_inc(sem["top_ready"], 1)
                nc.vector.tensor_scalar(part[:, 0], pos[:], 4, None, ALU.logical_shift_right)
                done(nc.vector.tensor_scalar(part[:, 1], pos[:], 15, None, ALU.bitwise_and))
                done(nc.vector.tensor_copy(partf[:], part[:]))
                pairf = bestf[:].rearrange("p (h two) k -> p h two k", two=2)
                full = [P, HEADS, TOPK, TOPK]
                eq = mem_["eq"][:].rearrange("p (h k a) -> p h k a", h=HEADS, k=TOPK)
                for n in range(2):
                    if n == 0:
                        held(dve, (sem["turn_room"], tile + 1))
                    done(nc.vector.tensor_tensor(eq, partf[:, n].unsqueeze(3).to_broadcast(full),
                                                 mem_["iota"][:, 0:TOPK].unsqueeze(1).unsqueeze(1).to_broadcast(full),
                                                 ALU.is_equal))
                    done(nc.vector.tensor_tensor(eq, eq, pairf[:, :, n, :].unsqueeze(2).to_broadcast(full), ALU.mult))
                    nc.vector.tensor_reduce(pick[:, n, :].rearrange("p (h k) -> p h k", h=HEADS), eq, AX_X,
                                            ALU.add).then_inc(sem["picked"], 1)
                    held(dve, (sem["picked"], 3 * tile + n + 1))
                held(dve, (sem["expo_ready"], tile + 1))
                done(nc.vector.tensor_reduce(mem_["esum"][:], mem_["expo"][:], AX_X, ALU.add))
                done(nc.vector.reciprocal(mem_["einv"][:], mem_["esum"][:]))
                nc.vector.tensor_tensor(pick[:, 2, :].rearrange("p (h k) -> p h k", h=HEADS), mem_["expo"][:],
                                        mem_["einv"][:].unsqueeze(2).to_broadcast([P, HEADS, TOPK]),
                                        ALU.mult).then_inc(sem["picked"], 1)
            assert count[0] == PER_TILE


def stage_table(nc, sem, mem_, io):
    bank = mem_["bank"]
    selT, one, two, block_ = mem_["selT"], mem_["onehot1"], mem_["onehot2"], mem_["table"]
    STEP = 4
    PER = 2 * TB // STEP
    with nc.Block() as block:

        @block.vector
        def _(dve):
            dve.sem_inc(sem["onehot_room"], 2)
            with dve.Fori(0, NTB // 2) as it:
                for s in range(PER):
                    dve.wait_ge(sem["onehot_room"], PER * it + s + 1)
                    for q in range(STEP):
                        t = bass.ds(it * (2 * TB) + (s * STEP + q), 1)
                        slot = (s * STEP + q) % (2 * STEP)
                        nc.vector.tensor_scalar(one[:, slot, :], mem_["iota"], selT[:, 0, t], None, ALU.is_equal)
                        last = nc.vector.tensor_scalar(two[:, slot, :], mem_["iota"], selT[:, 1, t], selT[:, 2, t],
                                                       ALU.is_equal, ALU.mult)
                    last.then_inc(sem["onehots"], 1)

        @block.tensor
        def _(pe):
            with pe.Fori(0, NTB // 2) as it:
                for s in range(PER):
                    pe.wait_ge(sem["onehots"], PER * it + s + 1)
                    pe.wait_ge(sem["table_room"], PER * it + s + 1)
                    for q in range(STEP):
                        slot = (s * STEP + q) % (2 * STEP)
                        last = nc.tensor.matmul(bank4(bank[s % 4])[:, q, :], one[:, slot, :], two[:, slot, :],
                                                start=True, stop=True)
                    last.then_inc(sem["onehot_room"], 1)

        @block.scalar
        def _(act):
            act.sem_inc(sem["table_room"], 4)
            with act.Fori(0, NTB // 2) as it:
                for s in range(PER):
                    waits = [(sem["onehot_room"], PER * it + s + 3)]
                    if s % (PER // 2) == 0:
                        waits.append((sem["table_stored"][2 * s // PER], 16 * it + 16))
                    held(act, *waits)
                    b, t0 = divmod(s * STEP, TB)
                    nc.scalar.activation(block_[:, b, :, t0:t0 + STEP],
                                         bank4(bank[s % 4]).rearrange("p t i -> p i t"),
                                         ACT.Copy).then_inc(sem["table_room"], 1)

        @block.sync
        def _(sp):
            for b in range(2):
                sp.sem_inc(sem["table_stored"][b], 16)
            with sp.Fori(0, NTB // 2) as it:
                for b in range(2):
                    sp.wait_ge(sem["table_room"], PER * it + (PER // 2) * (b + 1) + 4)
                    sp.dma_start(io["table"][:, bass.ds(2 * it + b, 1), :],
                                 block_[:, b].rearrange("p i t -> p (i t)").unsqueeze(1)
                                 ).then_inc(sem["table_stored"][b], 16)
            for b in range(2):
                sp.wait_ge(sem["table_stored"][b], 16 * (NTB // 2) + 16)


def stage_experts(nc, sem, mem_, io):
    bank = mem_["bank"]
    hid_bank, sum_bank = bank[0:2], bank[2:6]
    h, hnr, hnl = mem_["h"], mem_["hnr"], mem_["hnl"]
    uraw, vraw, ur, ul, vr, vl = (mem_[n] for n in ("uraw", "vraw", "ur", "ul", "vr", "vl"))
    wr, wl, act_, w32, tab = (mem_[n] for n in ("wr", "wl", "act", "w32", "tab"))
    LOOPS = (GROUPS - 4) // 2

    def groups(eng, body):
        for g in range(2):
            for k in range(GC):
                body(g, g, k, g * GC + k, g == 0, False)
        with eng.Fori(0, LOOPS) as it:
            for gg in range(2):
                for k in range(GC):
                    body(2 * it + (2 + gg), gg, k, 2 * GC * it + (GC * (2 + gg) + k), False, False)
        for g in (GROUPS - 2, GROUPS - 1):
            for k in range(GC):
                body(g, g % 2, k, g * GC + k, False, g == GROUPS - 1)

    with nc.Block() as block:

        @block.sync
        def _(sp):
            def load(g, par, k, c, first, final):
                s = k % 2
                per = g * (GC // 2) + (k // 2)
                if not (first and k < 2):
                    sp.wait_ge(sem["u_rest"], c - 1)
                sp.dma_start(uraw[:, s, :], io["u"][bass.ds(c, 1)].rearrange("a p n -> p (a n)")
                             ).then_inc(sem["u_loaded"][s], 16)
                if not (first and k < 2):
                    sp.wait_ge(sem["v_rest"], c - 1)
                sp.dma_start(vraw[:, s, :], io["v"][bass.ds(c, 1)].rearrange("a p n -> p (a n)")
                             ).then_inc(sem["v_loaded"][s], 16)
                if k == 0:
                    if not first:
                        at_least(sp, sem["weighted"], GC * g - GC)
                    sp.dma_start(tab[:, par], io["table"][:, :, bass.ds(g * (GC * TB), GC * TB)]
                                 ).then_inc(sem["tab_loaded"][par], 16)

            groups(sp, load)
            for i in range(TT):
                sp.wait_ge(sem["sum_room"], 4 + 2 * TT * (GROUPS - 1) + 2 * (i + 1))
                sp.dma_start(io["out"][i * P:(i + 1) * P, :], h[:, i, :]).then_inc(sem["stored"], 16)
            sp.wait_ge(sem["stored"], 16 * TT)

        @block.scalar
        def _(act):
            def round_u(c, s, n):
                waits = [(sem["u_loaded"][s], n)]
                if not (isinstance(c, int) and c < 2):
                    waits.append((sem["hidden"], c - 1))
                held(act, *waits)
                nc.scalar.activation(ur[:, s, :], uraw[:, s, :], ACT.Copy).then_inc(sem["u_rounded"], 1)

            def step(g, par, k, c, first, final):
                half = g * (GC // 2)
                if not (final and k == GC - 1):
                    k1 = k + 1
                    round_u(c + 1, k1 % 2, 16 * half + 16 * (k1 // 2 + 1))
                waits = [(sem["v_loaded"][k % 2], 16 * half + 16 * (k // 2 + 1))]
                if not first:
                    waits.append((sem["summed"], 2 * TT * g - 2 * TT))
                held(act, *waits)
                nc.scalar.activation(vr[:, par, k, :], vraw[:, k % 2, :], ACT.Copy).then_inc(sem["v_rounded"], 1)
                waits = [(sem["hidden"], c + 1)]
                if not (first and k < 2):
                    waits.append((sem["weighted"], c - 1))
                held(act, *waits)
                nc.scalar.activation(act_[:, k % 2, :], hid_bank[k % 2][:], ACT.Gelu).then_inc(sem["gelus"], 1)

            round_u(0, 0, 16)
            groups(act, step)

        @block.vector
        def _(dve):
            def rest_u(c, s):
                dve.wait_ge(sem["u_rounded"], c + 1)
                if not (isinstance(c, int) and c < 2):
                    dve.wait_ge(sem["hidden"], c - 1)
                nc.vector.tensor_tensor(ul[:, s, :], uraw[:, s, :], ur[:, s, :].bitcast(F32),
                                        ALU.subtract).then_inc(sem["u_rest"], 1)

            def add_sum(j, n):
                dve.wait_ge(sem["summed"], n + 1)
                i, half = divmod(j, 2)
                part = h[:, i, half * HALF:(half + 1) * HALF]
                return nc.vector.tensor_tensor(part, part, sum_bank[j % 4][:], ALU.add)

            def step(g, par, k, c, first, final):
                if not (final and k == GC - 1):
                    rest_u(c + 1, (k + 1) % 2)
                dve.wait_ge(sem["v_rounded"], c + 1)
                if not first:
                    at_least(dve, sem["summed"], 2 * TT * g - 2 * TT)
                nc.vector.tensor_tensor(vl[:, par, k, :], vraw[:, k % 2, :], vr[:, par, k, :].bitcast(F32),
                                        ALU.subtract).then_inc(sem["v_rest"], 1)
                dve.wait_ge(sem["gelus"], c + 1)
                if k == 0:
                    dve.wait_ge(sem["tab_loaded"][par], (g + (2 - par)) * 8)
                blocks = [P, NTB, TB]
                nc.vector.tensor_tensor(w32[:, k % 2, :].rearrange("p (a b) -> p a b", a=NTB),
                                        act_[:, k % 2, :].rearrange("p (a b) -> p a b", a=NTB),
                                        tab[:, par, :, k * TB:(k + 1) * TB], ALU.mult).then_inc(sem["weighted"], 1)
                dve.wait_ge(sem["weighted"], c + 1)
                nc.vector.tensor_copy(wr[:, par, k, :], w32[:, k % 2, :]).then_inc(sem["w_rounded"], 1)
                dve.wait_ge(sem["w_rounded"], c + 1)
                nc.vector.tensor_tensor(wl[:, par, k, :], w32[:, k % 2, :], wr[:, par, k, :].bitcast(F32),
                                        ALU.subtract).then_inc(sem["w_rest"], 1)
                if not first:
                    for j in (2 * k, 2 * k + 1):
                        add_sum(j, 2 * TT * g + (j - 2 * TT)).then_inc(sem["sum_room"], 1)

            dve.sem_inc(sem["sum_room"], 4)
            rest_u(0, 0)
            groups(dve, step)
            for j in range(2 * TT):
                add_sum(j, 2 * TT * (GROUPS - 1) + j).then_inc(sem["sum_room"], 1)

        @block.tensor
        def _(pe):
            def hidden(k, c):
                pe.wait_ge(sem["u_rest"], c + 1)
                if not (isinstance(c, int) and c < 2):
                    pe.wait_ge(sem["gelus"], c - 1)
                s, out = k % 2, hid_bank[k % 2][:]
                for d in range(KD):
                    cols = slice(d * P, (d + 1) * P)
                    nc.tensor.matmul(out, ur[:, s, cols], hnr[:, d, :], start=(d == 0), stop=False)
                    nc.tensor.matmul(out, ur[:, s, cols], hnl[:, d, :], start=False, stop=False)
                    last = nc.tensor.matmul(out, ul[:, s, cols], hnr[:, d, :], start=False, stop=(d == KD - 1))
                last.then_inc(sem["hidden"], 1)

            def sum_tile(j, n, par):
                pe.wait_ge(sem["sum_room"], n + 1)
                i, half = divmod(j, 2)
                out = sum_bank[j % 4][:]
                rows, cols = slice(i * P, (i + 1) * P), slice(half * HALF, (half + 1) * HALF)
                for k in range(GC):
                    nc.tensor.matmul(out, wr[:, par, k, rows], vr[:, par, k, cols], start=(k == 0), stop=False)
                    nc.tensor.matmul(out, wr[:, par, k, rows], vl[:, par, k, cols], start=False, stop=False)
                    last = nc.tensor.matmul(out, wl[:, par, k, rows], vr[:, par, k, cols],
                                            start=False, stop=(k == GC - 1))
                last.then_inc(sem["summed"], 1)

            def step(g, par, k, c, first, final):
                hidden(k, c)
                if not first:
                    if k == 0:
                        pe.wait_ge(sem["w_rest"], GC * g)
                        pe.wait_ge(sem["v_rest"], GC * g)
                    for j in (2 * k, 2 * k + 1):
                        sum_tile(j, 2 * TT * g + (j - 2 * TT), 1 - par)

            groups(pe, step)
            pe.wait_ge(sem["w_rest"], GC * GROUPS)
            pe.wait_ge(sem["v_rest"], GC * GROUPS)
            for j in range(2 * TT):
                sum_tile(j, 2 * TT * (GROUPS - 1) + j, 1)


def build(nc, io):
    names = """consts_loaded eps_set x_squares x_roots x_rstd x_normed xT_ready xT_copied
        bias_loaded gains_loaded pool_loaded prod_ready prod_copied vsh_loaded normed turn_ready turn_copied
        scored logits maxima exps invs probs probsT probsT_copied mixed mixed_copied pads_cleared pool_step
        pooled squares sums roots grstds scaled masked gates_ready gates gated branches_ready merged
        wout_loaded h_loaded h_added out_ready keys_loaded query_ready query_copied h_squares h_roots h_rstd
        h_normed hT_ready hT_copied hT_rounded hT_rest scores_ready score_room scores_used turn_room tile_queries
        top_ready expo_ready picks_turned picked select_step onehot_room onehots table_room
        u_rest v_rest u_rounded v_rounded hidden gelus weighted w_rounded w_rest summed sum_room
        stored""".split()
    sem = {n: nc.alloc_semaphore(n) for n in names}
    for n, k in (("x_loaded", TT + MT), ("w_loaded", 2), ("wbr_loaded", 3), ("table_stored", 2), ("u_loaded", 2),
                 ("v_loaded", 2), ("tab_loaded", 2)):
        sem[n] = [nc.alloc_semaphore(f"{n}{i}") for i in range(k)]

    m = {"bank": [nc.alloc_psum_tensor(f"bank{i}", [P, HALF], F32) for i in range(8)]}

    def at(kb, name, shape, dtype=F32):
        m[name] = sbuf(nc, name, shape, dtype, kb)

    at(0, "wring", [P, 2, KD * W])
    at(32, "h", [P, TT, D])
    at(48, "xnT", [P, KD, T])
    at(64, "memnT", [P, KD, M])
    at(203.5, "consts", [P, CONST_COLS])
    c0 = 0
    for name, cols in CONSTS:
        m[name] = m["consts"][:, c0:c0 + cols]
        c0 += cols
    m["mask"] = m["mask"].rearrange("p (v c) -> p v c", v=3)
    m["edge"] = m["edge"].rearrange("p (g e t) -> p g e t", g=4, e=2)
    at(206.5, "eps", [P, 8])
    at(206.625, "ss", [P, 8])
    at(206.75, "sd", [P, 8])
    at(206.875, "rstd", [P, 8])
    at(160, "xbuf", [P, TT + MT, D])
    at(184, "junk", [P, D])
    at(72, "yT", [P, 3, KW, T])
    at(96, "nraw", [P, 3, TT, W])
    at(120, "vna", [P, TT, W])
    at(128, "vsh", [P, 3, W])
    at(134, "kvmem", [P, 2, MT, W])
    at(142, "qkxT", [P, 3, KW, T])
    at(166, "kmT", [P, XA_H, M])
    at(170, "tmp", [P, TT * W])
    at(170, "logit", [P, 2, M])
    at(172, "prob", [P, 3, M])
    at(175, "probT", [P, 2, M])
    at(178, "bias", [P, 3, NA_H, M])
    at(64, "pooledT", [P, 4, T])
    at(32, "ppad", [P, 4, T + 2 * PAD])
    at(40.5, "wsum", [P, 2, T + 2 * PAD])
    at(45, "gains", [P, 2 * NA_D + 2 * XA_D])
    at(202, "stats", [P, 4 * UNITS])
    m["nmax"], m["total"], m["inv"] = (m["stats"][:, i * UNITS:(i + 1) * UNITS] for i in range(3))
    at(46.5, "gss", [P, 4, 32])
    at(47, "gsd", [P, 4, 32])
    at(47.5, "grstd", [P, 4, 32])
    at(96, "pool_w", [P, 4, P])
    at(96, "wbr", [P, 3, KW, D])
    at(144, "wout", [P, KD, D])
    at(176, "gate", [P, 4, T])
    at(184, "merged", [P, KD, T])
    at(64, "gtmp", [P, 2, T])
    at(48, "hnr", [P, KD, T], F32R)
    at(64, "hnl", [P, KD, T], F32R)
    at(80, "hn32", [P, KD, T])
    at(96, "qpT", [P, HP, T])
    at(128, "hn", [P, 2, D])
    at(136, "junk2", [P, D])
    at(140, "keysT", [P, HP, KEYS])
    at(80, "selT", [P, 3, T])
    at(86, "best", [P, HP, TOPK])
    at(87, "where", [P, HP, TOPK], U32)
    at(88, "wheref", [P, HP, TOPK])
    at(89, "top", [P, HEADS, TOPK])
    at(89.5, "pos", [P, HEADS, TOPK], U32)
    at(90, "part", [P, 2, HEADS, TOPK], U32)
    at(91, "partf", [P, 2, HEADS, TOPK])
    at(92, "pick", [P, 3, HEADS * TOPK])
    at(93.5, "shifted", [P, HEADS, TOPK])
    at(94, "expo", [P, HEADS, TOPK])
    at(94.5, "esum", [P, HEADS])
    at(94.625, "einv", [P, HEADS])
    at(148, "score", [P, HP, KEYS])
    at(156, "score_rest", [P, HP, KEYS])
    at(164, "cand", [P, HEADS, TOPK * TOPK])
    at(172, "cand_rest", [P, HEADS, TOPK * TOPK])
    at(188, "qtile", [P, HP, P])
    at(180, "eq", [P, HEADS * TOPK * TOPK])
    at(96, "table", [P, 2, KEYS, TB])
    at(128, "onehot1", [P, 8, KEYS])
    at(132, "onehot2", [P, 8, KEYS])
    at(0, "uraw", [P, 2, D])
    at(8, "vraw", [P, 2, D])
    at(16, "ur", [P, 2, D], F32R)
    at(24, "ul", [P, 2, D], F32R)
    at(80, "tab", [P, 2, NTB, GC * TB])
    at(96, "wr", [P, 2, GC, T], F32R)
    at(112, "wl", [P, 2, GC, T], F32R)
    at(128, "vr", [P, 2, GC, D], F32R)
    at(160, "vl", [P, 2, GC, D], F32R)
    at(192, "act", [P, 2, T])
    at(196, "w32", [P, 2, T])

    stage_norm(nc, sem, m, io)
    stage_attend(nc, sem, m, io)
    stage_merge(nc, sem, m, io)
    stage_query(nc, sem, m, io)
    stage_select(nc, sem, m, io)
    stage_table(nc, sem, m, io)
    stage_experts(nc, sem, m, io)


CONSTS = [("ident", P), ("iota", P), ("edge", 4 * 2 * PAD), ("mix_g", KD), ("mem_g", KD), ("ffn_g", KD),
          ("gate_b", 3 * KD), ("pool_scale", KW), ("mask", 3 * KCOLS)]
CONST_COLS = sum(c for _, c in CONSTS)


def host_constants():
    col = np.arange(QCOLS)
    mask = np.zeros((QCOLS, 3, KCOLS), np.float32)
    for v, j in enumerate((0, 1, 3)):
        first = np.clip(j * QCOLS + col - WCOLS // 2, 0, GRID_C - WCOLS)[:, None]
        key = KEY0[j] // GRID_R + np.arange(KCOLS)[None, :]
        mask[:, v] = np.where((key >= first) & (key < first + WCOLS), 0.0, MASKED)
    mask = np.repeat(mask, GRID_R, axis=0).reshape(P, 3 * KCOLS)
    edge = np.ones((4, 2, PAD), np.float32)
    t = np.arange(T)
    for g, w in enumerate(POOL):
        count = np.clip(t + w // 2, 0, T) - np.clip(t - w // 2, 0, T)
        ratio = (w / count).astype(np.float32)
        edge[g] = ratio[:PAD], ratio[-PAD:]
    edge = np.broadcast_to(edge.reshape(1, -1), (P, 4 * 2 * PAD))
    return mask, edge


def rpb_windows(rpb):
    c, r = np.arange(P) // GRID_R, np.arange(P) % GRID_R
    kc, kr = np.arange(M) // GRID_R, np.arange(M) % GRID_R
    out = []
    for j in (0, 1, 3):
        dc = np.clip(KEY0[j] // GRID_R + kc[None, :] - (j * QCOLS + c[:, None]), 1 - WCOLS, WCOLS - 1) + WCOLS - 1
        dr = kr[None, :] - r[:, None] + GRID_R - 1
        out.append(rpb[:, dr, dc])
    return np.stack(out).transpose(2, 0, 1, 3)


def kernel(x, mem, mix_norm_g, mem_norm_g, w_in, gate_b, w_mem_kv, na_q_g, na_k_g, na_rpb,
           pool_w, pool_scale, xa_q_g, xa_k_g, w_branch_na, w_branch_pool, w_branch_xa, w_out,
           ffn_norm_g, peer_w_q, peer_sub_keys, peer_u, peer_v):
    import concourse.bacc as bacc
    from concourse.bass_utils import run_bass_kernel_spmd

    def arr(a):
        return np.asarray(a)

    def by_rows(w, blocks):
        w = arr(w)
        k, n = w.shape[0] // P, w.shape[1] // blocks
        return w.reshape(k, P, blocks, n).transpose(2, 1, 0, 3).reshape(blocks, P, k * n)

    def per_feature(v):
        return arr(v).reshape(-1, P).T

    def rows(v):
        return np.broadcast_to(arr(v).reshape(1, -1), (P, arr(v).size))

    mask, edge = host_constants()
    f32 = np.float32
    w = arr(w_in)[0]
    mixer, gates = w[:, :N_MIX * W], w[:, N_MIX * W:]
    order = (0, 1, 4, 2, 3)
    mixer = by_rows(mixer, N_MIX)[list(order)]
    gates = gates.reshape(KD, P, 3, KD, P).transpose(3, 1, 0, 2, 4).reshape(KD, P, KD * 3 * P)
    consts = np.concatenate([
        np.eye(P, dtype=f32), np.broadcast_to(np.arange(P, dtype=f32), (P, P)), edge, per_feature(mix_norm_g),
        per_feature(mem_norm_g), per_feature(ffn_norm_g), per_feature(gate_b), per_feature(pool_scale), mask], axis=1)
    by_column = arr(x).reshape(GRID_R, GRID_C, D).transpose(1, 0, 2).reshape(T, D)
    ins = {
        "x": by_column,
        "mem": arr(mem)[0],
        "consts": consts,
        "gains": np.concatenate([rows(na_q_g), rows(na_k_g), rows(xa_q_g), rows(xa_k_g)], axis=1),
        "w_kv": by_rows(arr(w_mem_kv)[0], N_KV),
        "w_mix": mixer,
        "w_gate": gates,
        "bias": rpb_windows(arr(na_rpb)[0]),
        "pool_w": arr(pool_w)[0].transpose(1, 0, 2),
        "w_branch": np.stack([arr(b)[0].reshape(KW, P, D).transpose(1, 0, 2)
                              for b in (w_branch_na, w_branch_pool, w_branch_xa)]),
        "w_out": arr(w_out)[0].reshape(KD, P, D).transpose(1, 0, 2),
        "w_q": by_rows(arr(peer_w_q)[0], N_WQ),
        "keysT": arr(peer_sub_keys)[0].reshape(HP, KEYS, P).transpose(2, 0, 1),
        "u": arr(peer_u)[0].reshape(KEYS, KEYS, KD, P).transpose(1, 3, 2, 0).reshape(KEYS, P, D),
        "v": arr(peer_v)[0].reshape(KEYS, KEYS, D).transpose(1, 0, 2),
    }
    ins = {n: np.ascontiguousarray(a) for n, a in ins.items()}
    nc = bacc.Bacc("TRN2", target_bir_lowering=False, num_devices=1)
    io = {n: nc.dram_tensor(f"in_{n}", a.shape, F32, kind="ExternalInput").ap() for n, a in ins.items()}
    io["out"] = nc.dram_tensor("out_h", (T, D), F32, kind="ExternalOutput").ap()
    io["table"] = nc.dram_tensor("table_spilled", (P, NTB, KEYS * TB), F32, kind="Internal").ap()
    build(nc, io)
    r = run_bass_kernel_spmd(nc, [{f"in_{n}": a for n, a in ins.items()}], core_ids=[0])
    out = np.asarray(r.results[0]["out_h"])
    return out.reshape(GRID_C, GRID_R, D).transpose(1, 0, 2).reshape(1, T, D)
```

```python
import numpy as np

import concourse.bass as bass
from concourse import mybir
from concourse.alu_op_type import AluOpType as ALU

F32 = mybir.dt.float32
F32R = mybir.dt.float32r
U32 = mybir.dt.uint32
ACT = mybir.ActivationFunctionType
AX_X = mybir.AxisListType.X

P = 128
D = 1024
KD = D // P
T = 512
TT = T // P
M = 256
MT = M // P
W = 512
KW = W // P
NORM_EPS = 1e-6
MASKED = -1e30

GRID_R, GRID_C = 8, 64
NA_H, NA_D = 8, 64
XA_H, XA_D = 4, 128
QCOLS, KCOLS, WCOLS = 16, 32, 16
NJ = GRID_C // QCOLS
KEY0 = [min(max(j * QCOLS - WCOLS // 2, 0), GRID_C - KCOLS) * GRID_R for j in range(NJ)]
VARIANT = [0, 1, 1, 2]
POOL = (2, 4, 8, 16)
PAD = 8

HEADS, KEYS, TOPK = 8, 128, 16
HP = 2 * HEADS
TB = 32
NTB = T // TB
GC = 4
CHUNKS = KEYS
GROUPS = CHUNKS // GC
HALF = 512

BASE = 16640
KB = 1024


def at_least(eng, sem, value):
    if isinstance(value, int) and value <= 0:
        return
    eng.wait_ge(sem, value)


def held(eng, *waits):
    for sem, value in waits:
        at_least(eng, sem, value)
    eng.nop(nofuse=True)


def sbuf(nc, name, shape, dtype, kb):
    return nc.alloc_sbuf_tensor_at(name, shape, dtype, offset=BASE + int(kb * KB))


def stage_norm(nc, sem, mem_, io):
    x, ident = mem_["xbuf"], mem_["ident"]
    bank = mem_["bank"]
    NT = TT + MT
    with nc.Block() as block:

        @block.sync
        def _(sp):
            for i in range(NT):
                src = io["x"][i * P:(i + 1) * P, :] if i < TT else io["mem"][(i - TT) * P:(i - TT + 1) * P, :]
                sp.dma_start(x[:, i, :], src).then_inc(sem["x_loaded"][i], 16)
            sp.dma_start(mem_["consts"][:], io["consts"]).then_inc(sem["consts_loaded"], 16)
            for n in range(2):
                load_weights(sp, sem, mem_, io, n)

        @block.scalar
        def _(act):
            act.wait_ge(sem["eps_set"], 1)
            for i in range(NT):
                act.wait_ge(sem["x_loaded"][i], 16)
                if i:
                    act.wait_ge(sem["x_squares"], i)
                nc.scalar.activation(mem_["junk"][:], x[:, i, :], ACT.Square,
                                     accum_out=mem_["ss"][:, i:i + 1]).then_inc(sem["x_squares"], 1)
                act.wait_ge(sem["x_squares"], i + 1)
                nc.scalar.activation(mem_["sd"][:, i:i + 1], mem_["ss"][:, i:i + 1], ACT.Sqrt,
                                     scale=1.0 / D, bias=mem_["eps"][:, 0:1]).then_inc(sem["x_roots"], 1)

        @block.vector
        def _(dve):
            nc.vector.memset(mem_["eps"][:], NORM_EPS).then_inc(sem["eps_set"], 1)
            dve.wait_ge(sem["consts_loaded"], 16)

            def evacuate(i):
                g = mem_["mix_g"] if i < TT else mem_["mem_g"]
                dst = mem_["xnT"] if i < TT else mem_["memnT"]
                t0 = (i if i < TT else i - TT) * P
                for h in range(2):
                    n = 2 * i + h
                    dve.wait_ge(sem["xT_ready"], n + 1)
                    gain = g[:, 4 * h:4 * h + 4].unsqueeze(2).to_broadcast([P, 4, P])
                    nc.vector.tensor_tensor(dst[:, 4 * h:4 * h + 4, t0:t0 + P], bank4(bank[n % 2]), gain,
                                            ALU.mult).then_inc(sem["xT_copied"], 1)

            for i in range(NT):
                dve.wait_ge(sem["x_roots"], i + 1)
                nc.vector.reciprocal(mem_["rstd"][:, i:i + 1], mem_["sd"][:, i:i + 1]).then_inc(sem["x_rstd"], 1)
                dve.wait_ge(sem["x_rstd"], i + 1)
                nc.vector.tensor_scalar(x[:, i, :], x[:, i, :], mem_["rstd"][:, i:i + 1], None,
                                        ALU.mult).then_inc(sem["x_normed"], 1)
                if i:
                    evacuate(i - 1)
            evacuate(NT - 1)

        @block.tensor
        def _(pe):
            pe.wait_ge(sem["consts_loaded"], 16)
            for i in range(NT):
                pe.wait_ge(sem["x_normed"], i + 1)
                for h in range(2):
                    n = 2 * i + h
                    if n >= 2:
                        pe.wait_ge(sem["xT_copied"], n - 1)
                    for q in range(4):
                        last = nc.tensor.transpose(bank4(bank[n % 2])[:, q, :],
                                                   x[:, i, (4 * h + q) * P:(4 * h + q + 1) * P], ident)
                    last.then_inc(sem["xT_ready"], 1)


def bank4(bank):
    return bank[:].rearrange("p (a b) -> p a b", a=4)


N_KV, N_MIX, N_GATE, N_WQ = 2, 5, KD, 4
FIRST_GATE = N_KV + N_MIX
FIRST_WQ = FIRST_GATE + N_GATE


def load_weights(sp, sem, mem_, io, n):
    ring = mem_["wring"]
    if n < N_KV:
        src = io["w_kv"][n]
    elif n < FIRST_GATE:
        src = io["w_mix"][n - N_KV]
    elif n < FIRST_WQ:
        src = io["w_gate"][n - FIRST_GATE]
    else:
        src = io["w_q"][n - FIRST_WQ]
    sp.dma_start(ring[:, n % 2, 0:src.shape[1]], src).then_inc(sem["w_loaded"][n % 2], 16)


def weights_arrived(eng, sem, n):
    eng.wait_ge(sem["w_loaded"][n % 2], 16 * (n // 2 + 1))


KV_JOBS = 2 * MT
MIX_JOBS = KV_JOBS + N_MIX * TT
POOL_MIX = MIX_JOBS
TURNS = 2 + 3 * TT
UNITS = NJ * NA_H + TT * XA_H


def stage_attend(nc, sem, mem_, io):
    bank, ident = mem_["bank"], mem_["ident"]
    prod_bank, turn_bank, score_bank, out_bank = bank[0:2], bank[2:4], bank[4:6], bank[6:8]
    ring, xnT, memnT = mem_["wring"], mem_["xnT"], mem_["memnT"]
    nraw, kvmem, vna, vsh = mem_["nraw"], mem_["kvmem"], mem_["vna"], mem_["vsh"]
    qkxT, kmT, yT = mem_["qkxT"], mem_["kmT"], mem_["yT"]
    bias = mem_["bias"]
    ppad, pooled = mem_["ppad"], mem_["pooledT"]

    def is_na(u):
        return u < NJ * NA_H

    with nc.Block() as block:

        @block.sync
        def _(sp):
            sp.dma_start(mem_["gains"][:], io["gains"]).then_inc(sem["gains_loaded"], 16)
            for n in range(2, FIRST_GATE + 2):
                used = n - 2
                sp.wait_ge(sem["prod_ready"], 2 * (used + 1) if used < N_KV else KV_JOBS + TT * (used - N_KV + 1))
                load_weights(sp, sem, mem_, io, n)
                if n == 4:
                    sp.dma_start(bias[:], io["bias"]).then_inc(sem["bias_loaded"], 16)
            sp.wait_ge(sem["prod_copied"], KV_JOBS + 4 * TT)
            sp.dma_start(vsh[0:64, :, :], vna[64:128, 0:3, :]).then_inc(sem["vsh_loaded"], 16)
            sp.dma_start(vsh[64:128, :, :], vna[0:64, 1:4, :]).then_inc(sem["vsh_loaded"], 16)
            sp.wait_ge(sem["turn_ready"], 2 + TT)
            sp.dma_start(mem_["pool_w"][:], io["pool_w"]).then_inc(sem["pool_loaded"], 16)

        @block.tensor
        def _(pe):
            job = 0
            for n in range(FIRST_GATE):
                weights_arrived(pe, sem, n)
                w = ring[:, n % 2, :].rearrange("p (k f) -> p k f", k=KD)
                for i in range(MT if n < N_KV else TT):
                    if job >= 2:
                        pe.wait_ge(sem["prod_copied"], job - 1)
                    for k in range(KD):
                        if n < N_KV:
                            lhsT, rhs = memnT[:, k, i * P:(i + 1) * P], w[:, k, :]
                        elif n < N_KV + 4:
                            lhsT, rhs = xnT[:, k, i * P:(i + 1) * P], w[:, k, :]
                        else:
                            lhsT, rhs = w[:, k, i * P:(i + 1) * P], xnT[:, k, :]
                        last = nc.tensor.matmul(prod_bank[job % 2][:], lhsT, rhs, start=(k == 0), stop=(k == KD - 1))
                    last.then_inc(sem["prod_ready"], 1)
                    job += 1

            for n in range(TURNS):
                stage = 0 if n < 2 else 1 + (n - 2) // TT
                pe.wait_ge(sem["normed"], stage + 1)
                if n >= 2:
                    pe.wait_ge(sem["turn_copied"], n - 1)
                for q in range(4):
                    if n < 2:
                        src = kvmem[:, 0, q % 2, (2 * n + q // 2) * P:(2 * n + q // 2 + 1) * P]
                    else:
                        f = (n - 2) % TT
                        src = nraw[:, stage - 1, q, f * P:(f + 1) * P]
                    last = nc.tensor.transpose(bank4(turn_bank[n % 2])[:, q, :], src, ident)
                last.then_inc(sem["turn_ready"], 1)

            def scores(u):
                if u == 0:
                    pe.wait_ge(sem["turn_copied"], TURNS)
                if u >= 2:
                    pe.wait_ge(sem["logits"], u - 1)
                out = score_bank[u % 2][:, 0:M]
                if is_na(u):
                    j, h = divmod(u, NA_H)
                    rows = slice(64 * (h % 2), 64 * (h % 2) + 64)
                    lhsT = qkxT[rows, 0, h // 2, j * P:(j + 1) * P]
                    rhs = qkxT[rows, 1, h // 2, KEY0[j]:KEY0[j] + M]
                else:
                    i, h = divmod(u - NJ * NA_H, XA_H)
                    lhsT, rhs = qkxT[:, 2, h, i * P:(i + 1) * P], kmT[:, h, :]
                nc.tensor.matmul(out, lhsT, rhs, start=True, stop=True).then_inc(sem["scored"], 1)

            def turn(u):
                pe.wait_ge(sem["probs"], u + 1)
                if u >= 2:
                    pe.wait_ge(sem["probsT_copied"], u - 1)
                for q in range(2):
                    last = nc.tensor.transpose(turn_bank[u % 2][:, q * P:(q + 1) * P],
                                               mem_["prob"][:, u % 3, q * P:(q + 1) * P], ident)
                last.then_inc(sem["probsT"], 1)

            def values(u):
                pe.wait_ge(sem["probsT_copied"], u + 1)
                if u == 0:
                    pe.wait_ge(sem["vsh_loaded"], 32)
                if u >= 2:
                    pe.wait_ge(sem["mixed_copied"], u - 1)
                for q in range(2):
                    if is_na(u):
                        j, h = divmod(u, NA_H)
                        cols = slice(h * NA_D, (h + 1) * NA_D)
                        k0 = KEY0[j] // P + q
                        v = vna[:, k0, cols] if KEY0[j] % P == 0 else vsh[:, k0, cols]
                        out = out_bank[u % 2][64 * (h % 2):64 * (h % 2) + 64, 0:P]
                    else:
                        h = (u - NJ * NA_H) % XA_H
                        v = kvmem[:, 1, q, h * P:(h + 1) * P]
                        out = out_bank[u % 2][:, 0:P]
                    last = nc.tensor.matmul(out, v, mem_["probT"][:, u % 2, q * P:(q + 1) * P],
                                            start=(q == 0), stop=(q == 1))
                last.then_inc(sem["mixed"], 1)

            for s in range(UNITS + 3):
                if s < UNITS:
                    scores(s)
                if 0 <= s - 2 < UNITS:
                    turn(s - 2)
                if 0 <= s - 3 < UNITS:
                    values(s - 3)
            pe.wait_ge(sem["pooled"], 4)
            pe.wait_ge(sem["pool_loaded"], 16)
            for g in range(4):
                pe.wait_ge(sem["prod_copied"], POOL_MIX + g - 1)
                nc.tensor.matmul(prod_bank[g % 2][:], mem_["pool_w"][:, g, :], pooled[:, g, :],
                                 start=True, stop=True).then_inc(sem["prod_ready"], 1)

        @block.scalar
        def _(act):
            def copied(n, out, src, **how):
                act.wait_ge(sem["prod_ready"], n + 1)
                nc.scalar.activation(out, src, ACT.Copy, **how).then_inc(sem["prod_copied"], 1)

            def root(stage, groups, dim):
                act.wait_ge(sem["sums"], stage + 1)
                nc.scalar.activation(mem_["gsd"][:, stage, 0:groups], mem_["gss"][:, stage, 0:groups], ACT.Sqrt,
                                     scale=1.0 / dim, bias=mem_["eps"][:, 0:1]).then_inc(sem["roots"], 1)

            for n in range(KV_JOBS):
                copied(n, kvmem[:, n // MT, n % MT, :], prod_bank[n % 2][:])
            act.wait_ge(sem["pads_cleared"], 1)
            for n in range(KV_JOBS, MIX_JOBS):
                part, i = divmod(n - KV_JOBS, TT)
                if part < 3:
                    copied(n, nraw[:, part, i, :], prod_bank[n % 2][:])
                elif part == 3:
                    copied(n, vna[:, i, :], prod_bank[n % 2][:])
                else:
                    copied(n, ppad[:, i, PAD:PAD + T].rearrange("p (r c) -> p c r", c=GRID_C),
                           prod_bank[n % 2][:].rearrange("p (c r) -> p c r", r=GRID_R))
                if i == TT - 1 and part < 4:
                    root(*[(0, XA_H * MT, XA_D), (1, NA_H * TT, NA_D), (2, NA_H * TT, NA_D), (3, XA_H * TT, XA_D)][part])
            for s in range(UNITS + 2):
                if s < UNITS:
                    act.wait_ge(sem["maxima"], s + 1)
                    if s >= 3:
                        act.wait_ge(sem["probsT"], s - 2)
                    nc.scalar.activation(mem_["prob"][:, s % 3, :], mem_["logit"][:, s % 2, :], ACT.Exp,
                                         bias=mem_["nmax"][:, s:s + 1], scale=1.0,
                                         accum_out=mem_["total"][:, s:s + 1]).then_inc(sem["exps"], 1)
                u = s - 2
                if 0 <= u < UNITS:
                    act.wait_ge(sem["probsT"], u + 1)
                    if u >= 2:
                        act.wait_ge(sem["mixed"], u - 1)
                    nc.scalar.activation(mem_["probT"][:, u % 2, :], turn_bank[u % 2][:, 0:M],
                                         ACT.Copy).then_inc(sem["probsT_copied"], 1)
            for g in range(4):
                act.wait_ge(sem["prod_ready"], POOL_MIX + g + 1)
                nc.scalar.activation(yT[:, 1, g, :], prod_bank[g % 2][:], ACT.Copy,
                                     scale=mem_["pool_scale"][:, g:g + 1]).then_inc(sem["prod_copied"], 1)

        @block.gpsimd
        def _(pool):
            nc.gpsimd.memset(ppad[:], 0.0).then_inc(sem["pads_cleared"], 1)
            rows = mem_["wsum"]
            step = 0
            for g in range(4):
                pool.wait_ge(sem["prod_copied"], KV_JOBS + 4 * TT + g + 1)
                src = ppad[:, g, :]
                lo, hi = 0, T + 2 * PAD
                half = 1
                for level in range(g + 1):
                    shift_lo, shift_hi = (1, 0) if level == 0 else (half // 2, half // 2)
                    lo, hi = lo + shift_lo, hi - shift_hi
                    dst = rows[:, level % 2, :]
                    nc.gpsimd.tensor_tensor(dst[:, lo:hi], src[:, lo - shift_lo:hi - shift_lo],
                                            src[:, lo + shift_hi:hi + shift_hi], ALU.add).then_inc(sem["pool_step"], 1)
                    step += 1
                    pool.wait_ge(sem["pool_step"], step)
                    src = dst
                    half *= 2
                w = POOL[g]
                mean = rows[:, g % 2, PAD:PAD + T]
                nc.gpsimd.tensor_scalar(mean, mean, 1.0 / w, None, ALU.mult).then_inc(sem["pool_step"], 1)
                step += 1
                pool.wait_ge(sem["pool_step"], step)
                for e, cols in ((0, slice(0, PAD)), (1, slice(T - PAD, T))):
                    nc.gpsimd.tensor_tensor(mean[:, cols], mean[:, cols], mem_["edge"][:, g, e, :],
                                            ALU.mult).then_inc(sem["pool_step"], 1)
                    step += 1
                pool.wait_ge(sem["pool_step"], step)
                nc.gpsimd.tensor_tensor(pooled[:, g, :].rearrange("p (c r) -> p c r", r=GRID_R),
                                        mean.rearrange("p (r c) -> p c r", c=GRID_C),
                                        ppad[:, g, PAD:PAD + T].rearrange("p (r c) -> p c r", c=GRID_C),
                                        ALU.subtract).then_inc(sem["pooled"], 1)
                pool.wait_ge(sem["pooled"], g + 1)

        @block.vector
        def _(dve):
            tmp = mem_["tmp"]
            stages = [
                (kvmem[:, 0], MT, XA_H, XA_D, MT, 256),
                (nraw[:, 0], TT, NA_H, NA_D, KV_JOBS + TT, 0),
                (nraw[:, 1], TT, NA_H, NA_D, KV_JOBS + 2 * TT, 64),
                (nraw[:, 2], TT, XA_H, XA_D, KV_JOBS + 3 * TT, 128),
            ]

            def sums(s):
                t, tiles, heads, dim, need, _ = stages[s]
                n = tiles * heads
                dve.wait_ge(sem["prod_copied"], need)
                flat = t.rearrange("p a b -> p (a b)")
                nc.vector.tensor_tensor(tmp[:, 0:n * dim], flat, flat, ALU.mult).then_inc(sem["squares"], 1)
                dve.wait_ge(sem["squares"], s + 1)
                nc.vector.tensor_reduce(mem_["gss"][:, s, 0:n], tmp[:, 0:n * dim].rearrange("p (g d) -> p g d", d=dim),
                                        AX_X, ALU.add).then_inc(sem["sums"], 1)
                dve.wait_ge(sem["sums"], s + 1)

            def norm(s):
                t, tiles, heads, dim, _, g0 = stages[s]
                n = tiles * heads
                dve.wait_ge(sem["roots"], s + 1)
                nc.vector.reciprocal(mem_["grstd"][:, s, 0:n], mem_["gsd"][:, s, 0:n]).then_inc(sem["grstds"], 1)
                dve.wait_ge(sem["grstds"], s + 1)
                v = t.rearrange("p a (h d) -> p (a h) d", d=dim)
                nc.vector.tensor_tensor(v, v, mem_["grstd"][:, s, 0:n].unsqueeze(2).to_broadcast([P, n, dim]),
                                        ALU.mult).then_inc(sem["scaled"], 1)
                dve.wait_ge(sem["scaled"], s + 1)
                nc.vector.tensor_tensor(v, v, mem_["gains"][:, g0:g0 + dim].unsqueeze(1).to_broadcast([P, n, dim]),
                                        ALU.mult).then_inc(sem["normed"], 1)

            dve.wait_ge(sem["gains_loaded"], 16)
            sums(0)
            sums(1)
            norm(0)
            sums(2)
            norm(1)
            sums(3)
            norm(2)
            norm(3)
            dve.wait_ge(sem["bias_loaded"], 16)
            for v in range(3):
                for h in range(NA_H):
                    table = bias[:, v, h, :].rearrange("p (c r) -> p c r", r=GRID_R)
                    last = nc.vector.tensor_tensor(table, table, mem_["mask"][:, v, :].unsqueeze(2)
                                                   .to_broadcast([P, KCOLS, GRID_R]), ALU.add)
                last.then_inc(sem["masked"], 1)
            dve.wait_ge(sem["masked"], 3)
            for n in range(TURNS):
                dve.wait_ge(sem["turn_ready"], n + 1)
                if n < 2:
                    dst = kmT[:, 2 * n:2 * n + 2, :].rearrange("p a b -> p (a b)")
                else:
                    dst = qkxT[:, (n - 2) // TT, (n - 2) % TT, :]
                nc.vector.tensor_copy(dst, turn_bank[n % 2][:]).then_inc(sem["turn_copied"], 1)

            def logits(u):
                dve.wait_ge(sem["scored"], u + 1)
                if u >= 2:
                    dve.wait_ge(sem["exps"], u - 1)
                out, src = mem_["logit"][:, u % 2, :], score_bank[u % 2][:, 0:M]
                if is_na(u):
                    j, h = divmod(u, NA_H)
                    nc.vector.scalar_tensor_tensor(out, src, NA_D ** -0.5, bias[:, VARIANT[j], h, :],
                                                   ALU.mult, ALU.add).then_inc(sem["logits"], 1)
                else:
                    nc.vector.tensor_scalar(out, src, XA_D ** -0.5, None, ALU.mult).then_inc(sem["logits"], 1)
                dve.wait_ge(sem["logits"], u + 1)
                nc.vector.tensor_reduce(mem_["nmax"][:, u:u + 1], out, AX_X, ALU.max,
                                        negate=True).then_inc(sem["maxima"], 1)

            def normalise(u):
                dve.wait_ge(sem["exps"], u + 1)
                nc.vector.reciprocal(mem_["inv"][:, u:u + 1], mem_["total"][:, u:u + 1]).then_inc(sem["invs"], 1)
                dve.wait_ge(sem["invs"], u + 1)
                p = mem_["prob"][:, u % 3, :]
                nc.vector.tensor_scalar(p, p, mem_["inv"][:, u:u + 1], None, ALU.mult).then_inc(sem["probs"], 1)

            def mixed(u):
                dve.wait_ge(sem["mixed"], u + 1)
                if is_na(u):
                    j, h = divmod(u, NA_H)
                    rows = slice(64 * (h % 2), 64 * (h % 2) + 64)
                    dst, src = yT[rows, 0, h // 2, j * P:(j + 1) * P], out_bank[u % 2][rows, 0:P]
                else:
                    i, h = divmod(u - NJ * NA_H, XA_H)
                    dst, src = yT[:, 2, h, i * P:(i + 1) * P], out_bank[u % 2][:, 0:P]
                nc.vector.tensor_copy(dst, src).then_inc(sem["mixed_copied"], 1)

            for s in range(UNITS + 4):
                if s < UNITS:
                    logits(s)
                if 0 <= s - 1 < UNITS:
                    normalise(s - 1)
                if 0 <= s - 4 < UNITS:
                    mixed(s - 4)


def stage_merge(nc, sem, mem_, io):
    bank = mem_["bank"]
    gate_bank, branch_bank, out_bank = bank[0:2], bank[2:4], bank[4:8]
    ring, xnT, yT = mem_["wring"], mem_["xnT"], mem_["yT"]
    wbr, wout, gate, merged, h = mem_["wbr"], mem_["wout"], mem_["gate"], mem_["merged"], mem_["h"]
    JOBS = 3 * KD
    with nc.Block() as block:

        @block.sync
        def _(sp):
            for b in range(3):
                sp.dma_start(wbr[:, b], io["w_branch"][b]).then_inc(sem["wbr_loaded"][b], 16)
            for cc in range(2, N_GATE):
                sp.wait_ge(sem["gates_ready"], 3 * (cc - 1))
                load_weights(sp, sem, mem_, io, FIRST_GATE + cc)
                if cc == 2:
                    sp.dma_start(wout[:], io["w_out"]).then_inc(sem["wout_loaded"], 16)
                    for i in range(TT):
                        sp.dma_start(h[:, i, :], io["x"][i * P:(i + 1) * P, :]).then_inc(sem["h_loaded"], 16)
            for n in range(2):
                sp.wait_ge(sem["gates_ready"], 3 * (N_GATE - 1 + n))
                load_weights(sp, sem, mem_, io, FIRST_WQ + n)

        @block.tensor
        def _(pe):
            for cc in range(KD):
                n = FIRST_GATE + cc
                weights_arrived(pe, sem, n)
                w = ring[:, n % 2, 0:KD * 3 * P].rearrange("p (k f) -> p k f", k=KD)
                for b in range(3):
                    job = 3 * cc + b
                    if job >= 2:
                        pe.wait_ge(sem["gates"], job - 1)
                    for k in range(KD):
                        last = nc.tensor.matmul(gate_bank[job % 2][:], w[:, k, b * P:(b + 1) * P], xnT[:, k, :],
                                                start=(k == 0), stop=(k == KD - 1))
                    last.then_inc(sem["gates_ready"], 1)
                for b in range(3):
                    job = 3 * cc + b
                    if cc == 0:
                        pe.wait_ge(sem["wbr_loaded"][b], 16)
                    if job >= 2:
                        pe.wait_ge(sem["gated"], job - 1)
                    for k in range(KW):
                        last = nc.tensor.matmul(branch_bank[job % 2][:], wbr[:, b, k, cc * P:(cc + 1) * P],
                                                yT[:, b, k, :], start=(k == 0), stop=(k == KW - 1))
                    last.then_inc(sem["branches_ready"], 1)
            pe.wait_ge(sem["wout_loaded"], 16)
            pe.wait_ge(sem["merged"], 2 * KD)
            for n in range(2 * TT):
                i, half = divmod(n, 2)
                if n >= 4:
                    pe.wait_ge(sem["h_added"], n - 3)
                for k in range(KD):
                    last = nc.tensor.matmul(out_bank[n % 4][:], merged[:, k, i * P:(i + 1) * P],
                                            wout[:, k, half * HALF:(half + 1) * HALF],
                                            start=(k == 0), stop=(k == KD - 1))
                last.then_inc(sem["out_ready"], 1)

        @block.scalar
        def _(act):
            for job in range(JOBS):
                cc, b = divmod(job, 3)
                act.wait_ge(sem["gates_ready"], job + 1)
                if job >= 4:
                    act.wait_ge(sem["gated"], job - 3)
                nc.scalar.activation(gate[:, job % 4, :], gate_bank[job % 2][:], ACT.Sigmoid,
                                     bias=mem_["gate_b"][:, b * KD + cc:b * KD + cc + 1],
                                     scale=1.0).then_inc(sem["gates"], 1)

        @block.vector
        def _(dve):
            tmp = mem_["gtmp"]
            for job in range(JOBS):
                cc, b = divmod(job, 3)
                dve.wait_ge(sem["gates"], job + 1)
                dve.wait_ge(sem["branches_ready"], job + 1)
                dst = merged[:, cc, :] if b == 0 else tmp[:, b - 1, :]
                if b and cc:
                    dve.wait_ge(sem["merged"], 2 * (cc - 1) + b)
                nc.vector.tensor_tensor(dst, branch_bank[job % 2][:], gate[:, job % 4, :],
                                        ALU.mult).then_inc(sem["gated"], 1)
                dve.wait_ge(sem["gated"], job + 1)
                if b:
                    if b == 2:
                        dve.wait_ge(sem["merged"], 2 * cc + 1)
                    nc.vector.tensor_tensor(merged[:, cc, :], merged[:, cc, :], dst,
                                            ALU.add).then_inc(sem["merged"], 1)
            dve.wait_ge(sem["h_loaded"], 16 * TT)
            for n in range(2 * TT):
                i, half = divmod(n, 2)
                dve.wait_ge(sem["out_ready"], n + 1)
                part = h[:, i, half * HALF:(half + 1) * HALF]
                nc.vector.tensor_tensor(part, part, out_bank[n % 4][:], ALU.add).then_inc(sem["h_added"], 1)


def stage_query(nc, sem, mem_, io):
    bank, ident = mem_["bank"], mem_["ident"]
    prod_bank, turn_bank = bank[0:4], bank[4:6]
    h, ring = mem_["h"], mem_["wring"]
    hn32, hnr, hnl, qpT = mem_["hn32"], mem_["hnr"], mem_["hnl"], mem_["qpT"]
    with nc.Block() as block:

        @block.sync
        def _(sp):
            sp.dma_start(mem_["keysT"][:], io["keysT"]).then_inc(sem["keys_loaded"], 16)
            for n in range(2, N_WQ):
                sp.wait_ge(sem["query_ready"], 4 * (n - 1))
                load_weights(sp, sem, mem_, io, FIRST_WQ + n)
            sp.wait_ge(sem["query_ready"], 4 * (N_WQ - 1))
            for s in range(2):
                load_u(sp, mem_, sem, io, s, s)

        @block.scalar
        def _(act):
            for i in range(TT):
                if i:
                    act.wait_ge(sem["h_squares"], i)
                nc.scalar.activation(mem_["junk2"][:], h[:, i, :], ACT.Square,
                                     accum_out=mem_["ss"][:, i:i + 1]).then_inc(sem["h_squares"], 1)
                act.wait_ge(sem["h_squares"], i + 1)
                nc.scalar.activation(mem_["sd"][:, i:i + 1], mem_["ss"][:, i:i + 1], ACT.Sqrt,
                                     scale=1.0 / D, bias=mem_["eps"][:, 0:1]).then_inc(sem["h_roots"], 1)
            for n in range(HP):
                act.wait_ge(sem["query_ready"], n + 1)
                nc.scalar.activation(qpT[:, n, :], prod_bank[n % 4][:], ACT.Copy).then_inc(sem["query_copied"], 1)

        @block.vector
        def _(dve):
            def split(i):
                for half in range(2):
                    n = 2 * i + half
                    dve.wait_ge(sem["hT_ready"], n + 1)
                    where = (slice(None), slice(4 * half, 4 * half + 4), slice(i * P, (i + 1) * P))
                    gain = mem_["ffn_g"][:, 4 * half:4 * half + 4].unsqueeze(2).to_broadcast([P, 4, P])
                    nc.vector.tensor_tensor(hn32[where], bank4(turn_bank[n % 2]), gain,
                                            ALU.mult).then_inc(sem["hT_copied"], 1)
                    dve.wait_ge(sem["hT_copied"], n + 1)
                    nc.vector.tensor_copy(hnr[where], hn32[where]).then_inc(sem["hT_rounded"], 1)
                    dve.wait_ge(sem["hT_rounded"], n + 1)
                    nc.vector.tensor_tensor(hnl[where], hn32[where], hnr[where].bitcast(F32),
                                            ALU.subtract).then_inc(sem["hT_rest"], 1)

            for i in range(TT):
                dve.wait_ge(sem["h_roots"], i + 1)
                nc.vector.reciprocal(mem_["rstd"][:, i:i + 1], mem_["sd"][:, i:i + 1]).then_inc(sem["h_rstd"], 1)
                dve.wait_ge(sem["h_rstd"], i + 1)
                if i >= 2:
                    dve.wait_ge(sem["hT_ready"], 2 * (i - 1))
                nc.vector.tensor_scalar(mem_["hn"][:, i % 2, :], h[:, i, :], mem_["rstd"][:, i:i + 1], None,
                                        ALU.mult).then_inc(sem["h_normed"], 1)
                if i:
                    split(i - 1)
            split(TT - 1)

        @block.tensor
        def _(pe):
            for i in range(TT):
                pe.wait_ge(sem["h_normed"], i + 1)
                for half in range(2):
                    n = 2 * i + half
                    if n >= 2:
                        pe.wait_ge(sem["hT_copied"], n - 1)
                    for q in range(4):
                        k = 4 * half + q
                        last = nc.tensor.transpose(bank4(turn_bank[n % 2])[:, q, :],
                                                   mem_["hn"][:, i % 2, k * P:(k + 1) * P], ident)
                    last.then_inc(sem["hT_ready"], 1)
            pe.wait_ge(sem["hT_copied"], 2 * TT)
            for n in range(HP):
                load = FIRST_WQ + n // 4
                if n % 4 == 0:
                    weights_arrived(pe, sem, load)
                w = ring[:, load % 2, :].rearrange("p (k f) -> p k f", k=KD)
                if n >= 4:
                    pe.wait_ge(sem["query_copied"], n - 3)
                for k in range(KD):
                    last = nc.tensor.matmul(prod_bank[n % 4][:], w[:, k, (n % 4) * P:(n % 4 + 1) * P], hn32[:, k, :],
                                            start=(k == 0), stop=(k == KD - 1))
                last.then_inc(sem["query_ready"], 1)


SELECT_PRE = 12
TABLE_PRE = 4
PRE = SELECT_PRE * TT + TABLE_PRE * (NTB // 2)
LIVE = CHUNKS - PRE
LIVE_GROUPS = LIVE // GC



def hidden_products(pe, mem_, sem, s, c, part=0, parts=1):
    if part == 0:
        pe.wait_ge(sem["u_rest"], c + 1)
        pe.wait_ge(sem["gelus"], c + 1)
    ur, ul, hnr, hnl = mem_["ur"], mem_["ul"], mem_["hnr"], mem_["hnl"]
    out = mem_["bank"][s][:]
    for d in range(part * KD // parts, (part + 1) * KD // parts):
        cols = slice(d * P, (d + 1) * P)
        pe.matmul(out, ur[:, s, cols], hnr[:, d, :], start=(d == 0), stop=False)
        pe.matmul(out, ur[:, s, cols], hnl[:, d, :], start=False, stop=False)
        last = pe.matmul(out, ul[:, s, cols], hnr[:, d, :], start=False, stop=(d == KD - 1))
    if part == parts - 1:
        last.then_inc(sem["hidden"], 1)


def round_u(act, mem_, sem, s, c, loads):
    held(act, (sem["u_loaded"][s], 16 * loads), (sem["hidden"], c + 1))
    act.activation(mem_["ur"][:, s, :], mem_["uraw"][:, s, :], ACT.Copy).then_inc(sem["u_rounded"], 1)


def rest_of_u(pool, mem_, sem, s, c):
    pool.wait_ge(sem["u_rounded"], c + 1)
    pool.wait_ge(sem["hidden"], c + 1)
    pool.tensor_tensor(mem_["ul"][:, s, :], mem_["uraw"][:, s, :], mem_["ur"][:, s, :].bitcast(F32),
                       ALU.subtract).then_inc(sem["u_rest"], 1)


def load_u(sp, mem_, sem, io, s, c):
    sp.dma_start(mem_["uraw"][:, s, :], io["u"][bass.ds(c, 1)].rearrange("a p n -> p (a n)")
                 ).then_inc(sem["u_loaded"][s], 16)


def early_gelu(act, mem_, sem, s, c, half):
    held(act, (sem["hidden"], c + 3), (sem["hid_stored"][s], 16 * half + 16))
    act.activation(mem_["act"][:, s, :], mem_["bank"][s][:], ACT.Gelu).then_inc(sem["gelus"], 1)


def store_and_load(sp, mem_, sem, io, s, c):
    sp.wait_ge(sem["u_rest"], c + 1)
    load_u(sp, mem_, sem, io, s, c + 2)
    sp.wait_ge(sem["gelus"], c + 3)
    sp.dma_start(io["hid"][bass.ds(c, 1)].rearrange("a p n -> p (a n)"), mem_["act"][:, s, :]
                 ).then_inc(sem["hid_stored"][s], 16)


def stage_select(nc, sem, mem_, io):
    bank, ident = mem_["bank"], mem_["ident"]
    qpT, keysT, selT = mem_["qpT"], mem_["keysT"], mem_["selT"]
    score_bank, turn_bank = bank[2:6], bank[6]
    scores, score, rest = mem_["scores"], mem_["score"], mem_["score_rest"]
    best, where, bestf = mem_["best"], mem_["where"], mem_["wheref"]
    cand, crest = mem_["cand"], mem_["cand_rest"]
    top, pos = mem_["top"], mem_["pos"]
    part, partf, pick = mem_["part"], mem_["partf"], mem_["pick"]
    low = -3.0e38

    with nc.Block() as block:

        @block.sync
        def _(sp):
            for s in range(2):
                sp.sem_inc(sem["hid_stored"][s], 16)
            with sp.Fori(0, TT) as i:
                for k in range(SELECT_PRE):
                    store_and_load(sp, mem_, sem, io, k % 2, SELECT_PRE * i + k)

        @block.gpsimd
        def _(pool):
            rest_of_u(pool, mem_, sem, 0, 0)
            with pool.Fori(0, TT) as i:
                for k in range(SELECT_PRE):
                    rest_of_u(pool, mem_, sem, (k + 1) % 2, SELECT_PRE * i + (k + 1))

        @block.tensor
        def _(pe):
            pe.sem_inc(sem["hidden"], 2)
            pe.wait_ge(sem["keys_loaded"], 16)
            for n in range(4 * TT):
                i, b = divmod(n, 4)
                if n >= 4:
                    pe.wait_ge(sem["scores_copied"], n - 3)
                for q in range(4):
                    f = 4 * b + q
                    last = nc.tensor.matmul(bank4(score_bank[n % 4])[:, q, :], qpT[:, f, i * P:(i + 1) * P],
                                            keysT[:, f, :], start=True, stop=True)
                last.then_inc(sem["scores_ready"], 1)
            with pe.Fori(0, TT) as i:
                for k in range(SELECT_PRE):
                    hidden_products(pe, mem_, sem, k % 2, SELECT_PRE * i + k)
                pe.wait_ge(sem["picked"], 3 * i + 3)
                pe.wait_ge(sem["turn_room"], i + 1)
                for n in range(3):
                    last = nc.tensor.transpose(bank4(turn_bank)[:, n, :], pick[:, n, :], ident)
                last.then_inc(sem["picks_turned"], 1)

        @block.scalar
        def _(act):
            act.sem_inc(sem["gelus"], 2)
            act.sem_inc(sem["turn_room"], 1)
            round_u(act, mem_, sem, 0, 0, 1)
            for n in range(4 * TT):
                act.wait_ge(sem["scores_ready"], n + 1)
                nc.scalar.activation(scores[:, n // 4, 4 * (n % 4):4 * (n % 4) + 4, :], bank4(score_bank[n % 4]),
                                     ACT.Copy).then_inc(sem["scores_copied"], 1)
            with act.Fori(0, TT) as i:
                held(act, (sem["scores_used"], i + 1), (sem["scores_copied"], 4 * TT))
                nc.scalar.activation(score[:], scores[:, bass.ds(i, 1)].rearrange("p a f n -> p (a f) n"),
                                     ACT.Copy).then_inc(sem["score_ready"], 1)
                for k in range(SELECT_PRE):
                    c = SELECT_PRE * i + k
                    round_u(act, mem_, sem, (k + 1) % 2, c + 1, (SELECT_PRE // 2) * i + ((k + 1) // 2 + 1))
                    early_gelu(act, mem_, sem, k % 2, c, (SELECT_PRE // 2) * i + k // 2)
                    if k == EXP_AFTER:
                        held(act, (sem["top_ready"], i + 1))
                        nc.scalar.activation(mem_["expo"][:], mem_["shifted"][:], ACT.Exp).then_inc(sem["expo_ready"], 1)
                held(act, (sem["picks_turned"], i + 1))
                nc.scalar.activation(selT[:, :, bass.ds(i * P, P)], bank4(turn_bank)[:, 0:3, :],
                                     ACT.Copy).then_inc(sem["turn_room"], 1)

        @block.vector
        def _(dve):
            count = [0]
            PER_TILE = 18

            def done(ins):
                ins.then_inc(sem["select_step"], 1)
                count[0] += 1
                held(dve, (sem["select_step"], tile * PER_TILE + count[0]))

            dve.sem_inc(sem["scores_used"], 1)
            with dve.Fori(0, TT) as tile:
                held(dve, (sem["score_ready"], tile + 1))
                for f in range(HP):
                    ins = nc.vector.max(best[:, f, 0:8], score[:, f, :])
                done(ins)
                for f in range(HP):
                    nc.vector.max_index(where[:, f, 0:8], best[:, f, 0:8], score[:, f, :])
                for f in range(HP):
                    ins = nc.vector.match_replace(rest[:, f, :], best[:, f, 0:8], score[:, f, :], low)
                done(ins)
                dve.sem_inc(sem["scores_used"], 1)
                for f in range(HP):
                    ins = nc.vector.max(best[:, f, 8:16], rest[:, f, :])
                done(ins)
                for f in range(HP):
                    ins = nc.vector.max_index(where[:, f, 8:16], best[:, f, 8:16], rest[:, f, :])
                done(ins)
                done(nc.vector.tensor_copy(bestf[:], where[:]))
                pair = best[:].rearrange("p (h two) k -> p h two k", two=2)
                a = pair[:, :, 0, :].unsqueeze(3).to_broadcast([P, HEADS, TOPK, TOPK])
                b = pair[:, :, 1, :].unsqueeze(2).to_broadcast([P, HEADS, TOPK, TOPK])
                done(nc.vector.tensor_tensor(cand[:].rearrange("p h (a b) -> p h a b", a=TOPK), a, b, ALU.add))
                for h in range(HEADS):
                    ins = nc.vector.max(top[:, h, 0:8], cand[:, h, :])
                done(ins)
                for h in range(HEADS):
                    nc.vector.max_index(pos[:, h, 0:8], top[:, h, 0:8], cand[:, h, :])
                for h in range(HEADS):
                    ins = nc.vector.match_replace(crest[:, h, :], top[:, h, 0:8], cand[:, h, :], low)
                done(ins)
                for h in range(HEADS):
                    ins = nc.vector.max(top[:, h, 8:16], crest[:, h, :])
                done(ins)
                for h in range(HEADS):
                    ins = nc.vector.max_index(pos[:, h, 8:16], top[:, h, 8:16], crest[:, h, :])
                done(ins)
                nc.vector.tensor_tensor(mem_["shifted"][:], top[:], top[:, :, 0:1].to_broadcast([P, HEADS, TOPK]),
                                        ALU.subtract).then_inc(sem["top_ready"], 1)
                nc.vector.tensor_scalar(part[:, 0], pos[:], 4, None, ALU.logical_shift_right)
                done(nc.vector.tensor_scalar(part[:, 1], pos[:], 15, None, ALU.bitwise_and))
                done(nc.vector.tensor_copy(partf[:], part[:]))
                pairf = bestf[:].rearrange("p (h two) k -> p h two k", two=2)
                full = [P, HEADS, TOPK, TOPK]
                eq = mem_["eq"][:].rearrange("p (h k a) -> p h k a", h=HEADS, k=TOPK)
                for n in range(2):
                    if n == 0:
                        held(dve, (sem["turn_room"], tile + 1))
                    done(nc.vector.tensor_tensor(eq, partf[:, n].unsqueeze(3).to_broadcast(full),
                                                 mem_["iota"][:, 0:TOPK].unsqueeze(1).unsqueeze(1).to_broadcast(full),
                                                 ALU.is_equal))
                    done(nc.vector.tensor_tensor(eq, eq, pairf[:, :, n, :].unsqueeze(2).to_broadcast(full), ALU.mult))
                    nc.vector.tensor_reduce(pick[:, n, :].rearrange("p (h k) -> p h k", h=HEADS), eq, AX_X,
                                            ALU.add).then_inc(sem["picked"], 1)
                    held(dve, (sem["picked"], 3 * tile + n + 1))
                held(dve, (sem["expo_ready"], tile + 1))
                done(nc.vector.tensor_reduce(mem_["esum"][:], mem_["expo"][:], AX_X, ALU.add))
                done(nc.vector.reciprocal(mem_["einv"][:], mem_["esum"][:]))
                nc.vector.tensor_tensor(pick[:, 2, :].rearrange("p (h k) -> p h k", h=HEADS), mem_["expo"][:],
                                        mem_["einv"][:].unsqueeze(2).to_broadcast([P, HEADS, TOPK]),
                                        ALU.mult).then_inc(sem["picked"], 1)
            assert count[0] == PER_TILE


def stage_table(nc, sem, mem_, io):
    bank = mem_["bank"]
    table_bank = bank[2:6]
    selT, one, two, block_ = mem_["selT"], mem_["onehot1"], mem_["onehot2"], mem_["table"]
    STEP = 4
    PER = 2 * TB // STEP
    SPREAD = PER // TABLE_PRE
    FIRST = SELECT_PRE * TT

    def chunk(it, k):
        return TABLE_PRE * it + (FIRST + k), (TABLE_PRE // 2) * it + (FIRST // 2 + k // 2)

    with nc.Block() as block:

        @block.vector
        def _(dve):
            dve.sem_inc(sem["onehot_room"], 2)
            with dve.Fori(0, NTB // 2) as it:
                for s in range(PER):
                    dve.wait_ge(sem["onehot_room"], PER * it + s + 1)
                    for q in range(STEP):
                        t = bass.ds(it * (2 * TB) + (s * STEP + q), 1)
                        slot = (s * STEP + q) % (2 * STEP)
                        nc.vector.tensor_scalar(one[:, slot, :], mem_["iota"], selT[:, 0, t], None, ALU.is_equal)
                        last = nc.vector.tensor_scalar(two[:, slot, :], mem_["iota"], selT[:, 1, t], selT[:, 2, t],
                                                       ALU.is_equal, ALU.mult)
                    last.then_inc(sem["onehots"], 1)

        @block.gpsimd
        def _(pool):
            with pool.Fori(0, NTB // 2) as it:
                for k in range(TABLE_PRE):
                    rest_of_u(pool, mem_, sem, (k + 1) % 2, chunk(it, k)[0] + 1)

        @block.tensor
        def _(pe):
            with pe.Fori(0, NTB // 2) as it:
                for s in range(PER):
                    k = s // SPREAD
                    hidden_products(pe, mem_, sem, k % 2, chunk(it, k)[0], s % SPREAD, SPREAD)
                    pe.wait_ge(sem["onehots"], PER * it + s + 1)
                    pe.wait_ge(sem["table_room"], PER * it + s + 1)
                    for q in range(STEP):
                        slot = (s * STEP + q) % (2 * STEP)
                        last = nc.tensor.matmul(bank4(table_bank[s % 4])[:, q, :], one[:, slot, :], two[:, slot, :],
                                                start=True, stop=True)
                    last.then_inc(sem["onehot_room"], 1)

        @block.scalar
        def _(act):
            act.sem_inc(sem["table_room"], 4)
            with act.Fori(0, NTB // 2) as it:
                for s in range(PER):
                    k = s // SPREAD
                    c, half = chunk(it, k)
                    if s % SPREAD == 0:
                        k1 = k + 1
                        round_u(act, mem_, sem, k1 % 2, c + 1, (TABLE_PRE // 2) * it + (FIRST // 2 + k1 // 2 + 1))
                    if s % SPREAD == SPREAD - 1:
                        early_gelu(act, mem_, sem, k % 2, c, half)
                    waits = [(sem["onehot_room"], PER * it + s + 3)]
                    if s % (PER // 2) == 0:
                        waits.append((sem["table_stored"][2 * s // PER], 16 * it + 16))
                    held(act, *waits)
                    b, t0 = divmod(s * STEP, TB)
                    nc.scalar.activation(block_[:, b, :, t0:t0 + STEP],
                                         bank4(table_bank[s % 4]).rearrange("p t i -> p i t"),
                                         ACT.Copy).then_inc(sem["table_room"], 1)

        @block.sync
        def _(sp):
            for b in range(2):
                sp.sem_inc(sem["table_stored"][b], 16)
            with sp.Fori(0, NTB // 2) as it:
                for b in range(2):
                    for k in range(b * TABLE_PRE // 2, (b + 1) * TABLE_PRE // 2):
                        store_and_load(sp, mem_, sem, io, k % 2, chunk(it, k)[0])
                    sp.wait_ge(sem["table_room"], PER * it + (PER // 2) * (b + 1) + 4)
                    sp.dma_start(io["table"][:, bass.ds(2 * it + b, 1), :],
                                 block_[:, b].rearrange("p i t -> p (i t)").unsqueeze(1)
                                 ).then_inc(sem["table_stored"][b], 16)
            for b in range(2):
                sp.wait_ge(sem["table_stored"][b], 16 * (NTB // 2) + 16)
                sp.wait_ge(sem["hid_stored"][b], 16 * (PRE // 2) + 16)


def stage_experts(nc, sem, mem_, io):
    bank = mem_["bank"]
    hid_bank, sum_bank = bank[0:2], bank[2:6]
    h = mem_["h"]
    vraw, vr, vl = (mem_[n] for n in ("vraw", "vr", "vl"))
    wr, wl, act_, w32, tab = (mem_[n] for n in ("wr", "wl", "act", "w32", "tab"))
    TILES = 2 * TT

    def groups(eng, body):
        for k in range(GC):
            body(0, 0, k, True, "first")
        with eng.Fori(0, (LIVE_GROUPS - 2) // 2) as it:
            for gg in range(2):
                for k in range(GC):
                    body(2 * it + (1 + gg), (1 + gg) % 2, k, True, None)
        for k in range(GC):
            body(LIVE_GROUPS - 1, (LIVE_GROUPS - 1) % 2, k, True, "last live")
        with eng.Fori(0, (GROUPS - LIVE_GROUPS) // 2) as it:
            for gg in range(2):
                for k in range(GC):
                    body(2 * it + (LIVE_GROUPS + gg), gg, k, False, None)

    assert LIVE_GROUPS % 2 == 0 and (GROUPS - LIVE_GROUPS) % 2 == 0

    def place(g, live):
        return g + PRE // GC if live else g - LIVE_GROUPS

    with nc.Block() as block:

        @block.sync
        def _(sp):
            def load(g, par, k, live, edge):
                s, n = k % 2, GC * g + k
                c = GC * place(g, live) + k
                if live and not (edge == "last live" and k >= 2):
                    sp.wait_ge(sem["u_rest"], c + 1)
                    load_u(sp, mem_, sem, io, s, c + 2)
                if not (edge == "first" and k < 2):
                    sp.wait_ge(sem["v_rest"], n - 1)
                sp.dma_start(vraw[:, s, :], io["v"][bass.ds(c, 1)].rearrange("a p n -> p (a n)")
                             ).then_inc(sem["v_loaded"][s], 16)
                if k == 0:
                    if edge != "first":
                        sp.wait_ge(sem["weighted"], GC * g)
                    sp.dma_start(tab[:, par], io["table"][:, :, bass.ds(place(g, live) * (GC * TB), GC * TB)]
                                 ).then_inc(sem["tab_loaded"][par], 16)
                if not live:
                    sp.wait_ge(sem["weighted"], n + (GC - 1))
                    sp.dma_start(act_[:, s, :], io["hid"][bass.ds(c, 1)].rearrange("a p n -> p (a n)")
                                 ).then_inc(sem["hid_loaded"][s], 16)

            groups(sp, load)
            for i in range(TT):
                sp.wait_ge(sem["sum_room"], 4 + TILES * (GROUPS - 1) + 2 * (i + 1))
                sp.dma_start(io["out"][i * P:(i + 1) * P, :], h[:, i, :]).then_inc(sem["stored"], 16)
            sp.wait_ge(sem["stored"], 16 * TT)

        @block.gpsimd
        def _(pool):
            def rest(g, par, k, live, edge):
                if live and not (edge == "last live" and k == GC - 1):
                    rest_of_u(pool, mem_, sem, (k + 1) % 2, GC * place(g, live) + (k + 1))

            for k in range(GC):
                rest(0, 0, k, True, "first")
            with pool.Fori(0, (LIVE_GROUPS - 2) // 2) as it:
                for gg in range(2):
                    for k in range(GC):
                        rest(2 * it + (1 + gg), 0, k, True, None)
            for k in range(GC):
                rest(LIVE_GROUPS - 1, 0, k, True, "last live")

        @block.scalar
        def _(act):
            def step(g, par, k, live, edge):
                s, n = k % 2, GC * g + k
                c = GC * place(g, live) + k
                if live and not (edge == "last live" and k == GC - 1):
                    k1 = k + 1
                    round_u(act, mem_, sem, k1 % 2, c + 1, (GC // 2) * place(g, live) + (k1 // 2 + 1))
                waits = [(sem["v_loaded"][s], 16 * (GC // 2) * g + 16 * (k // 2 + 1))]
                if edge != "first":
                    waits.append((sem["summed"], TILES * g))
                held(act, *waits)
                nc.scalar.activation(vr[:, par, k, :], vraw[:, s, :], ACT.Copy).then_inc(sem["v_rounded"], 1)
                if live:
                    waits = [(sem["hidden"], c + 3)]
                    if not (edge == "first" and k < 2):
                        waits.append((sem["weighted"], n + (GC - 1)))
                    held(act, *waits)
                    nc.scalar.activation(act_[:, s, :], hid_bank[s][:], ACT.Gelu).then_inc(sem["gelus"], 1)

            groups(act, step)

        @block.vector
        def _(dve):
            def add_sum(j, n):
                dve.wait_ge(sem["summed"], n + 1 + TILES)
                i, half = divmod(j, 2)
                part = h[:, i, half * HALF:(half + 1) * HALF]
                nc.vector.tensor_tensor(part, part, sum_bank[j % 4][:], ALU.add).then_inc(sem["sum_room"], 1)

            def step(g, par, k, live, edge):
                s, n = k % 2, GC * g + k
                c = GC * place(g, live) + k
                dve.wait_ge(sem["v_rounded"], n + 1)
                if edge != "first":
                    dve.wait_ge(sem["summed"], TILES * g)
                nc.vector.tensor_tensor(vl[:, par, k, :], vraw[:, s, :], vr[:, par, k, :].bitcast(F32),
                                        ALU.subtract).then_inc(sem["v_rest"], 1)
                if live:
                    dve.wait_ge(sem["gelus"], c + 3)
                else:
                    dve.wait_ge(sem["hid_loaded"][s], (16 * (GC // 2)) * (g - LIVE_GROUPS) + 16 * (k // 2 + 1))
                if k == 0:
                    dve.wait_ge(sem["tab_loaded"][par], (g + (2 - par)) * 8)
                nc.vector.tensor_tensor(w32[:, s, :].rearrange("p (a b) -> p a b", a=NTB),
                                        act_[:, s, :].rearrange("p (a b) -> p a b", a=NTB),
                                        tab[:, par, :, k * TB:(k + 1) * TB], ALU.mult).then_inc(sem["weighted"], 1)
                dve.wait_ge(sem["weighted"], n + 1 + GC)
                nc.vector.tensor_copy(wr[:, par, k, :], w32[:, s, :]).then_inc(sem["w_rounded"], 1)
                dve.wait_ge(sem["w_rounded"], n + 1)
                nc.vector.tensor_tensor(wl[:, par, k, :], w32[:, s, :], wr[:, par, k, :].bitcast(F32),
                                        ALU.subtract).then_inc(sem["w_rest"], 1)
                if edge != "first":
                    for j in (2 * k, 2 * k + 1):
                        add_sum(j, TILES * g + (j - TILES))

            dve.sem_inc(sem["sum_room"], 4)
            dve.sem_inc(sem["weighted"], GC)
            groups(dve, step)
            for j in range(TILES):
                add_sum(j, TILES * (GROUPS - 1) + j)

        @block.tensor
        def _(pe):
            def sum_tile(j, n, par):
                pe.wait_ge(sem["sum_room"], n + 1)
                i, half = divmod(j, 2)
                out = sum_bank[j % 4][:]
                rows, cols = slice(i * P, (i + 1) * P), slice(half * HALF, (half + 1) * HALF)
                for k in range(GC):
                    nc.tensor.matmul(out, wr[:, par, k, rows], vr[:, par, k, cols], start=(k == 0), stop=False)
                    nc.tensor.matmul(out, wr[:, par, k, rows], vl[:, par, k, cols], start=False, stop=False)
                    last = nc.tensor.matmul(out, wl[:, par, k, rows], vr[:, par, k, cols],
                                            start=False, stop=(k == GC - 1))
                last.then_inc(sem["summed"], 1)

            def step(g, par, k, live, edge):
                if live:
                    hidden_products(pe, mem_, sem, k % 2, GC * place(g, live) + k)
                if edge != "first":
                    if k == 0:
                        pe.wait_ge(sem["w_rest"], GC * g)
                        pe.wait_ge(sem["v_rest"], GC * g)
                    for j in (2 * k, 2 * k + 1):
                        sum_tile(j, TILES * g + (j - TILES), 1 - par)

            pe.sem_inc(sem["summed"], TILES)
            groups(pe, step)
            pe.wait_ge(sem["w_rest"], GC * GROUPS)
            pe.wait_ge(sem["v_rest"], GC * GROUPS)
            for j in range(TILES):
                sum_tile(j, TILES * (GROUPS - 1) + j, 1)


EXP_AFTER = 8


def build(nc, io):
    names = """consts_loaded eps_set x_squares x_roots x_rstd x_normed xT_ready xT_copied
        bias_loaded gains_loaded pool_loaded prod_ready prod_copied vsh_loaded normed turn_ready turn_copied
        scored logits maxima exps invs probs probsT probsT_copied mixed mixed_copied pads_cleared pool_step
        pooled squares sums roots grstds scaled masked gates_ready gates gated branches_ready merged
        wout_loaded h_loaded h_added out_ready keys_loaded query_ready query_copied h_squares h_roots h_rstd
        h_normed hT_ready hT_copied hT_rounded hT_rest scores_ready scores_copied score_ready scores_used turn_room
        top_ready expo_ready picks_turned picked select_step onehot_room onehots table_room
        u_rest v_rest u_rounded v_rounded hidden gelus weighted w_rounded w_rest summed sum_room
        stored""".split()
    sem = {n: nc.alloc_semaphore(n) for n in names}
    for n, k in (("x_loaded", TT + MT), ("w_loaded", 2), ("wbr_loaded", 3), ("table_stored", 2), ("u_loaded", 2), ("hid_stored", 2), ("hid_loaded", 2),
                 ("v_loaded", 2), ("tab_loaded", 2)):
        sem[n] = [nc.alloc_semaphore(f"{n}{i}") for i in range(k)]

    m = {"bank": [nc.alloc_psum_tensor(f"bank{i}", [P, HALF], F32) for i in range(8)]}

    def at(kb, name, shape, dtype=F32):
        m[name] = sbuf(nc, name, shape, dtype, kb)

    at(0, "wring", [P, 2, KD * W])
    at(32, "h", [P, TT, D])
    at(48, "xnT", [P, KD, T])
    at(64, "memnT", [P, KD, M])
    at(203.5, "consts", [P, CONST_COLS])
    c0 = 0
    for name, cols in CONSTS:
        m[name] = m["consts"][:, c0:c0 + cols]
        c0 += cols
    m["mask"] = m["mask"].rearrange("p (v c) -> p v c", v=3)
    m["edge"] = m["edge"].rearrange("p (g e t) -> p g e t", g=4, e=2)
    at(206.5, "eps", [P, 8])
    at(206.625, "ss", [P, 8])
    at(206.75, "sd", [P, 8])
    at(206.875, "rstd", [P, 8])
    at(160, "xbuf", [P, TT + MT, D])
    at(184, "junk", [P, D])
    at(72, "yT", [P, 3, KW, T])
    at(96, "nraw", [P, 3, TT, W])
    at(120, "vna", [P, TT, W])
    at(128, "vsh", [P, 3, W])
    at(134, "kvmem", [P, 2, MT, W])
    at(142, "qkxT", [P, 3, KW, T])
    at(166, "kmT", [P, XA_H, M])
    at(170, "tmp", [P, TT * W])
    at(170, "logit", [P, 2, M])
    at(172, "prob", [P, 3, M])
    at(175, "probT", [P, 2, M])
    at(178, "bias", [P, 3, NA_H, M])
    at(64, "pooledT", [P, 4, T])
    at(32, "ppad", [P, 4, T + 2 * PAD])
    at(40.5, "wsum", [P, 2, T + 2 * PAD])
    at(45, "gains", [P, 2 * NA_D + 2 * XA_D])
    at(202, "stats", [P, 4 * UNITS])
    m["nmax"], m["total"], m["inv"] = (m["stats"][:, i * UNITS:(i + 1) * UNITS] for i in range(3))
    at(46.5, "gss", [P, 4, 32])
    at(47, "gsd", [P, 4, 32])
    at(47.5, "grstd", [P, 4, 32])
    at(96, "pool_w", [P, 4, P])
    at(96, "wbr", [P, 3, KW, D])
    at(144, "wout", [P, KD, D])
    at(176, "gate", [P, 4, T])
    at(184, "merged", [P, KD, T])
    at(64, "gtmp", [P, 2, T])
    at(48, "hnr", [P, KD, T], F32R)
    at(64, "hnl", [P, KD, T], F32R)
    at(80, "hn32", [P, KD, T])
    at(96, "qpT", [P, HP, T])
    at(128, "hn", [P, 2, D])
    at(136, "junk2", [P, D])
    at(140, "keysT", [P, HP, KEYS])
    at(80, "selT", [P, 3, T])
    at(86, "best", [P, HP, TOPK])
    at(87, "where", [P, HP, TOPK], U32)
    at(88, "wheref", [P, HP, TOPK])
    at(89, "top", [P, HEADS, TOPK])
    at(89.5, "pos", [P, HEADS, TOPK], U32)
    at(90, "part", [P, 2, HEADS, TOPK], U32)
    at(91, "partf", [P, 2, HEADS, TOPK])
    at(92, "pick", [P, 3, HEADS * TOPK])
    at(93.5, "shifted", [P, HEADS, TOPK])
    at(94, "expo", [P, HEADS, TOPK])
    at(94.5, "esum", [P, HEADS])
    at(94.625, "einv", [P, HEADS])
    at(148, "scores", [P, TT, HP, KEYS])
    at(180, "score", [P, HP, KEYS])
    at(188, "score_rest", [P, HP, KEYS])
    at(128, "cand", [P, HEADS, TOPK * TOPK])
    at(136, "cand_rest", [P, HEADS, TOPK * TOPK])
    at(96, "eq", [P, HEADS * TOPK * TOPK])
    at(96, "table", [P, 2, KEYS, TB])
    at(128, "onehot1", [P, 8, KEYS])
    at(132, "onehot2", [P, 8, KEYS])
    at(0, "vraw", [P, 2, D])
    at(8, "ur", [P, 2, D], F32R)
    at(16, "uraw", [P, 2, D])
    at(24, "ul", [P, 2, D], F32R)
    at(80, "tab", [P, 2, NTB, GC * TB])
    at(96, "wr", [P, 2, GC, T], F32R)
    at(112, "wl", [P, 2, GC, T], F32R)
    at(128, "vr", [P, 2, GC, D], F32R)
    at(160, "vl", [P, 2, GC, D], F32R)
    at(196, "act", [P, 2, T])
    at(192, "w32", [P, 2, T])

    stage_norm(nc, sem, m, io)
    stage_attend(nc, sem, m, io)
    stage_merge(nc, sem, m, io)
    stage_query(nc, sem, m, io)
    stage_select(nc, sem, m, io)
    stage_table(nc, sem, m, io)
    stage_experts(nc, sem, m, io)


CONSTS = [("ident", P), ("iota", P), ("edge", 4 * 2 * PAD), ("mix_g", KD), ("mem_g", KD), ("ffn_g", KD),
          ("gate_b", 3 * KD), ("pool_scale", KW), ("mask", 3 * KCOLS)]
CONST_COLS = sum(c for _, c in CONSTS)


def host_constants():
    col = np.arange(QCOLS)
    mask = np.zeros((QCOLS, 3, KCOLS), np.float32)
    for v, j in enumerate((0, 1, 3)):
        first = np.clip(j * QCOLS + col - WCOLS // 2, 0, GRID_C - WCOLS)[:, None]
        key = KEY0[j] // GRID_R + np.arange(KCOLS)[None, :]
        mask[:, v] = np.where((key >= first) & (key < first + WCOLS), 0.0, MASKED)
    mask = np.repeat(mask, GRID_R, axis=0).reshape(P, 3 * KCOLS)
    edge = np.ones((4, 2, PAD), np.float32)
    t = np.arange(T)
    for g, w in enumerate(POOL):
        count = np.clip(t + w // 2, 0, T) - np.clip(t - w // 2, 0, T)
        ratio = (w / count).astype(np.float32)
        edge[g] = ratio[:PAD], ratio[-PAD:]
    edge = np.broadcast_to(edge.reshape(1, -1), (P, 4 * 2 * PAD))
    return mask, edge


def rpb_windows(rpb):
    c, r = np.arange(P) // GRID_R, np.arange(P) % GRID_R
    kc, kr = np.arange(M) // GRID_R, np.arange(M) % GRID_R
    out = []
    for j in (0, 1, 3):
        dc = np.clip(KEY0[j] // GRID_R + kc[None, :] - (j * QCOLS + c[:, None]), 1 - WCOLS, WCOLS - 1) + WCOLS - 1
        dr = kr[None, :] - r[:, None] + GRID_R - 1
        out.append(rpb[:, dr, dc])
    return np.stack(out).transpose(2, 0, 1, 3)


def kernel(x, mem, mix_norm_g, mem_norm_g, w_in, gate_b, w_mem_kv, na_q_g, na_k_g, na_rpb,
           pool_w, pool_scale, xa_q_g, xa_k_g, w_branch_na, w_branch_pool, w_branch_xa, w_out,
           ffn_norm_g, peer_w_q, peer_sub_keys, peer_u, peer_v):
    import concourse.bacc as bacc
    from concourse.bass_utils import run_bass_kernel_spmd

    def arr(a):
        return np.asarray(a)

    def by_rows(w, blocks):
        w = arr(w)
        k, n = w.shape[0] // P, w.shape[1] // blocks
        return w.reshape(k, P, blocks, n).transpose(2, 1, 0, 3).reshape(blocks, P, k * n)

    def per_feature(v):
        return arr(v).reshape(-1, P).T

    def rows(v):
        return np.broadcast_to(arr(v).reshape(1, -1), (P, arr(v).size))

    mask, edge = host_constants()
    f32 = np.float32
    w = arr(w_in)[0]
    mixer, gates = w[:, :N_MIX * W], w[:, N_MIX * W:]
    order = (0, 1, 4, 2, 3)
    mixer = by_rows(mixer, N_MIX)[list(order)]
    gates = gates.reshape(KD, P, 3, KD, P).transpose(3, 1, 0, 2, 4).reshape(KD, P, KD * 3 * P)
    consts = np.concatenate([
        np.eye(P, dtype=f32), np.broadcast_to(np.arange(P, dtype=f32), (P, P)), edge, per_feature(mix_norm_g),
        per_feature(mem_norm_g), per_feature(ffn_norm_g), per_feature(gate_b), per_feature(pool_scale), mask], axis=1)
    by_column = arr(x).reshape(GRID_R, GRID_C, D).transpose(1, 0, 2).reshape(T, D)
    ins = {
        "x": by_column,
        "mem": arr(mem)[0],
        "consts": consts,
        "gains": np.concatenate([rows(na_q_g), rows(na_k_g), rows(xa_q_g), rows(xa_k_g)], axis=1),
        "w_kv": by_rows(arr(w_mem_kv)[0], N_KV),
        "w_mix": mixer,
        "w_gate": gates,
        "bias": rpb_windows(arr(na_rpb)[0]),
        "pool_w": arr(pool_w)[0].transpose(1, 0, 2),
        "w_branch": np.stack([arr(b)[0].reshape(KW, P, D).transpose(1, 0, 2)
                              for b in (w_branch_na, w_branch_pool, w_branch_xa)]),
        "w_out": arr(w_out)[0].reshape(KD, P, D).transpose(1, 0, 2),
        "w_q": by_rows(arr(peer_w_q)[0], N_WQ),
        "keysT": arr(peer_sub_keys)[0].reshape(HP, KEYS, P).transpose(2, 0, 1),
        "u": arr(peer_u)[0].reshape(KEYS, KEYS, KD, P).transpose(1, 3, 2, 0).reshape(KEYS, P, D),
        "v": arr(peer_v)[0].reshape(KEYS, KEYS, D).transpose(1, 0, 2),
    }
    ins = {n: np.ascontiguousarray(a) for n, a in ins.items()}
    nc = bacc.Bacc("TRN2", target_bir_lowering=False, num_devices=1)
    io = {n: nc.dram_tensor(f"in_{n}", a.shape, F32, kind="ExternalInput").ap() for n, a in ins.items()}
    io["out"] = nc.dram_tensor("out_h", (T, D), F32, kind="ExternalOutput").ap()
    io["hid"] = nc.dram_tensor("hidden_spilled", (PRE, P, T), F32, kind="Internal").ap()
    io["table"] = nc.dram_tensor("table_spilled", (P, NTB, KEYS * TB), F32, kind="Internal").ap()
    build(nc, io)
    r = run_bass_kernel_spmd(nc, [{f"in_{n}": a for n, a in ins.items()}], core_ids=[0])
    out = np.asarray(r.results[0]["out_h"])
    return out.reshape(GRID_C, GRID_R, D).transpose(1, 0, 2).reshape(1, T, D)
```

```python
import numpy as np

import concourse.bass as bass
from concourse import mybir
from concourse.alu_op_type import AluOpType as ALU

F32 = mybir.dt.float32
F32R = mybir.dt.float32r
U32 = mybir.dt.uint32
ACT = mybir.ActivationFunctionType
AX_X = mybir.AxisListType.X

P = 128
D = 1024
KD = D // P
T = 512
TT = T // P
M = 256
MT = M // P
W = 512
KW = W // P
NORM_EPS = 1e-6
MASKED = -1e30

GRID_R, GRID_C = 8, 64
NA_H, NA_D = 8, 64
XA_H, XA_D = 4, 128
QCOLS, KCOLS, WCOLS = 16, 32, 16
NJ = GRID_C // QCOLS
KEY0 = [min(max(j * QCOLS - WCOLS // 2, 0), GRID_C - KCOLS) * GRID_R for j in range(NJ)]
VARIANT = [0, 1, 1, 2]
POOL = (2, 4, 8, 16)
PAD = 8

HEADS, KEYS, TOPK = 8, 128, 16
HP = 2 * HEADS
TB = 32
NTB = T // TB
GC = 4
CHUNKS = KEYS
GROUPS = CHUNKS // GC
HALF = 512

BASE = 16640
KB = 1024


def at_least(eng, sem, value):
    if isinstance(value, int) and value <= 0:
        return
    eng.wait_ge(sem, value)


def held(eng, *waits):
    for sem, value in waits:
        at_least(eng, sem, value)
    eng.nop(nofuse=True)


def sbuf(nc, name, shape, dtype, kb):
    return nc.alloc_sbuf_tensor_at(name, shape, dtype, offset=BASE + int(kb * KB))


def bank4(bank):
    return bank[:].rearrange("p (a b) -> p a b", a=4)


N_KV, N_MIX, N_GATE, N_OUT, N_WQ = 2, 5, KD, 2, 4
FIRST_GATE = N_KV + N_MIX
FIRST_OUT = FIRST_GATE + N_GATE
LAST_OUT = FIRST_OUT + N_OUT - 1
FIRST_WQ = FIRST_OUT + N_OUT
LOADS = FIRST_WQ + N_WQ
PARTS = 4
NT = MT + TT
LAG = PARTS - 1


def is_gate(load):
    return FIRST_GATE <= load < FIRST_OUT


def count_pieces():
    pieces, done, ready, first = [], [], {}, []
    n = 0
    for load in range(LOADS):
        first.append(len(pieces))
        banks = MT if load < N_KV else 3 if is_gate(load) else TT
        for k in range(KD):
            pieces.append((load, k))
            if load == LAST_OUT and k < KD - 1:
                done.append(n + TT)
                continue
            if k == KD - 1:
                for i in range(banks):
                    n += 1
                    ready[load, i] = n
            else:
                n += 1
            done.append(n)
        if is_gate(load):
            for b in range(3):
                pieces.append((load, KD + b))
                n += 1
                ready[load, 3 + b] = n
                done.append(n)
    return pieces, done, ready, first + [len(pieces)]


PIECES, PIECE_DONE, BANK_READY, FIRST_PIECE = count_pieces()


def piece_source(mem_, p):
    load, k = PIECES[p]
    if is_gate(load):
        if k >= KD:
            return mem_["wbr_raw"][:, load % 2, (k - KD) * W:(k - KD + 1) * W]
        return mem_["wring"][:, load % 2, k * 3 * P:(k + 1) * 3 * P]
    return mem_["wring"][:, load % 2, k * W:(k + 1) * W]


def piece_loaded(eng, sem, p):
    load, k = PIECES[p]
    if p == 0:
        eng.wait_ge(sem["w_begun"], 16)
    elif k == 0 or p == KD // 2:
        eng.wait_ge(sem["w_loaded"][load % 2], 16 * (load // 2 + 1))
    if k == KD:
        eng.wait_ge(sem["wbr_loaded"][load % 2], 16 * ((load - FIRST_GATE) // 2 + 1))


def piece_part(mem_, name, p):
    load, k = PIECES[p]
    if load == LAST_OUT:
        return mem_[{"wr_part": "wo_r", "wl_part": "wo_l"}[name]][:, k, :]
    return mem_[name][:, p % PARTS, 0:piece_source(mem_, p).shape[1]]


def part_free(eng, sem, p):
    load, k = PIECES[p]
    if load == LAST_OUT:
        eng.wait_ge(sem["pe_steps"], PIECE_DONE[FIRST_PIECE[FIRST_OUT] - 1])
    elif load == FIRST_WQ and k < PARTS:
        eng.wait_ge(sem["pe_steps"], PIECE_DONE[p - KD - PARTS])
    elif p >= PARTS:
        eng.wait_ge(sem["pe_steps"], PIECE_DONE[p - PARTS])


def round_piece(act, mem_, sem, p):
    piece_loaded(act, sem, p)
    part_free(act, sem, p)
    act.activation(piece_part(mem_, "wr_part", p), piece_source(mem_, p), ACT.Copy).then_inc(sem["w_rounded"], 1)


def rest_of_piece(pool, mem_, sem, p):
    pool.wait_ge(sem["w_rounded"], p + 1)
    part_free(pool, sem, p)
    pool.tensor_tensor(piece_part(mem_, "wl_part", p), piece_source(mem_, p),
                       piece_part(mem_, "wr_part", p).bitcast(F32), ALU.subtract).then_inc(sem["w_split"], 1)


def load_weights(sp, sem, mem_, io, n):
    if n >= 2:
        last = FIRST_PIECE[n - 1] - (3 if is_gate(n - 2) else 0)
        sp.wait_ge(sem["w_split"], last)
    src = io["w"][n]
    if n == 0:
        half = KD * W // 2
        sp.dma_start(mem_["wring"][:, 0, 0:half], src[:, 0:half]).then_inc(sem["w_begun"], 16)
        sp.dma_start(mem_["wring"][:, 0, half:], src[:, half:]).then_inc(sem["w_loaded"][0], 16)
        return
    sp.dma_start(mem_["wring"][:, n % 2, 0:src.shape[1]], src).then_inc(sem["w_loaded"][n % 2], 16)


def load_branch(sp, sem, mem_, io, cc):
    if cc >= 2:
        sp.wait_ge(sem["w_split"], FIRST_PIECE[FIRST_GATE + cc - 1])
    sp.dma_start(mem_["wbr_raw"][:, (FIRST_GATE + cc) % 2, :], io["w_branch"][cc]
                 ).then_inc(sem["wbr_loaded"][(FIRST_GATE + cc) % 2], 16)


def gate_banks(bank, cc):
    return [bank[1:4], [bank[0], bank[4], bank[5]]][cc % 2]


def three_passes(pe, out, a, b, start, stop):
    pe.matmul(out, a[0], b[0], start=start, stop=False)
    pe.matmul(out, a[0], b[1], start=False, stop=False)
    return pe.matmul(out, a[1], b[0], start=False, stop=stop)


def piece_products(pe, mem_, sem, p, banks, lhs, rhs, free=None):
    load, k = PIECES[p]
    pe.wait_ge(sem["w_split"], p + 1)
    for i, bank in enumerate(banks):
        if free and k == 0:
            pe.wait_ge(sem["prod_copied"], free(i))
        last = three_passes(pe, bank, [lhs(i, n) for n in (0, 1)], [rhs(i, n) for n in (0, 1)],
                            k == 0, k == KD - 1)
        if k == KD - 1 or i == len(banks) - 1:
            last.then_inc(sem["pe_steps"], 1)


HALVES = [(0, 0), (1, 0), (0, 1), (1, 1)] + [(i, half) for i in range(MT, NT) for half in range(2)]
TILE_AT = [(0, 3), (0, 6), (1, 1), (1, 4)]


def split_turned(dve, mem_, sem, bank, gain, dst_r, dst_l, n):
    tmp = mem_["turned"][:, n % 2, :].rearrange("p (a b) -> p a b", a=4)
    dve.wait_ge(sem["x_turned"], n + 1)
    dve.tensor_tensor(tmp, bank4(bank), gain.unsqueeze(2).to_broadcast([P, 4, P]),
                      ALU.mult).then_inc(sem["x_gained"], 1)
    dve.wait_ge(sem["x_gained"], n + 1)
    dve.tensor_copy(dst_r, tmp).then_inc(sem["x_rounded"], 1)
    dve.wait_ge(sem["x_rounded"], n + 1)
    dve.tensor_tensor(dst_l, tmp, dst_r.bitcast(F32), ALU.subtract).then_inc(sem["x_split"], 1)


TURNS = 2 + 3 * TT
TURN_AT = [(4, 1), (4, 2), (4, 3), (4, 4), (4, 5), (4, 6), (5, 1), (5, 3), (5, 5), (5, 7),
           (6, 1), (6, 3), (6, 5), (6, 7)]
XA_PAIRS = TT * XA_H // 2
PAIRS = XA_PAIRS + NJ * NA_H // 2


GATE_AT = [0, 1, 6, 9, 13, 17, 22, 26]
POOL_AT = [24, 25, 26, 27]
PROBS = 4


def stage_attend(nc, sem, mem_, io):
    bank, ident = mem_["bank"], mem_["ident"]
    prod_bank, turn_bank, score_bank = bank[0:4], bank[4:6], bank[6:8]
    out_bank, pool_bank = bank[0], bank[6:8]
    gate_bank = gate_banks(bank, 0)
    x = mem_["xbuf"]
    nraw, kvmem, vna, vsh = mem_["nraw"], mem_["kvmem"], mem_["vna"], mem_["vsh"]
    qkxT, kmT, yT, bias = mem_["qkxT"], mem_["kmT"], mem_["yT"], mem_["bias"]
    ppad, pooled = mem_["ppad"], mem_["yT"][:, 1]
    xn = (mem_["xnr"], mem_["xnl"])
    memn = (mem_["memnr"], mem_["memnl"])
    wparts = (mem_["wr_part"], mem_["wl_part"])
    LAST = FIRST_PIECE[FIRST_GATE]

    def pair_of(u):
        if u < XA_PAIRS:
            return False, u // 2, (2 * (u % 2), 2 * (u % 2) + 1)
        u -= XA_PAIRS
        h0 = 4 * (u % 4 // 2) + u % 2
        return True, u // 4, (h0, h0 + 2)

    def copied_before(load):
        return MT * min(load, N_KV) + TT * max(load - N_KV, 0)

    STAGES = [(MT * XA_H, XA_D), (TT * NA_H, NA_D), (TT * NA_H, NA_D), (TT * XA_H, XA_D)]
    GROUP0 = [0, 8, 40, 72]
    GAIN0 = [2 * NA_D + XA_D, 0, NA_D, 2 * NA_D]
    ROOT_AT = 4

    with nc.Block() as block:

        @block.sync
        def _(sp):
            for i in range(MT):
                sp.dma_start(x[:, i, :], io["mem"][i * P:(i + 1) * P, :]).then_inc(sem["x_loaded"][i], 16)
            sp.dma_start(mem_["consts"][:], io["consts"]).then_inc(sem["consts_loaded"], 16)
            load_weights(sp, sem, mem_, io, 0)
            for i in range(TT):
                sp.dma_start(x[:, MT + i, :], io["x"][i * P:(i + 1) * P, :]).then_inc(sem["x_loaded"][MT + i], 16)
            load_weights(sp, sem, mem_, io, 1)
            sp.dma_start(mem_["gains"][:], io["gains"]).then_inc(sem["gains_loaded"], 16)
            for n in range(2, FIRST_GATE):
                load_weights(sp, sem, mem_, io, n)
            for v in range(3):
                sp.wait_ge(sem["turn_ready"], 2 + TT * (v + 1))
                sp.dma_start(bias[:, v], io["bias"][:, v]).then_inc(sem["bias_loaded"][v], 16)
                if v == 0:
                    load_weights(sp, sem, mem_, io, FIRST_GATE)
                    sp.dma_start(mem_["pool_w"][:], io["pool_w"]).then_inc(sem["pool_loaded"], 16)
            sp.wait_ge(sem["v_copied"], TT)
            sp.dma_start(vsh[0:64, :, :], vna[64:128, 0:3, :]).then_inc(sem["vsh_loaded"], 16)
            sp.dma_start(vsh[64:128, :, :], vna[0:64, 1:4, :]).then_inc(sem["vsh_loaded"], 16)
            load_weights(sp, sem, mem_, io, FIRST_GATE + 1)
            sp.wait_ge(sem["mixed"], XA_PAIRS)
            for cc in range(2):
                load_branch(sp, sem, mem_, io, cc)
            sp.wait_ge(sem["vsh_loaded"], 32)

        @block.tensor
        def _(pe):
            def turn_halves(n0, count):
                for n in range(n0, n0 + count):
                    i, half = HALVES[n]
                    pe.wait_ge(sem["x_normed"], i + 1)
                    if n >= 2:
                        pe.wait_ge(sem["x_gained"], n - 1)
                    for q in range(4):
                        k = 4 * half + q
                        last = pe.transpose(bank4(turn_bank[n % 2])[:, q, :], x[:, i, k * P:(k + 1) * P], ident)
                    last.then_inc(sem["x_turned"], 1)

            def turn_heads(n):
                stage = 0 if n < 2 else 1 + (n - 2) // TT
                pe.wait_ge(sem["normed"], stage + 1)
                if n >= 2:
                    pe.wait_ge(sem["turn_copied"], n - 1)
                for q in range(4):
                    if n < 2:
                        src = kvmem[:, 0, q % 2, (2 * n + q // 2) * P:(2 * n + q // 2 + 1) * P]
                    else:
                        f = (n - 2) % TT
                        src = nraw[:, stage - 1, q, f * P:(f + 1) * P]
                    last = pe.transpose(bank4(turn_bank[n % 2])[:, q, :], src, ident)
                last.then_inc(sem["turn_ready"], 1)

            pe.wait_ge(sem["consts_loaded"], 16)
            turn_halves(0, 2 * MT)
            for p in range(LAST):
                load, k = PIECES[p]
                rows = [w[:, p % PARTS, :] for w in wparts]
                banks_before = MT if load <= N_KV else TT
                free = (lambda i: copied_before(load - 1) + min(i + 1, banks_before)) if load else None
                if load == 0 and k in (0, 4):
                    pe.wait_ge(sem["x_split"], MT if k == 0 else 2 * MT)
                if load == N_KV and k == 0:
                    pe.wait_ge(sem["x_split"], 2 * NT)
                if load < N_KV:
                    piece_products(pe, mem_, sem, p, [b[:] for b in prod_bank[0:MT]],
                                   lambda i, n: memn[n][:, k, i * P:(i + 1) * P], lambda i, n: rows[n], free)
                elif load < N_KV + 4:
                    piece_products(pe, mem_, sem, p, [b[:] for b in prod_bank],
                                   lambda i, n: xn[n][:, k, i * P:(i + 1) * P], lambda i, n: rows[n], free)
                else:
                    piece_products(pe, mem_, sem, p, [b[:] for b in prod_bank],
                                   lambda i, n: rows[n][:, i * P:(i + 1) * P], lambda i, n: xn[n][:, k, :], free)
                if (load, k) in TILE_AT:
                    turn_halves(2 * (MT + TILE_AT.index((load, k))), 2)
                for n, at in enumerate(TURN_AT):
                    if at == (load, k):
                        turn_heads(n)

            def scores(u):
                if u == 0:
                    pe.wait_ge(sem["turn_copied"], TURNS)
                if u >= 2:
                    pe.wait_ge(sem["exps" if u - 2 < XA_PAIRS else "logits"], u - 1)
                na, i, heads = pair_of(u)
                for e, h in enumerate(heads):
                    if na:
                        rows = slice(64 * (h % 2), 64 * (h % 2) + 64)
                        lhsT = qkxT[rows, 0, h // 2, i * P:(i + 1) * P]
                        rhs = qkxT[rows, 1, h // 2, KEY0[i]:KEY0[i] + M]
                    else:
                        lhsT, rhs = qkxT[:, 2, h, i * P:(i + 1) * P], kmT[:, h, :]
                    last = pe.matmul(score_bank[u % 2][:, e * M:(e + 1) * M], lhsT, rhs, start=True, stop=True)
                last.then_inc(sem["scored"], 1)

            def turn(u):
                pe.wait_ge(sem["probs"], u + 1)
                if u >= 2:
                    pe.wait_ge(sem["probsT_copied"], u - 1)
                for q in range(4):
                    last = pe.transpose(bank4(turn_bank[u % 2])[:, q, :],
                                        mem_["prob"][:, u % PROBS, q * P:(q + 1) * P], ident)
                last.then_inc(sem["probsT"], 1)

            def values(u):
                pe.wait_ge(sem["probsT_copied"], u + 1)
                if u == 0:
                    pe.wait_ge(sem["prod_copied"], copied_before(FIRST_GATE))
                if u == XA_PAIRS:
                    pe.wait_ge(sem["vsh_loaded"], 32)
                if u >= 1:
                    pe.wait_ge(sem["mixed_copied"], u)
                na, i, heads = pair_of(u)
                for e, h in enumerate(heads):
                    for q in range(2):
                        if na:
                            cols = slice(h * NA_D, (h + 1) * NA_D)
                            k0 = KEY0[i] // P + q
                            v = vna[:, k0, cols] if KEY0[i] % P == 0 else vsh[:, k0, cols]
                            out = out_bank[64 * (h % 2):64 * (h % 2) + 64, e * P:(e + 1) * P]
                        else:
                            v = kvmem[:, 1, q, h * P:(h + 1) * P]
                            out = out_bank[:, e * P:(e + 1) * P]
                        last = pe.matmul(out, v, mem_["probT"][:, u % 2, (2 * e + q) * P:(2 * e + q + 1) * P],
                                         start=(q == 0), stop=(q == 1))
                last.then_inc(sem["mixed"], 1)

            def pool_products(g):
                if g == 0:
                    pe.wait_ge(sem["pool_loaded"], 16)
                if g < 2:
                    pe.wait_ge(sem["logits"], PAIRS - 1 + g)
                else:
                    pe.wait_ge(sem["pool_scaled"], g - 1)
                pe.wait_ge(sem["pooled"], g + 1)
                pe.matmul(pool_bank[g % 2][:], mem_["pool_w"][:, g, :], pooled[:, g, :],
                          start=True, stop=True).then_inc(sem["pool_mixed"], 1)

            for s in range(PAIRS + 4):
                if s < PAIRS:
                    scores(s)
                if 0 <= s - 3 < PAIRS:
                    turn(s - 3)
                if 0 <= s - 4 < PAIRS:
                    values(s - 4)
                if s in GATE_AT:
                    k = GATE_AT.index(s)
                    p = LAST + k
                    if k == 0:
                        pe.wait_ge(sem["prod_copied"], copied_before(FIRST_GATE))
                    rows = [w[:, p % PARTS, :] for w in wparts]
                    piece_products(pe, mem_, sem, p, [b[:] for b in gate_bank],
                                   lambda b, n: rows[n][:, b * P:(b + 1) * P], lambda b, n: xn[n][:, k, :])
                for g in range(4):
                    if POOL_AT[g] == s:
                        pool_products(g)

        @block.scalar
        def _(act):
            def square(i):
                act.wait_ge(sem["x_loaded"][i], 16)
                if i:
                    act.wait_ge(sem["x_squares"], i)
                act.activation(mem_["junk"][:], x[:, i, :], ACT.Square,
                               accum_out=mem_["ss"][:, i:i + 1]).then_inc(sem["x_squares"], 1)
                act.wait_ge(sem["x_squares"], i + 1)
                act.activation(mem_["sd"][:, i:i + 1], mem_["ss"][:, i:i + 1], ACT.Sqrt,
                               scale=1.0 / D, bias=mem_["eps"][:, 0:1]).then_inc(sem["x_roots"], 1)

            def copy_products(load):
                for i in range(MT if load < N_KV else TT):
                    act.wait_ge(sem["pe_steps"], BANK_READY[load, i])
                    src = prod_bank[i][:]
                    if load < N_KV:
                        dst = kvmem[:, load, i, :]
                    elif load < N_KV + 3:
                        dst = nraw[:, load - N_KV, i, :]
                    elif load == N_KV + 3:
                        dst = vna[:, i, :]
                    else:
                        dst = ppad[:, i, PAD:PAD + T].rearrange("p (r c) -> p c r", c=GRID_C)
                        src = src.rearrange("p (c r) -> p c r", r=GRID_R)
                    if load == N_KV + 4 and i == 0:
                        act.wait_ge(sem["pads_cleared"], 1)
                    act.activation(dst, src, ACT.Copy).then_inc(sem["prod_copied"], 1)
                    if load == N_KV + 3:
                        act.wait_ge(sem["prod_copied"], copied_before(load) + i + 1)
                        act.sem_inc(sem["v_copied"], 1)

            def root(stage):
                n, dim = STAGES[stage]
                act.wait_ge(sem["sums"], stage + 1)
                g0 = GROUP0[stage]
                act.activation(mem_["gsd"][:, g0:g0 + n], mem_["gss"][:, g0:g0 + n], ACT.Sqrt,
                               scale=1.0 / dim, bias=mem_["eps"][:, 0:1]).then_inc(sem["roots"], 1)

            def copy_turn(n):
                act.wait_ge(sem["turn_ready"], n + 1)
                if n < 2:
                    dst = kmT[:, 2 * n:2 * n + 2, :].rearrange("p a b -> p (a b)")
                else:
                    dst = qkxT[:, (n - 2) // TT, (n - 2) % TT, :]
                act.activation(dst, turn_bank[n % 2][:], ACT.Copy).then_inc(sem["turn_copied"], 1)

            act.wait_ge(sem["eps_set"], 1)
            act.activation(mem_["sd"][:, NT:NT + 1], mem_["eps"][:, 0:1], ACT.Sqrt)
            for i in range(MT):
                square(i)
            for p in range(LAST + LAG):
                round_piece(act, mem_, sem, p)
                if 1 <= p <= TT:
                    square(MT + p - 1)
                at = PIECES[p - LAG] if p >= LAG else None
                for n, where in enumerate(TURN_AT):
                    if at == where:
                        copy_turn(n)
                if at and at[1] == KD - 1:
                    copy_products(at[0])
                if at and at[1] == ROOT_AT and N_KV <= at[0] < N_KV + 4:
                    root(at[0] - N_KV)
            for s in range(PAIRS + 4):
                u = s - 3
                if 0 <= u < PAIRS:
                    act.wait_ge(sem["probsT"], u + 1)
                    if u >= 2:
                        act.wait_ge(sem["mixed"], u - 1)
                    act.activation(mem_["probT"][:, u % 2, :], turn_bank[u % 2][:],
                                   ACT.Copy).then_inc(sem["probsT_copied"], 1)
                if s < PAIRS:
                    act.wait_ge(sem["maxima"], s + 1)
                    if s >= PROBS and not pair_of(s)[0]:
                        act.wait_ge(sem["probsT"], s - PROBS + 1)
                    for e in range(2):
                        part = mem_["prob"][:, s % PROBS, e * M:(e + 1) * M]
                        na = pair_of(s)[0]
                        last = act.activation(part, part if na else score_bank[s % 2][:, e * M:(e + 1) * M], ACT.Exp,
                                              bias=mem_["nmax"][:, 2 * s + e:2 * s + e + 1],
                                              scale=1.0 if na else XA_D ** -0.5,
                                              accum_out=mem_["total"][:, 2 * s + e:2 * s + e + 1])
                    last.then_inc(sem["exps"], 1)
                u = s - 4
                if 0 <= u < PAIRS:
                    act.wait_ge(sem["mixed"], u + 1)
                    na, i, heads = pair_of(u)
                    src = out_bank[:, 0:2 * P].rearrange("p (a b) -> p a b", a=2)
                    if na:
                        rows = slice(64 * (heads[0] % 2), 64 * (heads[0] % 2) + 64)
                        dst = yT[rows, 0, heads[0] // 2:heads[0] // 2 + 2, i * P:(i + 1) * P]
                        src = src[rows]
                    else:
                        dst = yT[:, 2, heads[0]:heads[0] + 2, i * P:(i + 1) * P]
                    act.activation(dst, src, ACT.Copy).then_inc(sem["mixed_copied"], 1)
                if s in GATE_AT:
                    round_piece(act, mem_, sem, LAST + LAG + GATE_AT.index(s))
                for g in range(4):
                    if POOL_AT[g] == s:
                        act.wait_ge(sem["pool_mixed"], g + 1)
                        act.activation(yT[:, 1, g, :], pool_bank[g % 2][:], ACT.Copy,
                                       scale=mem_["pool_scale"][:, g:g + 1]).then_inc(sem["pool_scaled"], 1)

        @block.gpsimd
        def _(pool):
            for p in range(LAST + LAG):
                rest_of_piece(pool, mem_, sem, p)
                if p == FIRST_PIECE[N_KV + 1]:
                    pool.wait_ge(sem["pe_steps"], BANK_READY[N_KV - 1, MT - 1])
                    pool.memset(ppad[:], 0.0).then_inc(sem["pads_cleared"], 1)
            rows = mem_["wsum"]
            step = 0
            for g in range(4):
                pool.wait_ge(sem["prod_copied"], copied_before(N_KV + 4) + g + 1)
                src = ppad[:, g, :]
                lo, hi = 0, T + 2 * PAD
                half = 1
                for level in range(g + 1):
                    shift_lo, shift_hi = (1, 0) if level == 0 else (half // 2, half // 2)
                    lo, hi = lo + shift_lo, hi - shift_hi
                    dst = rows[:, level % 2, :]
                    pool.tensor_tensor(dst[:, lo:hi], src[:, lo - shift_lo:hi - shift_lo],
                                       src[:, lo + shift_hi:hi + shift_hi], ALU.add).then_inc(sem["pool_step"], 1)
                    step += 1
                    pool.wait_ge(sem["pool_step"], step)
                    src = dst
                    half *= 2
                w = POOL[g]
                mean = rows[:, g % 2, PAD:PAD + T]
                pool.tensor_scalar(mean, mean, 1.0 / w, None, ALU.mult).then_inc(sem["pool_step"], 1)
                step += 1
                pool.wait_ge(sem["pool_step"], step)
                for e, cols in ((0, slice(0, PAD)), (1, slice(T - PAD, T))):
                    pool.tensor_tensor(mean[:, cols], mean[:, cols], mem_["edge"][:, g, e, :],
                                       ALU.mult).then_inc(sem["pool_step"], 1)
                    step += 1
                pool.wait_ge(sem["pool_step"], step)
                pool.tensor_tensor(pooled[:, g, :].rearrange("p (c r) -> p c r", r=GRID_R),
                                   mean.rearrange("p (r c) -> p c r", c=GRID_C),
                                   ppad[:, g, PAD:PAD + T].rearrange("p (r c) -> p c r", c=GRID_C),
                                   ALU.subtract).then_inc(sem["pooled"], 1)
                pool.wait_ge(sem["pooled"], g + 1)
                rest_of_piece(pool, mem_, sem, LAST + LAG + g)
            for p in range(LAST + LAG + 4, LAST + LAG + KD):
                rest_of_piece(pool, mem_, sem, p)


        @block.vector
        def _(dve):
            tmp = mem_["tmp"]
            source = [kvmem[:, 0], nraw[:, 0], nraw[:, 1], nraw[:, 2]]
            need = [MT, copied_before(N_KV + 1), copied_before(N_KV + 2), copied_before(N_KV + 3)]

            def normalise_tile(i):
                dve.wait_ge(sem["x_roots"], i + 1)
                dve.reciprocal(mem_["rstd"][:, i:i + 1], mem_["sd"][:, i:i + 1]).then_inc(sem["x_rstd"], 1)
                dve.wait_ge(sem["x_rstd"], i + 1)
                dve.tensor_scalar(x[:, i, :], x[:, i, :], mem_["rstd"][:, i:i + 1], None,
                                  ALU.mult).then_inc(sem["x_normed"], 1)

            def split_half(n):
                i, half = HALVES[n]
                g, dst, t0 = (mem_["mem_g"], memn, i * P) if i < MT else (mem_["mix_g"], xn, (i - MT) * P)
                where = (slice(None), slice(4 * half, 4 * half + 4), slice(t0, t0 + P))
                split_turned(dve, mem_, sem, turn_bank[n % 2], g[:, 4 * half:4 * half + 4],
                             dst[0][where], dst[1][where], n)

            def sums(s):
                n, dim = STAGES[s]
                dve.wait_ge(sem["prod_copied"], need[s])
                flat = source[s].rearrange("p a b -> p (a b)")
                dve.tensor_tensor(tmp[:, 0:n * dim], flat, flat, ALU.mult).then_inc(sem["squares"], 1)
                dve.wait_ge(sem["squares"], s + 1)
                g0 = GROUP0[s]
                dve.tensor_reduce(mem_["gss"][:, g0:g0 + n], tmp[:, 0:n * dim].rearrange("p (g d) -> p g d", d=dim),
                                  AX_X, ALU.add).then_inc(sem["sums"], 1)
                dve.wait_ge(sem["sums"], s + 1)

            def norm(s):
                n, dim = STAGES[s]
                g0, a0 = GROUP0[s], GAIN0[s]
                dve.wait_ge(sem["roots"], s + 1)
                dve.reciprocal(mem_["grstd"][:, g0:g0 + n], mem_["gsd"][:, g0:g0 + n]).then_inc(sem["grstds"], 1)
                dve.wait_ge(sem["grstds"], s + 1)
                v = source[s].rearrange("p a (h d) -> p (a h) d", d=dim)
                dve.tensor_tensor(v, v, mem_["grstd"][:, g0:g0 + n].unsqueeze(2).to_broadcast([P, n, dim]),
                                  ALU.mult).then_inc(sem["scaled"], 1)
                dve.wait_ge(sem["scaled"], s + 1)
                dve.tensor_tensor(v, v, mem_["gains"][:, a0:a0 + dim].unsqueeze(1).to_broadcast([P, n, dim]),
                                  ALU.mult).then_inc(sem["normed"], 1)

            dve.memset(mem_["eps"][:], NORM_EPS).then_inc(sem["eps_set"], 1)
            dve.wait_ge(sem["consts_loaded"], 16)
            for i in range(MT):
                normalise_tile(i)
            for n in range(2 * MT):
                split_half(n)
            for i in range(MT, NT):
                normalise_tile(i)
            for n in range(2 * MT, 2 * NT):
                split_half(n)
            dve.wait_ge(sem["gains_loaded"], 16)
            dve.wait_ge(sem["x_split"], 2 * NT)
            for s in range(4):
                sums(s)
                norm(s)

            def add_mask(v, heads):
                dve.wait_ge(sem["bias_loaded"][v], 16)
                for h in heads:
                    table = bias[:, v, h, :].rearrange("p (c r) -> p c r", r=GRID_R)
                    dve.tensor_tensor(table, table, mem_["mask"][:, v, :].unsqueeze(2)
                                      .to_broadcast([P, KCOLS, GRID_R]), ALU.add).then_inc(sem["masked"], 1)

            def logits(u):
                dve.wait_ge(sem["scored"], u + 1)
                na, i, heads = pair_of(u)
                src = score_bank[u % 2][:].rearrange("p (a b) -> p a b", a=2)
                nmax = mem_["nmax"][:, 2 * u:2 * u + 2]
                if na:
                    out = mem_["prob"][:, u % PROBS, :].rearrange("p (a b) -> p a b", a=2)
                    v = VARIANT[i]
                    dve.wait_ge(sem["masked"], NA_H * (v + 1))
                    dve.wait_ge(sem["probsT"], u - PROBS + 1)
                    dve.scalar_tensor_tensor(out, src, NA_D ** -0.5, bias[:, v, heads[0]:heads[1] + 1:2, :],
                                             ALU.mult, ALU.add).then_inc(sem["logits"], 1)
                    dve.wait_ge(sem["logits"], u + 1)
                    dve.tensor_reduce(nmax, out, AX_X, ALU.max, negate=True).then_inc(sem["maxima"], 1)
                else:
                    dve.tensor_reduce(nmax, src, AX_X, ALU.max, negate=True).then_inc(sem["logits"], 1)
                    dve.wait_ge(sem["logits"], u + 1)
                    dve.tensor_scalar(nmax, nmax, XA_D ** -0.5, None, ALU.mult).then_inc(sem["maxima"], 1)

            def normalise(u):
                dve.wait_ge(sem["exps"], u + 1)
                dve.reciprocal(mem_["inv"][:, 2 * u:2 * u + 2], mem_["total"][:, 2 * u:2 * u + 2]
                               ).then_inc(sem["invs"], 1)
                dve.wait_ge(sem["invs"], u + 1)
                for e in range(2):
                    p = mem_["prob"][:, u % PROBS, e * M:(e + 1) * M]
                    last = dve.tensor_scalar(p, p, mem_["inv"][:, 2 * u + e:2 * u + e + 1], None, ALU.mult)
                last.then_inc(sem["probs"], 1)

            for s in range(PAIRS + 1):
                if s < XA_PAIRS:
                    add_mask(0, [s])
                elif s < XA_PAIRS + 4:
                    add_mask(1, [2 * (s - XA_PAIRS), 2 * (s - XA_PAIRS) + 1])
                elif s < XA_PAIRS + 12:
                    add_mask(2, [s - XA_PAIRS - 4])
                if s < PAIRS:
                    logits(s)
                if s >= 1:
                    normalise(s - 1)


def stage_merge_and_query(nc, sem, mem_, io):
    bank, ident = mem_["bank"], mem_["ident"]
    branch_bank = bank[6:8]
    xn = (mem_["xnr"], mem_["xnl"])
    y32, y = mem_["yT"], (mem_["yr"], mem_["yl"])
    gate, merged32, merged, h = mem_["gate"], mem_["merged"], (mem_["mr"], mem_["ml"]), mem_["h"]
    wparts = (mem_["wr_part"], mem_["wl_part"])
    turn_bank = bank[0:2]
    hn, qpT = (mem_["hnr"], mem_["hnl"]), mem_["qpT"]
    START, STOP = FIRST_PIECE[FIRST_GATE] + KD, FIRST_PIECE[LOADS]
    WQ = FIRST_PIECE[FIRST_WQ]

    with nc.Block() as block:

        @block.sync
        def _(sp):
            for cc in range(2, N_GATE):
                load_weights(sp, sem, mem_, io, FIRST_GATE + cc)
                load_branch(sp, sem, mem_, io, cc)
            for i in range(TT):
                sp.dma_start(h[:, i, :], io["x"][i * P:(i + 1) * P, :]).then_inc(sem["h_loaded"], 16)
            for n in range(FIRST_OUT, FIRST_WQ):
                load_weights(sp, sem, mem_, io, n)
            sp.wait_ge(sem["w_split"], FIRST_PIECE[FIRST_OUT])
            sp.dma_start(mem_["ffn_gain"][:], io["ffn_gain"]).then_inc(sem["gain_loaded"], 16)
            for n in range(FIRST_WQ, FIRST_WQ + 2):
                load_weights(sp, sem, mem_, io, n)
            sp.wait_ge(sem["pe_steps"], BANK_READY[LAST_OUT, TT - 1])
            sp.dma_start(mem_["keysT"][:], io["keysT"]).then_inc(sem["keys_loaded"], 16)
            for n in range(FIRST_WQ + 2, LOADS):
                load_weights(sp, sem, mem_, io, n)
            assert (LOADS - 2) % 2 == 1
            sp.wait_ge(sem["w_split"], FIRST_PIECE[LOADS - 1])
            for s in range(2):
                load_u(sp, mem_, sem, io, s, s)

        @block.gpsimd
        def _(pool):
            for p in range(START + LAG, STOP):
                rest_of_piece(pool, mem_, sem, p)

        def query_banks(n):
            return bank[4:8] if n % 2 == 0 else bank[0:4]

        @block.tensor
        def _(pe):
            def last_half(pe, i, p):
                for q in range(KD):
                    if i == 0:
                        pe.wait_ge(sem["w_split"], p + q + 1)
                    last = three_passes(pe, bank[4 + i][:], [m[:, q, i * P:(i + 1) * P] for m in merged],
                                        [mem_[n][:, q, :] for n in ("wo_r", "wo_l")], q == 0, q == KD - 1)
                last.then_inc(sem["pe_steps"], 1)

            def turn_tile(i):
                pe.wait_ge(sem["h_normed"], i + 1)
                if i == 0:
                    pe.wait_ge(sem["h_added"], TT)
                for half in range(2):
                    n = 2 * i + half
                    if n >= 2:
                        pe.wait_ge(sem["h_split"], n - 1)
                    for q in range(4):
                        k = 4 * half + q
                        last = pe.transpose(bank4(turn_bank[n % 2])[:, q, :],
                                            mem_["hn"][:, i % 2, k * P:(k + 1) * P], ident)
                    last.then_inc(sem["h_turned"], 1)

            for p in range(START, STOP):
                load, k = PIECES[p]
                cc = load - FIRST_GATE
                rows = [w[:, p % PARTS, :] for w in wparts]
                if is_gate(load) and k < KD:
                    banks = gate_banks(bank, cc)
                    if k == 0 and cc >= 2:
                        pe.wait_ge(sem["gates"], 3 * (cc - 1))
                    piece_products(pe, mem_, sem, p, [b[:] for b in banks],
                                   lambda b, n: rows[n][:, b * P:(b + 1) * P], lambda b, n: xn[n][:, k, :])
                elif is_gate(load):
                    b = k - KD
                    job = 3 * cc + b
                    pe.wait_ge(sem["w_split"], p + 1)
                    if job >= 2:
                        pe.wait_ge(sem["gated"], job - 1)
                    for q in range(KW):
                        if cc == 0:
                            pe.wait_ge(sem["y_split"], KW * b + q + 1)
                        last = three_passes(pe, branch_bank[job % 2][:], [r[:, q * P:(q + 1) * P] for r in rows],
                                            [t[:, b, q, :] for t in y], q == 0, q == KW - 1)
                    last.then_inc(sem["pe_steps"], 1)
                elif load == FIRST_OUT:
                    pe.wait_ge(sem["merged_split"], k + 1)
                    if k == 0:
                        pe.wait_ge(sem["gates"], 3 * N_GATE)
                    piece_products(pe, mem_, sem, p, [b[:] for b in bank[0:4]],
                                   lambda i, n: merged[n][:, k, i * P:(i + 1) * P], lambda i, n: rows[n])
                elif load == LAST_OUT:
                    if k == 0:
                        pe.wait_ge(sem["gated"], 3 * N_GATE)
                        for i in range(TT):
                            last_half(pe, i, p)
                            if i:
                                turn_tile(i - 1)
                        turn_tile(TT - 1)
                else:
                    n = load - FIRST_WQ
                    if n == 0 and k in (0, 4):
                        pe.wait_ge(sem["h_split"], 2 * TT - (k == 0))
                    if k == 0 and n >= 2:
                        pe.wait_ge(sem["query_copied"], 4 * (n - 1))
                    piece_products(pe, mem_, sem, p, [b[:] for b in query_banks(n)],
                                   lambda i, e: rows[e][:, i * P:(i + 1) * P], lambda i, e: hn[e][:, k, :])

        @block.scalar
        def _(act):
            def round_turned(i):
                for half in range(2):
                    act.wait_ge(sem["h_turned"], 2 * i + half + 1)
                    act.activation(hn[0][:, 4 * half:4 * half + 4, i * P:(i + 1) * P],
                                   bank4(turn_bank[half]), ACT.Copy).then_inc(sem["h_rounded"], 1)

            def norm_tiles():
                for i in range(TT):
                    act.wait_ge(sem["h_added"], TT + i + 1)
                    if i:
                        act.wait_ge(sem["h_squares"], i)
                    act.activation(mem_["junk2"][:], h[:, i, :], ACT.Square,
                                   accum_out=mem_["ss"][:, i:i + 1]).then_inc(sem["h_squares"], 1)
                    act.wait_ge(sem["h_squares"], i + 1)
                    act.activation(mem_["sd"][:, i:i + 1], mem_["ss"][:, i:i + 1], ACT.Sqrt,
                                   scale=1.0 / D, bias=mem_["eps"][:, 0:1]).then_inc(sem["h_roots"], 1)
                    if i:
                        round_turned(i - 1)
                round_turned(TT - 1)

            def copy_queries(load, k):
                if k == KD - 1:
                    for i in range(4):
                        act.wait_ge(sem["pe_steps"], BANK_READY[load, i])
                        act.activation(qpT[:, 4 * (load - FIRST_WQ) + i, :], query_banks(load - FIRST_WQ)[i][:],
                                       ACT.Copy).then_inc(sem["query_copied"], 1)

            for p in range(START, STOP + LAG):
                if p == WQ + PARTS:
                    norm_tiles()
                if START + 2 * LAG <= p < STOP:
                    round_piece(act, mem_, sem, p)
                if p >= WQ + LAG:
                    copy_queries(*PIECES[p - LAG])
                load, k = PIECES[p] if p < STOP else (LOADS, 0)
                if p in (START, START + 2):
                    for q in range(KW):
                        act.activation(y[0][:, k - KD, q], y32[:, k - KD, q], ACT.Copy).then_inc(sem["y_rounded"], 1)
                if p < START + LAG:
                    round_piece(act, mem_, sem, p + LAG)
                if is_gate(load) and (p == START or k == KD + 2 and load > FIRST_GATE):
                    cc = load - FIRST_GATE
                    for b in range(3):
                        job = 3 * cc + b
                        act.wait_ge(sem["pe_steps"], BANK_READY[load, b])
                        if job >= 4:
                            act.wait_ge(sem["gated"], job - 3)
                        act.activation(gate[:, job % 4, :], gate_banks(bank, cc)[b][:], ACT.Sigmoid,
                                       bias=mem_["gate_b"][:, b * KD + cc:b * KD + cc + 1],
                                       scale=1.0).then_inc(sem["gates"], 1)

        @block.vector
        def _(dve):
            for n in range(3 * KW):
                b, q = divmod(n, KW)
                if b == 1:
                    dve.tensor_copy(y[0][:, b, q], y32[:, b, q]).then_inc(sem["pooled_rounded"], 1)
                    dve.wait_ge(sem["pooled_rounded"], q + 1)
                else:
                    dve.wait_ge(sem["y_rounded"], KW * (b // 2) + q + 1)
                dve.tensor_tensor(y[1][:, b, q], y32[:, b, q], y[0][:, b, q].bitcast(F32),
                                  ALU.subtract).then_inc(sem["y_split"], 1)
            tmp = mem_["gtmp"]
            for job in range(3 * N_GATE):
                cc, b = divmod(job, 3)
                dve.wait_ge(sem["gates"], job + 1)
                dve.wait_ge(sem["pe_steps"], BANK_READY[FIRST_GATE + cc, 3 + b])
                dst = merged32[:, cc, :] if b == 0 else tmp[:, b - 1, :]
                if b and cc:
                    dve.wait_ge(sem["merged"], 2 * (cc - 1) + b)
                dve.tensor_tensor(dst, branch_bank[job % 2][:], gate[:, job % 4, :],
                                  ALU.mult).then_inc(sem["gated"], 1)
                dve.wait_ge(sem["gated"], job + 1)
                if b:
                    if b == 2:
                        dve.wait_ge(sem["merged"], 2 * cc + 1)
                    dve.tensor_tensor(merged32[:, cc, :], merged32[:, cc, :], dst,
                                      ALU.add).then_inc(sem["merged"], 1)
                if b == 2:
                    dve.wait_ge(sem["merged"], 2 * cc + 2)
                    dve.tensor_copy(merged[0][:, cc, :], merged32[:, cc, :]).then_inc(sem["merged_rounded"], 1)
                    dve.wait_ge(sem["merged_rounded"], cc + 1)
                    dve.tensor_tensor(merged[1][:, cc, :], merged32[:, cc, :], merged[0][:, cc, :].bitcast(F32),
                                      ALU.subtract).then_inc(sem["merged_split"], 1)
            dve.wait_ge(sem["h_loaded"], 16 * TT)
            def add_half(half, i):
                dve.wait_ge(sem["pe_steps"], BANK_READY[FIRST_OUT + half, i])
                part = h[:, i, half * HALF:(half + 1) * HALF]
                dve.tensor_tensor(part, part, bank[4 * half + i][:], ALU.add).then_inc(sem["h_added"], 1)

            def split_tile(i):
                for half in range(2):
                    dve.wait_ge(sem["h_rounded"], 2 * i + half + 1)
                    where = (slice(None), slice(4 * half, 4 * half + 4), slice(i * P, (i + 1) * P))
                    dve.tensor_tensor(hn[1][where], bank4(turn_bank[half]), hn[0][where].bitcast(F32),
                                      ALU.subtract).then_inc(sem["h_split"], 1)

            for i in range(TT):
                add_half(0, i)
            dve.wait_ge(sem["gain_loaded"], 16)
            for i in range(TT):
                add_half(1, i)
                dve.wait_ge(sem["h_roots"], i + 1)
                dve.reciprocal(mem_["rstd"][:, i:i + 1], mem_["sd"][:, i:i + 1]).then_inc(sem["h_rstd"], 1)
                dve.wait_ge(sem["h_rstd"], i + 1)
                if i >= 2:
                    dve.wait_ge(sem["h_turned"], 2 * (i - 1))
                dve.scalar_tensor_tensor(mem_["hn"][:, i % 2, :], h[:, i, :], mem_["rstd"][:, i:i + 1],
                                         mem_["ffn_gain"][:], ALU.mult, ALU.mult).then_inc(sem["h_normed"], 1)
                if i:
                    split_tile(i - 1)
            split_tile(TT - 1)


SELECT_PRE = 12
TABLE_PRE = 4
PRE = SELECT_PRE * TT + TABLE_PRE * (NTB // 2)
LIVE = CHUNKS - PRE
LIVE_GROUPS = LIVE // GC



def hidden_products(pe, mem_, sem, s, c, part=0, parts=1):
    if part == 0:
        pe.wait_ge(sem["u_rest"], c + 1)
        pe.wait_ge(sem["gelus"], c + 1)
    ur, ul, hnr, hnl = mem_["ur"], mem_["ul"], mem_["hnr"], mem_["hnl"]
    out = mem_["bank"][s][:]
    for d in range(part * KD // parts, (part + 1) * KD // parts):
        cols = slice(d * P, (d + 1) * P)
        pe.matmul(out, ur[:, s, cols], hnr[:, d, :], start=(d == 0), stop=False)
        pe.matmul(out, ur[:, s, cols], hnl[:, d, :], start=False, stop=False)
        last = pe.matmul(out, ul[:, s, cols], hnr[:, d, :], start=False, stop=(d == KD - 1))
    if part == parts - 1:
        last.then_inc(sem["hidden"], 1)


def round_u(act, mem_, sem, s, c, loads):
    held(act, (sem["u_loaded"][s], 16 * loads), (sem["hidden"], c + 1))
    act.activation(mem_["ur"][:, s, :], mem_["uraw"][:, s, :], ACT.Copy).then_inc(sem["u_rounded"], 1)


def rest_of_u(pool, mem_, sem, s, c):
    pool.wait_ge(sem["u_rounded"], c + 1)
    pool.wait_ge(sem["hidden"], c + 1)
    pool.tensor_tensor(mem_["ul"][:, s, :], mem_["uraw"][:, s, :], mem_["ur"][:, s, :].bitcast(F32),
                       ALU.subtract).then_inc(sem["u_rest"], 1)


def load_u(sp, mem_, sem, io, s, c):
    sp.dma_start(mem_["uraw"][:, s, :], io["u"][bass.ds(c, 1)].rearrange("a p n -> p (a n)")
                 ).then_inc(sem["u_loaded"][s], 16)


def early_gelu(act, mem_, sem, s, c, half):
    held(act, (sem["hidden"], c + 3), (sem["hid_stored"][s], 16 * half + 16))
    act.activation(mem_["act"][:, s, :], mem_["bank"][s][:], ACT.Gelu).then_inc(sem["gelus"], 1)


def store_and_load(sp, mem_, sem, io, s, c):
    sp.wait_ge(sem["gelus"], c + 3)
    sp.dma_start(io["hid"][bass.ds(c, 1)].rearrange("a p n -> p (a n)"), mem_["act"][:, s, :]
                 ).then_inc(sem["hid_stored"][s], 16)
    sp.wait_ge(sem["u_rest"], c + 2)
    load_u(sp, mem_, sem, io, 1 - s, c + 3)


def stage_select(nc, sem, mem_, io):
    bank, ident = mem_["bank"], mem_["ident"]
    qpT, keysT, selT = mem_["qpT"], mem_["keysT"], mem_["selT"]
    score_bank, turn_bank = bank[2:6], bank[6]
    scores, score, rest = mem_["scores"], mem_["score"], mem_["score_rest"]
    best, where, bestf = mem_["best"], mem_["where"], mem_["wheref"]
    cand, crest = mem_["cand"], mem_["cand_rest"]
    top, pos = mem_["top"], mem_["pos"]
    part, partf, pick = mem_["part"], mem_["partf"], mem_["pick"]
    low = -3.0e38

    with nc.Block() as block:

        @block.sync
        def _(sp):
            for s in range(2):
                sp.sem_inc(sem["hid_stored"][s], 16)
            sp.wait_ge(sem["u_rest"], 1)
            load_u(sp, mem_, sem, io, 0, 2)
            with sp.Fori(0, TT) as i:
                for k in range(SELECT_PRE):
                    store_and_load(sp, mem_, sem, io, k % 2, SELECT_PRE * i + k)

        @block.gpsimd
        def _(pool):
            rest_of_u(pool, mem_, sem, 0, 0)
            with pool.Fori(0, TT) as i:
                for k in range(SELECT_PRE):
                    rest_of_u(pool, mem_, sem, (k + 1) % 2, SELECT_PRE * i + (k + 1))

        @block.tensor
        def _(pe):
            pe.sem_inc(sem["hidden"], 2)
            pe.wait_ge(sem["keys_loaded"], 16)
            for n in range(4 * TT):
                i, b = divmod(n, 4)
                if n >= 4:
                    pe.wait_ge(sem["scores_copied"], n - 3)
                for q in range(4):
                    f = 4 * b + q
                    last = nc.tensor.matmul(bank4(score_bank[n % 4])[:, q, :], qpT[:, f, i * P:(i + 1) * P],
                                            keysT[:, f, :], start=True, stop=True)
                last.then_inc(sem["scores_ready"], 1)
            with pe.Fori(0, TT) as i:
                for k in range(SELECT_PRE):
                    hidden_products(pe, mem_, sem, k % 2, SELECT_PRE * i + k)
                pe.wait_ge(sem["picked"], 3 * i + 3)
                pe.wait_ge(sem["turn_room"], i + 1)
                for n in range(3):
                    last = nc.tensor.transpose(bank4(turn_bank)[:, n, :], pick[:, n, :], ident)
                last.then_inc(sem["picks_turned"], 1)

        @block.scalar
        def _(act):
            act.sem_inc(sem["gelus"], 2)
            act.sem_inc(sem["turn_room"], 1)
            round_u(act, mem_, sem, 0, 0, 1)
            for n in range(4 * TT):
                act.wait_ge(sem["scores_ready"], n + 1)
                nc.scalar.activation(scores[:, n // 4, 4 * (n % 4):4 * (n % 4) + 4, :], bank4(score_bank[n % 4]),
                                     ACT.Copy).then_inc(sem["scores_copied"], 1)
                if n == 3:
                    act.wait_ge(sem["scores_copied"], 4)
                    nc.scalar.activation(score[:], scores[:, 0], ACT.Copy).then_inc(sem["score_ready"], 1)

            def turn(i, is_last):
                for k in range(SELECT_PRE):
                    if k == SCORE_AFTER and not is_last:
                        held(act, (sem["scores_used"], i + 1), (sem["scores_copied"], 4 * TT))
                        nc.scalar.activation(score[:], scores[:, bass.ds(i + 1, 1)].rearrange("p a f n -> p (a f) n"),
                                             ACT.Copy).then_inc(sem["score_ready"], 1)
                    c = SELECT_PRE * i + k
                    round_u(act, mem_, sem, (k + 1) % 2, c + 1, (SELECT_PRE // 2) * i + ((k + 1) // 2 + 1))
                    early_gelu(act, mem_, sem, k % 2, c, (SELECT_PRE // 2) * i + k // 2)
                    if k == EXP_AFTER:
                        held(act, (sem["top_ready"], i + 1))
                        nc.scalar.activation(mem_["expo"][:], mem_["shifted"][:],
                                             ACT.Exp).then_inc(sem["expo_ready"], 1)
                held(act, (sem["picks_turned"], i + 1))
                nc.scalar.activation(selT[:, :, bass.ds(i * P, P)], bank4(turn_bank)[:, 0:3, :],
                                     ACT.Copy).then_inc(sem["turn_room"], 1)

            with act.Fori(0, TT - 1) as i:
                turn(i, False)
            turn(TT - 1, True)

        @block.vector
        def _(dve):
            count = [0]
            PER_TILE = 18

            def done(ins):
                ins.then_inc(sem["select_step"], 1)
                count[0] += 1
                held(dve, (sem["select_step"], tile * PER_TILE + count[0]))

            with dve.Fori(0, TT) as tile:
                held(dve, (sem["score_ready"], tile + 1))
                for f in range(HP):
                    ins = nc.vector.max(best[:, f, 0:8], score[:, f, :])
                done(ins)
                for f in range(HP):
                    nc.vector.max_index(where[:, f, 0:8], best[:, f, 0:8], score[:, f, :])
                for f in range(HP):
                    ins = nc.vector.match_replace(rest[:, f, :], best[:, f, 0:8], score[:, f, :], low)
                done(ins)
                dve.sem_inc(sem["scores_used"], 1)
                for f in range(HP):
                    ins = nc.vector.max(best[:, f, 8:16], rest[:, f, :])
                done(ins)
                for f in range(HP):
                    ins = nc.vector.max_index(where[:, f, 8:16], best[:, f, 8:16], rest[:, f, :])
                done(ins)
                done(nc.vector.tensor_copy(bestf[:], where[:]))
                held(dve, (sem["scores_copied"], 4 * TT))
                pair = best[:].rearrange("p (h two) k -> p h two k", two=2)
                a = pair[:, :, 0, :].unsqueeze(3).to_broadcast([P, HEADS, TOPK, TOPK])
                b = pair[:, :, 1, :].unsqueeze(2).to_broadcast([P, HEADS, TOPK, TOPK])
                done(nc.vector.tensor_tensor(cand[:].rearrange("p h (a b) -> p h a b", a=TOPK), a, b, ALU.add))
                for h in range(HEADS):
                    ins = nc.vector.max(top[:, h, 0:8], cand[:, h, :])
                done(ins)
                for h in range(HEADS):
                    nc.vector.max_index(pos[:, h, 0:8], top[:, h, 0:8], cand[:, h, :])
                for h in range(HEADS):
                    ins = nc.vector.match_replace(crest[:, h, :], top[:, h, 0:8], cand[:, h, :], low)
                done(ins)
                for h in range(HEADS):
                    ins = nc.vector.max(top[:, h, 8:16], crest[:, h, :])
                done(ins)
                for h in range(HEADS):
                    ins = nc.vector.max_index(pos[:, h, 8:16], top[:, h, 8:16], crest[:, h, :])
                done(ins)
                nc.vector.tensor_tensor(mem_["shifted"][:], top[:], top[:, :, 0:1].to_broadcast([P, HEADS, TOPK]),
                                        ALU.subtract).then_inc(sem["top_ready"], 1)
                nc.vector.tensor_scalar(part[:, 0], pos[:], 4, None, ALU.logical_shift_right)
                done(nc.vector.tensor_scalar(part[:, 1], pos[:], 15, None, ALU.bitwise_and))
                done(nc.vector.tensor_copy(partf[:], part[:]))
                pairf = bestf[:].rearrange("p (h two) k -> p h two k", two=2)
                full = [P, HEADS, TOPK, TOPK]
                eq = mem_["eq"][:].rearrange("p (h k a) -> p h k a", h=HEADS, k=TOPK)
                for n in range(2):
                    if n == 0:
                        held(dve, (sem["turn_room"], tile + 1))
                    done(nc.vector.tensor_tensor(eq, partf[:, n].unsqueeze(3).to_broadcast(full),
                                                 mem_["iota"][:, 0:TOPK].unsqueeze(1).unsqueeze(1).to_broadcast(full),
                                                 ALU.is_equal))
                    done(nc.vector.tensor_tensor(eq, eq, pairf[:, :, n, :].unsqueeze(2).to_broadcast(full), ALU.mult))
                    nc.vector.tensor_reduce(pick[:, n, :].rearrange("p (h k) -> p h k", h=HEADS), eq, AX_X,
                                            ALU.add).then_inc(sem["picked"], 1)
                    held(dve, (sem["picked"], 3 * tile + n + 1))
                held(dve, (sem["expo_ready"], tile + 1))
                done(nc.vector.tensor_reduce(mem_["esum"][:], mem_["expo"][:], AX_X, ALU.add))
                done(nc.vector.reciprocal(mem_["einv"][:], mem_["esum"][:]))
                nc.vector.tensor_tensor(pick[:, 2, :].rearrange("p (h k) -> p h k", h=HEADS), mem_["expo"][:],
                                        mem_["einv"][:].unsqueeze(2).to_broadcast([P, HEADS, TOPK]),
                                        ALU.mult).then_inc(sem["picked"], 1)
            assert count[0] == PER_TILE


def stage_table(nc, sem, mem_, io):
    bank = mem_["bank"]
    table_bank = bank[2:6]
    selT, one, two, block_ = mem_["selT"], mem_["onehot1"], mem_["onehot2"], mem_["table"]
    STEP = 4
    PER = 2 * TB // STEP
    SPREAD = PER // TABLE_PRE
    FIRST = SELECT_PRE * TT

    def chunk(it, k):
        return TABLE_PRE * it + (FIRST + k), (TABLE_PRE // 2) * it + (FIRST // 2 + k // 2)

    with nc.Block() as block:

        @block.vector
        def _(dve):
            dve.sem_inc(sem["onehot_room"], 2)
            with dve.Fori(0, NTB // 2) as it:
                for s in range(PER):
                    dve.wait_ge(sem["onehot_room"], PER * it + s + 1)
                    for q in range(STEP):
                        t = bass.ds(it * (2 * TB) + (s * STEP + q), 1)
                        slot = (s * STEP + q) % (2 * STEP)
                        nc.vector.tensor_scalar(one[:, slot, :], mem_["iota"], selT[:, 0, t], None, ALU.is_equal)
                        last = nc.vector.tensor_scalar(two[:, slot, :], mem_["iota"], selT[:, 1, t], selT[:, 2, t],
                                                       ALU.is_equal, ALU.mult)
                    last.then_inc(sem["onehots"], 1)

        @block.gpsimd
        def _(pool):
            with pool.Fori(0, NTB // 2) as it:
                for k in range(TABLE_PRE):
                    rest_of_u(pool, mem_, sem, (k + 1) % 2, chunk(it, k)[0] + 1)

        @block.tensor
        def _(pe):
            with pe.Fori(0, NTB // 2) as it:
                for s in range(PER):
                    k = s // SPREAD
                    hidden_products(pe, mem_, sem, k % 2, chunk(it, k)[0], s % SPREAD, SPREAD)
                    pe.wait_ge(sem["onehots"], PER * it + s + 1)
                    pe.wait_ge(sem["table_room"], PER * it + s + 1)
                    for q in range(STEP):
                        slot = (s * STEP + q) % (2 * STEP)
                        last = nc.tensor.matmul(bank4(table_bank[s % 4])[:, q, :], one[:, slot, :], two[:, slot, :],
                                                start=True, stop=True)
                    last.then_inc(sem["onehot_room"], 1)

        @block.scalar
        def _(act):
            act.sem_inc(sem["table_room"], 4)
            with act.Fori(0, NTB // 2) as it:
                for s in range(PER):
                    k = s // SPREAD
                    c, half = chunk(it, k)
                    if s % SPREAD == 0:
                        k1 = k + 1
                        round_u(act, mem_, sem, k1 % 2, c + 1, (TABLE_PRE // 2) * it + (FIRST // 2 + k1 // 2 + 1))
                    if s % SPREAD == SPREAD - 1:
                        early_gelu(act, mem_, sem, k % 2, c, half)
                    waits = [(sem["onehot_room"], PER * it + s + 3)]
                    if s % (PER // 2) == 0:
                        waits.append((sem["table_stored"][2 * s // PER], 16 * it + 16))
                    held(act, *waits)
                    b, t0 = divmod(s * STEP, TB)
                    nc.scalar.activation(block_[:, b, :, t0:t0 + STEP],
                                         bank4(table_bank[s % 4]).rearrange("p t i -> p i t"),
                                         ACT.Copy).then_inc(sem["table_room"], 1)

        @block.sync
        def _(sp):
            for b in range(2):
                sp.sem_inc(sem["table_stored"][b], 16)
            with sp.Fori(0, NTB // 2) as it:
                for b in range(2):
                    for k in range(b * TABLE_PRE // 2, (b + 1) * TABLE_PRE // 2):
                        store_and_load(sp, mem_, sem, io, k % 2, chunk(it, k)[0])
                    sp.wait_ge(sem["table_room"], PER * it + (PER // 2) * (b + 1) + 4)
                    sp.dma_start(io["table"][:, bass.ds(2 * it + b, 1), :],
                                 block_[:, b].rearrange("p i t -> p (i t)").unsqueeze(1)
                                 ).then_inc(sem["table_stored"][b], 16)

def stage_experts(nc, sem, mem_, io):
    bank = mem_["bank"]
    hid_bank, sum_bank = bank[0:2], bank[2:6]
    h = mem_["h"]
    vraw, vr, vl = (mem_[n] for n in ("vraw", "vr", "vl"))
    wr, wl, act_, w32, tab = (mem_[n] for n in ("wr", "wl", "act", "w32", "tab"))
    TILES = 2 * TT

    def groups(eng, body):
        for k in range(GC):
            body(0, 0, k, True, "first")
        with eng.Fori(0, (LIVE_GROUPS - 2) // 2) as it:
            for gg in range(2):
                for k in range(GC):
                    body(2 * it + (1 + gg), (1 + gg) % 2, k, True, None)
        for k in range(GC):
            body(LIVE_GROUPS - 1, (LIVE_GROUPS - 1) % 2, k, True, "last live")
        with eng.Fori(0, (GROUPS - LIVE_GROUPS) // 2) as it:
            for gg in range(2):
                for k in range(GC):
                    body(2 * it + (LIVE_GROUPS + gg), gg, k, False, None)

    assert LIVE_GROUPS % 2 == 0 and (GROUPS - LIVE_GROUPS) % 2 == 0

    def place(g, live):
        return g + PRE // GC if live else g - LIVE_GROUPS

    with nc.Block() as block:

        @block.sync
        def _(sp):
            def load(g, par, k, live, edge):
                s, n = k % 2, GC * g + k
                c = GC * place(g, live) + k
                if not (edge == "first" and k < 2):
                    sp.wait_ge(sem["v_rest"], n - 1)
                sp.dma_start(vraw[:, s, :], io["v"][bass.ds(c, 1)].rearrange("a p n -> p (a n)")
                             ).then_inc(sem["v_loaded"][s], 16)
                if live and not (edge == "last live" and k >= 1):
                    sp.wait_ge(sem["u_rest"], c + 2)
                    load_u(sp, mem_, sem, io, 1 - s, c + 3)
                if k == 0:
                    if edge != "first":
                        sp.wait_ge(sem["weighted"], GC * g)
                    if edge == "first":
                        for b in range(2):
                            sp.wait_ge(sem["table_stored"][b], 16 * (NTB // 2) + 16)
                    sp.dma_start(tab[:, par], io["table"][:, :, bass.ds(place(g, live) * (GC * TB), GC * TB)]
                                 ).then_inc(sem["tab_loaded"][par], 16)
                if edge == "last live" and k == GC - 1:
                    for b in range(2):
                        sp.wait_ge(sem["hid_stored"][b], 16 * (PRE // 2) + 16)
                if not live:
                    sp.wait_ge(sem["weighted"], n + (GC - 1))
                    sp.dma_start(act_[:, s, :], io["hid"][bass.ds(c, 1)].rearrange("a p n -> p (a n)")
                                 ).then_inc(sem["hid_loaded"][s], 16)

            groups(sp, load)
            for i in range(TT):
                sp.wait_ge(sem["sum_room"], 4 + TILES * (GROUPS - 1) + 2 * (i + 1))
                sp.dma_start(io["out"][i * P:(i + 1) * P, :], h[:, i, :]).then_inc(sem["stored"], 16)
            sp.wait_ge(sem["stored"], 16 * TT)

        @block.gpsimd
        def _(pool):
            def rest(g, par, k, live, edge):
                if live and not (edge == "last live" and k == GC - 1):
                    rest_of_u(pool, mem_, sem, (k + 1) % 2, GC * place(g, live) + (k + 1))

            for k in range(GC):
                rest(0, 0, k, True, "first")
            with pool.Fori(0, (LIVE_GROUPS - 2) // 2) as it:
                for gg in range(2):
                    for k in range(GC):
                        rest(2 * it + (1 + gg), 0, k, True, None)
            for k in range(GC):
                rest(LIVE_GROUPS - 1, 0, k, True, "last live")

        @block.scalar
        def _(act):
            def step(g, par, k, live, edge):
                s, n = k % 2, GC * g + k
                c = GC * place(g, live) + k
                if live and not (edge == "last live" and k == GC - 1):
                    k1 = k + 1
                    round_u(act, mem_, sem, k1 % 2, c + 1, (GC // 2) * place(g, live) + (k1 // 2 + 1))
                waits = [(sem["v_loaded"][s], 16 * (GC // 2) * g + 16 * (k // 2 + 1))]
                if edge != "first":
                    waits.append((sem["summed"], TILES * g))
                held(act, *waits)
                nc.scalar.activation(vr[:, par, k, :], vraw[:, s, :], ACT.Copy).then_inc(sem["v_rounded"], 1)
                if live:
                    waits = [(sem["hidden"], c + 3)]
                    if not (edge == "first" and k < 2):
                        waits.append((sem["weighted"], n + (GC - 1)))
                    held(act, *waits)
                    nc.scalar.activation(act_[:, s, :], hid_bank[s][:], ACT.Gelu).then_inc(sem["gelus"], 1)

            groups(act, step)

        @block.vector
        def _(dve):
            def add_sum(j, n):
                dve.wait_ge(sem["summed"], n + 1 + TILES)
                i, half = divmod(j, 2)
                part = h[:, i, half * HALF:(half + 1) * HALF]
                nc.vector.tensor_tensor(part, part, sum_bank[j % 4][:], ALU.add).then_inc(sem["sum_room"], 1)

            def step(g, par, k, live, edge):
                s, n = k % 2, GC * g + k
                c = GC * place(g, live) + k
                dve.wait_ge(sem["v_rounded"], n + 1)
                if edge != "first":
                    dve.wait_ge(sem["summed"], TILES * g)
                nc.vector.tensor_tensor(vl[:, par, k, :], vraw[:, s, :], vr[:, par, k, :].bitcast(F32),
                                        ALU.subtract).then_inc(sem["v_rest"], 1)
                if live:
                    dve.wait_ge(sem["gelus"], c + 3)
                else:
                    dve.wait_ge(sem["hid_loaded"][s], (16 * (GC // 2)) * (g - LIVE_GROUPS) + 16 * (k // 2 + 1))
                if k == 0:
                    dve.wait_ge(sem["tab_loaded"][par], (g + (2 - par)) * 8)
                nc.vector.tensor_tensor(w32[:, s, :].rearrange("p (a b) -> p a b", a=NTB),
                                        act_[:, s, :].rearrange("p (a b) -> p a b", a=NTB),
                                        tab[:, par, :, k * TB:(k + 1) * TB], ALU.mult).then_inc(sem["weighted"], 1)
                dve.wait_ge(sem["weighted"], n + 1 + GC)
                nc.vector.tensor_copy(wr[:, par, k, :], w32[:, s, :]).then_inc(sem["w_tops"], 1)
                dve.wait_ge(sem["w_tops"], n + 1)
                nc.vector.tensor_tensor(wl[:, par, k, :], w32[:, s, :], wr[:, par, k, :].bitcast(F32),
                                        ALU.subtract).then_inc(sem["w_rest"], 1)
                if edge != "first":
                    for j in (2 * k, 2 * k + 1):
                        add_sum(j, TILES * g + (j - TILES))

            dve.sem_inc(sem["sum_room"], 4)
            dve.sem_inc(sem["weighted"], GC)
            groups(dve, step)
            for j in range(TILES):
                add_sum(j, TILES * (GROUPS - 1) + j)

        @block.tensor
        def _(pe):
            def sum_tile(j, n, par):
                pe.wait_ge(sem["sum_room"], n + 1)
                i, half = divmod(j, 2)
                out = sum_bank[j % 4][:]
                rows, cols = slice(i * P, (i + 1) * P), slice(half * HALF, (half + 1) * HALF)
                for k in range(GC):
                    nc.tensor.matmul(out, wr[:, par, k, rows], vr[:, par, k, cols], start=(k == 0), stop=False)
                    nc.tensor.matmul(out, wr[:, par, k, rows], vl[:, par, k, cols], start=False, stop=False)
                    last = nc.tensor.matmul(out, wl[:, par, k, rows], vr[:, par, k, cols],
                                            start=False, stop=(k == GC - 1))
                last.then_inc(sem["summed"], 1)

            def step(g, par, k, live, edge):
                if live:
                    hidden_products(pe, mem_, sem, k % 2, GC * place(g, live) + k)
                if edge != "first":
                    if k == 0:
                        pe.wait_ge(sem["w_rest"], GC * g)
                        pe.wait_ge(sem["v_rest"], GC * g)
                    for j in (2 * k, 2 * k + 1):
                        sum_tile(j, TILES * g + (j - TILES), 1 - par)

            pe.sem_inc(sem["summed"], TILES)
            groups(pe, step)
            pe.wait_ge(sem["w_rest"], GC * GROUPS)
            pe.wait_ge(sem["v_rest"], GC * GROUPS)
            for j in range(TILES):
                sum_tile(j, TILES * (GROUPS - 1) + j, 1)


SCORE_AFTER, EXP_AFTER = 4, 9


def build(nc, io):
    names = """consts_loaded eps_set x_squares x_roots x_rstd x_normed x_turned x_gained x_rounded x_split
        gain_loaded w_begun pooled_rounded
        gains_loaded pool_loaded pe_steps w_rounded w_split prod_copied v_copied vsh_loaded normed turn_ready
        turn_copied scored logits maxima exps invs probs probsT probsT_copied mixed mixed_copied pads_cleared
        pool_step pooled pool_mixed pool_scaled squares sums roots grstds scaled masked gates gated merged
        merged_rounded merged_split y_rounded y_split h_loaded h_added keys_loaded query_copied h_squares
        h_roots h_rstd h_normed h_turned h_rounded h_split scores_ready scores_copied score_ready
        scores_used turn_room top_ready expo_ready picks_turned picked select_step onehot_room onehots
        table_room u_rest v_rest u_rounded v_rounded hidden gelus weighted w_tops w_rest summed sum_room
        stored""".split()
    sem = {n: nc.alloc_semaphore(n) for n in names}
    for n, k in (("x_loaded", NT), ("w_loaded", 2), ("wbr_loaded", 2), ("bias_loaded", 3), ("table_stored", 2),
                 ("u_loaded", 2), ("hid_stored", 2), ("hid_loaded", 2), ("v_loaded", 2), ("tab_loaded", 2)):
        sem[n] = [nc.alloc_semaphore(f"{n}{i}") for i in range(k)]

    m = {"bank": [nc.alloc_psum_tensor(f"bank{i}", [P, HALF], F32) for i in range(8)]}

    def at(kb, name, shape, dtype=F32):
        m[name] = sbuf(nc, name, shape, dtype, kb)

    at(0, "wring", [P, 2, KD * W])
    at(186, "wr_part", [P, PARTS, W], F32R)
    at(194, "wl_part", [P, PARTS, W], F32R)
    at(32, "h", [P, TT, D])
    at(203.5, "consts", [P, CONST_COLS])
    c0 = 0
    for name, cols in CONSTS:
        m[name] = m["consts"][:, c0:c0 + cols]
        c0 += cols
    m["mask"] = m["mask"].rearrange("p (v c) -> p v c", v=3)
    m["edge"] = m["edge"].rearrange("p (g e t) -> p g e t", g=4, e=2)
    at(206.5, "eps", [P, 8])
    at(206.625, "ss", [P, 8])
    at(206.75, "sd", [P, 8])
    at(206.875, "rstd", [P, 8])
    at(150, "xbuf", [P, NT, D])
    at(174, "junk", [P, D])
    at(178, "turned", [P, 2, T])
    at(32, "memnr", [P, KD, M], F32R)
    at(40, "memnl", [P, KD, M], F32R)
    at(48, "xnr", [P, KD, T], F32R)
    at(64, "xnl", [P, KD, T], F32R)
    at(80, "yT", [P, 3, KW, T])
    at(104, "nraw", [P, 3, TT, W])
    at(104, "bias", [P, 3, NA_H, M])
    at(128, "vna", [P, TT, W])
    at(136, "vsh", [P, 3, W])
    at(142, "kvmem", [P, 2, MT, W])
    at(150, "qkxT", [P, 3, KW, T])
    at(174, "kmT", [P, XA_H, M])
    at(178, "tmp", [P, TT * W])
    at(178, "prob", [P, PROBS, 2 * M])
    at(32, "ppad", [P, 4, T + 2 * PAD])
    at(40.25, "wsum", [P, 2, T + 2 * PAD])
    at(44.5, "pool_w", [P, 4, P])
    at(46.5, "stats", [P, 3 * 2 * PAIRS])
    m["nmax"], m["total"], m["inv"] = (m["stats"][:, 2 * i * PAIRS:2 * (i + 1) * PAIRS] for i in range(3))
    at(202, "gains", [P, 2 * NA_D + 2 * XA_D])
    at(205.375, "gss", [P, 88])
    at(205.75, "gsd", [P, 88])
    at(206.125, "grstd", [P, 88])
    at(142, "probT", [P, 2, 2 * M])
    at(80, "yl", [P, 3, KW, T], F32R)
    at(104, "yr", [P, 3, KW, T], F32R)
    at(166, "wbr_raw", [P, 2, 3 * KW * P])
    at(128, "merged", [P, KD, T])
    at(128, "ml", [P, KD, T], F32R)
    at(178, "gate", [P, 4, T])
    at(160, "gtmp", [P, 2, T])
    at(144, "mr", [P, KD, T], F32R)
    at(80, "wo_r", [P, KD, W], F32R)
    at(96, "wo_l", [P, KD, W], F32R)
    at(48, "hnr", [P, KD, T], F32R)
    at(64, "hnl", [P, KD, T], F32R)
    at(96, "qpT", [P, HP, T])
    at(160, "hn", [P, 2, D])
    at(168, "junk2", [P, D])
    at(172, "ffn_gain", [P, D])
    at(128, "keysT", [P, HP, KEYS])
    at(80, "selT", [P, 3, T])
    at(86, "best", [P, HP, TOPK])
    at(87, "where", [P, HP, TOPK], U32)
    at(88, "wheref", [P, HP, TOPK])
    at(89, "top", [P, HEADS, TOPK])
    at(89.5, "pos", [P, HEADS, TOPK], U32)
    at(90, "part", [P, 2, HEADS, TOPK], U32)
    at(91, "partf", [P, 2, HEADS, TOPK])
    at(92, "pick", [P, 3, HEADS * TOPK])
    at(93.5, "shifted", [P, HEADS, TOPK])
    at(94, "expo", [P, HEADS, TOPK])
    at(94.5, "esum", [P, HEADS])
    at(94.625, "einv", [P, HEADS])
    at(148, "scores", [P, TT, HP, KEYS])
    at(180, "score", [P, HP, KEYS])
    at(188, "score_rest", [P, HP, KEYS])
    at(128, "cand", [P, HEADS, TOPK * TOPK])
    at(136, "cand_rest", [P, HEADS, TOPK * TOPK])
    at(96, "eq", [P, HEADS * TOPK * TOPK])
    at(96, "table", [P, 2, KEYS, TB])
    at(128, "onehot1", [P, 8, KEYS])
    at(132, "onehot2", [P, 8, KEYS])
    at(0, "vraw", [P, 2, D])
    at(8, "ur", [P, 2, D], F32R)
    at(16, "uraw", [P, 2, D])
    at(24, "ul", [P, 2, D], F32R)
    at(80, "tab", [P, 2, NTB, GC * TB])
    at(96, "wr", [P, 2, GC, T], F32R)
    at(112, "wl", [P, 2, GC, T], F32R)
    at(128, "vr", [P, 2, GC, D], F32R)
    at(160, "vl", [P, 2, GC, D], F32R)
    at(196, "act", [P, 2, T])
    at(192, "w32", [P, 2, T])

    stage_attend(nc, sem, m, io)
    stage_merge_and_query(nc, sem, m, io)
    stage_select(nc, sem, m, io)
    stage_table(nc, sem, m, io)
    stage_experts(nc, sem, m, io)


CONSTS = [("ident", P), ("iota", P), ("edge", 4 * 2 * PAD), ("mix_g", KD), ("mem_g", KD),
          ("gate_b", 3 * KD), ("pool_scale", KW), ("mask", 3 * KCOLS)]
CONST_COLS = sum(c for _, c in CONSTS)


def host_constants():
    col = np.arange(QCOLS)
    mask = np.zeros((QCOLS, 3, KCOLS), np.float32)
    for v, j in enumerate((0, 1, 3)):
        first = np.clip(j * QCOLS + col - WCOLS // 2, 0, GRID_C - WCOLS)[:, None]
        key = KEY0[j] // GRID_R + np.arange(KCOLS)[None, :]
        mask[:, v] = np.where((key >= first) & (key < first + WCOLS), 0.0, MASKED)
    mask = np.repeat(mask, GRID_R, axis=0).reshape(P, 3 * KCOLS)
    edge = np.ones((4, 2, PAD), np.float32)
    t = np.arange(T)
    for g, w in enumerate(POOL):
        count = np.clip(t + w // 2, 0, T) - np.clip(t - w // 2, 0, T)
        ratio = (w / count).astype(np.float32)
        edge[g] = ratio[:PAD], ratio[-PAD:]
    edge = np.broadcast_to(edge.reshape(1, -1), (P, 4 * 2 * PAD))
    return mask, edge


def rpb_windows(rpb):
    c, r = np.arange(P) // GRID_R, np.arange(P) % GRID_R
    kc, kr = np.arange(M) // GRID_R, np.arange(M) % GRID_R
    out = []
    for j in (0, 1, 3):
        dc = np.clip(KEY0[j] // GRID_R + kc[None, :] - (j * QCOLS + c[:, None]), 1 - WCOLS, WCOLS - 1) + WCOLS - 1
        dr = kr[None, :] - r[:, None] + GRID_R - 1
        out.append(rpb[:, dr, dc])
    return np.stack(out).transpose(2, 0, 1, 3)


def kernel(x, mem, mix_norm_g, mem_norm_g, w_in, gate_b, w_mem_kv, na_q_g, na_k_g, na_rpb,
           pool_w, pool_scale, xa_q_g, xa_k_g, w_branch_na, w_branch_pool, w_branch_xa, w_out,
           ffn_norm_g, peer_w_q, peer_sub_keys, peer_u, peer_v):
    import concourse.bacc as bacc
    from concourse.bass_utils import run_bass_kernel_spmd

    def arr(a):
        return np.asarray(a)

    def by_rows(w, blocks):
        w = arr(w)
        k, n = w.shape[0] // P, w.shape[1] // blocks
        return w.reshape(k, P, blocks, n).transpose(2, 1, 0, 3).reshape(blocks, P, k * n)

    def per_feature(v):
        return arr(v).reshape(-1, P).T

    def rows(v):
        return np.broadcast_to(arr(v).reshape(1, -1), (P, arr(v).size))

    mask, edge = host_constants()
    f32 = np.float32
    w = arr(w_in)[0]
    mixer, gates = w[:, :N_MIX * W], w[:, N_MIX * W:]
    order = (0, 1, 4, 2, 3)
    mixer = by_rows(mixer, N_MIX)[list(order)]
    gates = gates.reshape(KD, P, 3, KD, P).transpose(3, 1, 0, 2, 4).reshape(KD, P, KD * 3 * P)
    consts = np.concatenate([
        np.eye(P, dtype=f32), np.broadcast_to(np.arange(P, dtype=f32), (P, P)), edge, per_feature(mix_norm_g),
        per_feature(mem_norm_g), per_feature(gate_b), per_feature(pool_scale), mask], axis=1)
    by_column = arr(x).reshape(GRID_R, GRID_C, D).transpose(1, 0, 2).reshape(T, D)
    ins = {
        "x": by_column,
        "mem": arr(mem)[0],
        "consts": consts,
        "ffn_gain": rows(ffn_norm_g),
        "gains": np.concatenate([rows(na_q_g), rows(na_k_g), rows(xa_q_g), rows(xa_k_g)], axis=1),
        "bias": rpb_windows(arr(na_rpb)[0]),
        "pool_w": arr(pool_w)[0].transpose(1, 0, 2),
        "w_branch": np.stack([arr(b)[0].reshape(KW, P, KD, P) for b in (w_branch_na, w_branch_pool, w_branch_xa)])
        .transpose(3, 2, 0, 1, 4).reshape(KD, P, 3 * KW * P),
        "keysT": arr(peer_sub_keys)[0].reshape(HP, KEYS, P).transpose(2, 0, 1),
        "u": arr(peer_u)[0].reshape(KEYS, KEYS, KD, P).transpose(1, 3, 2, 0).reshape(KEYS, P, D),
        "v": arr(peer_v)[0].reshape(KEYS, KEYS, D).transpose(1, 0, 2),
    }
    parts = [by_rows(arr(w_mem_kv)[0], N_KV), mixer, gates, by_rows(arr(w_out)[0], N_OUT),
             by_rows(arr(peer_w_q)[0], N_WQ)]
    ins.update({f"w{n}": w for n, w in enumerate(x for part in parts for x in part)})
    ins = {n: np.ascontiguousarray(a) for n, a in ins.items()}
    nc = bacc.Bacc("TRN2", target_bir_lowering=False, num_devices=1)
    io = {n: nc.dram_tensor(f"in_{n}", a.shape, F32, kind="ExternalInput").ap() for n, a in ins.items()}
    io["w"] = [io[f"w{n}"] for n in range(LOADS)]
    io["out"] = nc.dram_tensor("out_h", (T, D), F32, kind="ExternalOutput").ap()
    io["hid"] = nc.dram_tensor("hidden_spilled", (PRE, P, T), F32, kind="Internal").ap()
    io["table"] = nc.dram_tensor("table_spilled", (P, NTB, KEYS * TB), F32, kind="Internal").ap()
    build(nc, io)
    r = run_bass_kernel_spmd(nc, [{f"in_{n}": a for n, a in ins.items()}], core_ids=[0])
    out = np.asarray(r.results[0]["out_h"])
    return out.reshape(GRID_C, GRID_R, D).transpose(1, 0, 2).reshape(1, T, D)
```
